# Optimizing a Trainium2 kernel written in Bass

```python
import jax, jax.numpy as jnp
from jax import lax
import numpy as np

D_MODEL = 1024
BATCH = 1
SEQ = 128
DEPTH = 1
DEC_BATCH = 1
DEC_SEQ = 512
PAST_LEN = 128

GRID_W = 64
N_HEADS = 8
KV_HEADS = 2
HEAD_DIM = 128
Q_GROUP = N_HEADS // KV_HEADS
ATTN_WIDTH = N_HEADS * HEAD_DIM
KV_WIDTH = KV_HEADS * HEAD_DIM
WINDOW = 128
BLOCK = 128
ROPE_BASE = 10000.0
ROPE_AXIS_FREQS = HEAD_DIM // 4
LRU_WIDTH = 1024
LRU_BLOCKS = 8
LRU_BLOCK_W = LRU_WIDTH // LRU_BLOCKS
LRU_C = 8.0
CONV_W = 4
CONV_PAD_LEFT = 2
PEER_HEADS = 8
N_KEYS = 128
N_EXPERTS = N_KEYS * N_KEYS
PK_DIM = 256
PK_HALF = PK_DIM // 2
PEER_TOPK = 16
PEER_CHUNK = 128
NORM_EPS = 1e-6
NEG_INF = -1e30
IN_COLS = ATTN_WIDTH + 2 * KV_WIDTH + 2 * LRU_WIDTH + 2 * D_MODEL
IN_SPLITS = (ATTN_WIDTH,
             ATTN_WIDTH + KV_WIDTH,
             ATTN_WIDTH + 2 * KV_WIDTH,
             ATTN_WIDTH + 2 * KV_WIDTH + LRU_WIDTH,
             ATTN_WIDTH + 2 * KV_WIDTH + 2 * LRU_WIDTH,
             ATTN_WIDTH + 2 * KV_WIDTH + 2 * LRU_WIDTH + D_MODEL)

kernel_name = "hybrid_diffusion_prefix_step"

def rmsnorm(x, g):
    xf = x.astype(jnp.float32)
    y = xf * lax.rsqrt(jnp.mean(xf * xf, axis=-1, keepdims=True) + NORM_EPS)
    return (y * g.astype(jnp.float32)).astype(x.dtype)

def adaln(cond, w_ada, b_ada):
    m = jax.nn.silu(cond) @ w_ada + b_ada
    return [t[:, None, :] for t in jnp.split(m, 6, axis=-1)]

def rope_2d(x):
    S = x.shape[1]
    rows = S // GRID_W
    row = jnp.repeat(jnp.arange(rows, dtype=jnp.float32), GRID_W)
    col = jnp.tile(jnp.arange(GRID_W, dtype=jnp.float32), rows)
    inv = ROPE_BASE ** (-jnp.arange(ROPE_AXIS_FREQS, dtype=jnp.float32) / ROPE_AXIS_FREQS)
    ang = jnp.concatenate([row[:, None] * inv, col[:, None] * inv], axis=-1)
    cos = jnp.cos(ang)[None, :, None, :].astype(x.dtype)
    sin = jnp.sin(ang)[None, :, None, :].astype(x.dtype)
    x1, x2 = jnp.split(x, 2, axis=-1)
    return jnp.concatenate([x1 * cos - x2 * sin, x1 * sin + x2 * cos], axis=-1)

def attend_block(q, k, v, mask, sink):
    s = jnp.einsum('bqkgd,bskd->bkgqs', q, k).astype(jnp.float32) * (HEAD_DIM ** -0.5)
    if mask is not None:
        s = jnp.where(mask, s, NEG_INF)
    sink_col = jnp.broadcast_to(sink.astype(jnp.float32).reshape(1, KV_HEADS, Q_GROUP, 1, 1),
                                s.shape[:-1] + (1,))
    p = jax.nn.softmax(jnp.concatenate([s, sink_col], axis=-1), axis=-1)[..., :-1]
    o = jnp.einsum('bkgqs,bskd->bqkgd', p.astype(v.dtype), v)
    return o.reshape(o.shape[0], o.shape[1], ATTN_WIDTH)

def context_attention(q, k, v, sink):
    B, S = q.shape[:2]
    nb = S // BLOCK
    qb = jnp.moveaxis(q.reshape(B, nb, BLOCK, KV_HEADS, Q_GROUP, HEAD_DIM), 1, 0)
    o = lax.map(lambda qi: attend_block(qi, k, v, None, sink), qb)
    return jnp.moveaxis(o, 0, 1).reshape(B, S, ATTN_WIDTH)

def latent_attention(q, k, v, k_ctx, v_ctx, sink):
    B, S = q.shape[:2]
    nb = S // BLOCK
    Sc = k_ctx.shape[1]

    def windows(t):
        tp = jnp.pad(t, ((0, 0), (BLOCK, BLOCK), (0, 0), (0, 0)))
        tp = tp.reshape(B, nb + 2, BLOCK, KV_HEADS, HEAD_DIM)
        w = jnp.concatenate([tp[:, :-2], tp[:, 1:-1], tp[:, 2:]], axis=2)
        return jnp.moveaxis(w, 1, 0)

    kw, vw = windows(k), windows(v)
    qb = jnp.moveaxis(q.reshape(B, nb, BLOCK, KV_HEADS, Q_GROUP, HEAD_DIM), 1, 0)
    qi_idx = jnp.arange(BLOCK)[:, None]
    kj_idx = jnp.arange(3 * BLOCK)[None, :]
    band = jnp.abs(qi_idx + BLOCK - kj_idx) <= WINDOW
    ctx_ok = jnp.ones((BLOCK, Sc), dtype=bool)

    def one(args):
        qi, ki, vi, n = args
        kpos = (n - 1) * BLOCK + kj_idx
        valid = band & (kpos >= 0) & (kpos < S)
        mask = jnp.concatenate([valid, ctx_ok], axis=-1)
        keys = jnp.concatenate([ki, k_ctx], axis=1)
        vals = jnp.concatenate([vi, v_ctx], axis=1)
        return attend_block(qi, keys, vals, mask, sink)

    o = lax.map(one, (qb, kw, vw, jnp.arange(nb)))
    return jnp.moveaxis(o, 0, 1).reshape(B, S, ATTN_WIDTH)

def dwconv(x, w, b):
    S = x.shape[1]
    xp = jnp.pad(x, ((0, 0), (CONV_PAD_LEFT, CONV_W - 1 - CONV_PAD_LEFT), (0, 0)))
    y = b
    for t in range(CONV_W):
        y = y + xp[:, t:t + S] * w[t]
    return y

def blockdiag(x, w):
    xs = x.reshape(x.shape[:-1] + (LRU_BLOCKS, LRU_BLOCK_W))
    return jnp.einsum('bsnd,nde->bsne', xs, w).reshape(x.shape)

def _lin_combine(left, right):
    a1, b1 = left
    a2, b2 = right
    return a1 * a2, a2 * b1 + b2

def rglru_dir(xc, w_a, b_a, w_i, b_i, lam, h0, reverse):
    xf = xc.astype(jnp.float32)
    if reverse:
        xf = jnp.flip(xf, axis=1)
    r = jax.nn.sigmoid(blockdiag(xf, w_a.astype(jnp.float32)) + b_a.astype(jnp.float32))
    ig = jax.nn.sigmoid(blockdiag(xf, w_i.astype(jnp.float32)) + b_i.astype(jnp.float32))
    log_a = -LRU_C * r * jax.nn.softplus(-lam.astype(jnp.float32))
    a = jnp.exp(log_a)
    bterm = jnp.sqrt(-jnp.expm1(2.0 * log_a)) * ig * xf
    bterm = bterm.at[:, 0].add(a[:, 0] * h0.astype(jnp.float32))
    _, h = lax.associative_scan(_lin_combine, (a, bterm), axis=1)
    final = h[:, -1]
    if reverse:
        h = jnp.flip(h, axis=1)
    return h.astype(xc.dtype), final.astype(xc.dtype)

def rglru_branch(xr, conv_w, conv_b, w_a, b_a, w_i, b_i, lam, h0_f, h0_b):
    xc = dwconv(xr, conv_w, conv_b)
    hf, hf_last = rglru_dir(xc, w_a[0], b_a[0], w_i[0], b_i[0], lam[0], h0_f, False)
    hb, hb_last = rglru_dir(xc, w_a[1], b_a[1], w_i[1], b_i[1], lam[1], h0_b, True)
    return hf + hb, hf_last, hb_last

def peer(h, w_q, sub_keys, u_tab, v_tab):
    shape = h.shape
    xt = h.reshape(-1, PEER_CHUNK, D_MODEL)

    def chunk(x):
        q = (x @ w_q).reshape(PEER_CHUNK, PEER_HEADS, 2, PK_HALF)
        s = jnp.einsum('chpd,hpnd->chpn', q, sub_keys).astype(jnp.float32)
        st, it = lax.top_k(s, PEER_TOPK)
        cand = (st[:, :, 0, :, None] + st[:, :, 1, None, :]).reshape(PEER_CHUNK, PEER_HEADS, -1)
        cidx = (it[:, :, 0, :, None] * N_KEYS + it[:, :, 1, None, :]).reshape(PEER_CHUNK, PEER_HEADS, -1)
        best, pos = lax.top_k(cand, PEER_TOPK)
        eidx = jnp.take_along_axis(cidx, pos, axis=-1)
        g = jax.nn.softmax(best, axis=-1)
        act = jax.nn.gelu(jnp.einsum('chkd,cd->chk', u_tab[eidx], x).astype(jnp.float32))
        return jnp.einsum('chk,chkd->cd', (g * act).astype(x.dtype), v_tab[eidx])

    return lax.map(chunk, xt).reshape(shape)

def trunk_layer(x, cond, p, cache):
    sh_a, sc_a, g_a, sh_f, sc_f, g_f = adaln(cond, p['w_ada'], p['b_ada'])
    B, S = x.shape[:2]
    h = rmsnorm(x, p['norm_attn_g']) * (1.0 + sc_a) + sh_a
    z = h @ p['w_in']
    q, k, v, xr, xg, ga, gr = jnp.split(z, IN_SPLITS, axis=-1)
    q = q.reshape(B, S, N_HEADS, HEAD_DIM)
    k = k.reshape(B, S, KV_HEADS, HEAD_DIM)
    v = v.reshape(B, S, KV_HEADS, HEAD_DIM)
    if cache is None:
        attn = context_attention(q, k, v, p['attn_sink'])
        h0_f = jnp.zeros((B, LRU_WIDTH), x.dtype)
        h0_b = jnp.zeros((B, LRU_WIDTH), x.dtype)
    else:
        k_ctx, v_ctx, h0_f, h0_b = cache
        attn = latent_attention(rope_2d(q), rope_2d(k), v, k_ctx, v_ctx, p['attn_sink'])
    rnn, hf_last, hb_last = rglru_branch(xr, p['conv_w'], p['conv_b'], p['lru_w_a'], p['lru_b_a'],
                                         p['lru_w_i'], p['lru_b_i'], p['lru_lambda'], h0_f, h0_b)
    a_out = attn @ p['w_attn_o']
    r_out = (rnn * jax.nn.gelu(xg)) @ p['w_rnn_o']
    mix = (jax.nn.sigmoid(ga) * a_out + jax.nn.sigmoid(gr) * r_out) @ p['w_out']
    x = x + g_a * mix
    h = rmsnorm(x, p['norm_ffn_g']) * (1.0 + sc_f) + sh_f
    x = x + g_f * peer(h, p['peer_w_q'], p['peer_keys'], p['peer_u'], p['peer_v'])
    return x, k, v, hf_last, hb_last

def setup_inputs(seed: int = 0) -> dict:
    key = jax.random.key(seed)
    ks = jax.random.split(key, 32)

    def nrm(k, shape, s):
        return s * jax.random.normal(k, shape, jnp.float32)

    u = jax.random.uniform(ks[20], (DEPTH, 2, LRU_WIDTH), jnp.float32, 0.9, 0.999)
    sig = u ** (1.0 / LRU_C)
    lru_lambda = jnp.log(sig) - jnp.log1p(-sig)
    return {
        "x_prompt": nrm(ks[0], (BATCH, SEQ, D_MODEL), 1.0),
        "x_sample": nrm(ks[1], (DEC_BATCH, DEC_SEQ, D_MODEL), 1.0),
        "c": nrm(ks[2], (DEC_BATCH, D_MODEL), 1.0),
        "cache_k": nrm(ks[3], (DEC_BATCH, DEPTH, PAST_LEN, KV_HEADS, HEAD_DIM), 1.0),
        "cache_v": nrm(ks[4], (DEC_BATCH, DEPTH, PAST_LEN, KV_HEADS, HEAD_DIM), 1.0),
        "state_h_fwd": nrm(ks[5], (DEC_BATCH, DEPTH, LRU_WIDTH), 0.5),
        "state_h_bwd": nrm(ks[6], (DEC_BATCH, DEPTH, LRU_WIDTH), 0.5),
        "c_ctx": nrm(ks[7], (D_MODEL,), 1.0),
        "norm_attn_g": 1.0 + nrm(ks[8], (DEPTH, D_MODEL), 0.05),
        "norm_ffn_g": 1.0 + nrm(ks[9], (DEPTH, D_MODEL), 0.05),
        "final_g": 1.0 + nrm(ks[10], (D_MODEL,), 0.05),
        "w_ada": nrm(ks[11], (DEPTH, D_MODEL, 6 * D_MODEL), D_MODEL ** -0.5),
        "b_ada": nrm(ks[12], (DEPTH, 6 * D_MODEL), 0.02),
        "w_in": nrm(ks[13], (DEPTH, D_MODEL, IN_COLS), D_MODEL ** -0.5),
        "attn_sink": nrm(ks[14], (DEPTH, N_HEADS), 0.5),
        "conv_w": nrm(ks[15], (DEPTH, CONV_W, LRU_WIDTH), CONV_W ** -0.5),
        "conv_b": nrm(ks[16], (DEPTH, LRU_WIDTH), 0.02),
        "lru_w_a": nrm(ks[17], (DEPTH, 2, LRU_BLOCKS, LRU_BLOCK_W, LRU_BLOCK_W), LRU_BLOCK_W ** -0.5),
        "lru_b_a": nrm(ks[18], (DEPTH, 2, LRU_WIDTH), 0.1),
        "lru_w_i": nrm(ks[19], (DEPTH, 2, LRU_BLOCKS, LRU_BLOCK_W, LRU_BLOCK_W), LRU_BLOCK_W ** -0.5),
        "lru_b_i": nrm(ks[21], (DEPTH, 2, LRU_WIDTH), 0.1),
        "lru_lambda": lru_lambda,
        "w_attn_o": nrm(ks[22], (DEPTH, ATTN_WIDTH, D_MODEL), ATTN_WIDTH ** -0.5),
        "w_rnn_o": nrm(ks[23], (DEPTH, LRU_WIDTH, D_MODEL), LRU_WIDTH ** -0.5),
        "w_out": nrm(ks[24], (DEPTH, D_MODEL, D_MODEL), D_MODEL ** -0.5),
        "peer_w_q": nrm(ks[25], (DEPTH, D_MODEL, PEER_HEADS * PK_DIM), D_MODEL ** -0.5),
        "peer_keys": nrm(ks[26], (DEPTH, PEER_HEADS, 2, N_KEYS, PK_HALF), PK_HALF ** -0.5),
        "peer_u": nrm(ks[27], (DEPTH, N_EXPERTS, D_MODEL), D_MODEL ** -0.5),
        "peer_v": nrm(ks[28], (DEPTH, N_EXPERTS, D_MODEL), 0.5),
    }

def reference(x_prompt, x_sample, c, cache_k, cache_v, state_h_fwd, state_h_bwd, c_ctx,
              norm_attn_g, norm_ffn_g, final_g, w_ada, b_ada, w_in, attn_sink, conv_w, conv_b,
              lru_w_a, lru_b_a, lru_w_i, lru_b_i, lru_lambda, w_attn_o, w_rnn_o, w_out,
              peer_w_q, peer_keys, peer_u, peer_v):
    xp, xs = x_prompt, x_sample
    ks_out, vs_out, hf_out, hb_out = [], [], [], []
    for l in range(DEPTH):
        p = {
            'norm_attn_g': norm_attn_g[l], 'norm_ffn_g': norm_ffn_g[l],
            'w_ada': w_ada[l], 'b_ada': b_ada[l], 'w_in': w_in[l], 'attn_sink': attn_sink[l],
            'conv_w': conv_w[l], 'conv_b': conv_b[l],
            'lru_w_a': lru_w_a[l], 'lru_b_a': lru_b_a[l], 'lru_w_i': lru_w_i[l], 'lru_b_i': lru_b_i[l],
            'lru_lambda': lru_lambda[l], 'w_attn_o': w_attn_o[l], 'w_rnn_o': w_rnn_o[l], 'w_out': w_out[l],
            'peer_w_q': peer_w_q[l], 'peer_keys': peer_keys[l], 'peer_u': peer_u[l], 'peer_v': peer_v[l],
        }
        xp, k_l, v_l, hf_l, hb_l = trunk_layer(xp, c_ctx[None, :], p, None)
        ks_out.append(k_l)
        vs_out.append(v_l)
        hf_out.append(hf_l)
        hb_out.append(hb_l)
        xs, _, _, _, _ = trunk_layer(xs, c, p, (cache_k[:, l], cache_v[:, l],
                                                state_h_fwd[:, l], state_h_bwd[:, l]))
    y_prompt = rmsnorm(xp, final_g)
    y_sample = rmsnorm(xs, final_g)
    new_cache_k = jnp.stack(ks_out, axis=1)
    new_cache_v = jnp.stack(vs_out, axis=1)
    new_state_h_fwd = jnp.stack(hf_out, axis=1)
    new_state_h_bwd = jnp.stack(hb_out, axis=1)
    return (y_prompt, y_sample, new_cache_k, new_cache_v, new_state_h_fwd, new_state_h_bwd)


_drawn_inputs = setup_inputs


def setup_inputs(seed=0):
    import zlib

    import numpy as np

    out = dict(_drawn_inputs(seed))
    spreads = {}
    factors = {'cache_k': 3.556, 'cache_v': 3.646, 'attn_sink': 8.0, 'lru_b_a': 3.989}
    for name, (base, spread) in spreads.items():
        noise = np.random.default_rng([zlib.crc32(name.encode()), seed]).standard_normal(out[name].shape)
        drawn = base * np.exp(spread * noise) if base else spread * noise
        out[name] = __import__('jax').numpy.asarray(drawn.astype(out[name].dtype))
    for name, factor in factors.items():
        out[name] = (out[name] * factor).astype(out[name].dtype)
    return out
```

```python
from contextlib import ExitStack

import concourse.bass as bass
from concourse import mybir

ALU = mybir.AluOpType
ACT = mybir.ActivationFunctionType
AX_X = mybir.AxisListType.X
F32 = mybir.dt.float32
U32 = mybir.dt.uint32

P = 128
GELU_C = 0.044715
GELU_S = 0.7978845608028654
NEG_BIG = -3.0e38


class Chain:

    def __init__(self, eng, sem):
        self.eng, self.sem, self.n = eng, sem, 0

    def mark(self, ins):
        self.n += 1
        ins.then_inc(self.sem, 1)
        return self.n

    def wait(self, n=None):
        self.eng.wait_ge(self.sem, self.n if n is None else n)

    def link(self, ins):
        self.mark(ins)
        self.wait()


def hybrid_step(nc, ins, outs, ada_scratch):
    y_prompt, y_sample, new_k, new_v, new_hf, new_hb = outs
    D = ins["w_in"].shape[1]
    KD = D // P
    HD = ins["cache_k"].shape[-1]
    NKV = ins["cache_k"].shape[-2]
    NH = ins["attn_sink"].shape[-1]
    G = NH // NKV
    KVW = NKV * HD
    LB = ins["lru_w_a"].shape[2]
    HP = ins["peer_keys"].shape[1] * 2
    PH = HP // 2
    NKEY = ins["peer_keys"].shape[3]
    TOPK = 16
    SLOTS = PH * TOPK
    EPS = 1e-6
    SCALE = float(HD) ** -0.5
    TC = 256
    C_Q, C_K, C_V = 0, NH * HD, NH * HD + KVW
    C_XR = C_V + KVW
    C_XG, C_GA = C_XR + D, C_XR + 2 * D
    C_GR = C_GA + D
    assert HD == P and NKEY == P and SLOTS == P and LB == KD

    TOK = [ins["x_prompt"].shape[1], ins["x_sample"].shape[1]]
    NT = [n // P for n in TOK]
    CH0 = [0, NT[0]]
    NCH = sum(NT)
    PHASES = (0, 1)
    CTX = TOK[1]

    bank, use, order = {}, {}, []
    bank_uses = [0] * 8

    def unit(key, b):
        bank[key] = b
        bank_uses[b] += 1
        use[key] = bank_uses[b]
        order.append(key)

    def quads(ph):
        return [(n, kv) for kv in range(NKV) for n in range(NT[ph])]

    unit(("vcols",), 0)
    for i in range(HP // 4):
        unit(("keys", i), 1 + i % 3)
    unit(("kctx",), 4)
    NADA = ins["w_ada"].shape[2] // TC
    for n in range(NADA):
        unit(("ada", n), n % 4)
    unit(("mod",), 4)
    for ph in PHASES:
        for t in range(NT[ph]):
            for i in range(2):
                unit((ph, "xt", t, i), 2 * (t % 2) + i)

        def gates(j):
            for g in range(4):
                unit((ph, "gate", j, g), 4 + g)
        for j in range(LB):
            unit((ph, "xr", j), 2 * (j % 2))
            unit((ph, "xg", j), 2 * (j % 2) + 1)
            if j:
                gates(j - 1)
        gates(LB - 1)
        for m in range(KD):
            unit((ph, "gr", m), 2 * (m % 4))
            unit((ph, "ro", m), 2 * (m % 4) + 1)
        if ph == 0:
            unit((ph, "kv"), 0)
            unit((ph, "kt"), 1)
        else:
            for kv in range(NKV):
                unit((ph, "k", kv), kv)
            for i in range(NT[ph] // 2):
                unit((ph, "v", i), 2 + i)
        for kv in range(NKV):
            for h in range(G):
                unit((ph, "q", kv * G + h), 4 + h)
            qs = [q for q in quads(ph) if q[1] == kv]
            for h in range(G):
                unit((ph, "s", qs[0], h), h)
            for i, q in enumerate(qs):
                if i + 1 < len(qs):
                    for h in range(G):
                        unit((ph, "s", qs[i + 1], h), h)
                unit((ph, "o", q), 6)
                for h in range(G):
                    unit((ph, "pt", q, h), 4 + h % 2)
                unit((ph, "ot", q), 7)
        for m in range(KD):
            unit((ph, "ga", m), 2 * (m % 4))
            unit((ph, "ao", m), 2 * (m % 4) + 1)
        for n in range(D // TC):
            for t in range(NT[ph]):
                unit((ph, "mix", n, t), (n * NT[ph] + t) % 8)
        for t in range(NT[ph]):
            for i in range(2):
                unit((ph, "h2", t, i), 2 * (t % 2) + i)
        for hp in range(HP):
            unit((ph, "pq", hp), 4 + hp % 2)
            if hp:
                unit((ph, "sc", hp - 1), (hp - 1) % 2)
        unit((ph, "sc", HP - 1), (HP - 1) % 2)
        if ph == 0:
            unit(("state",), 7)

    WR = 4
    tiles, last_unit = [], {}

    def tile(key, unit_key):
        tiles.append(key)
        last_unit[key] = unit_key

    tile(("keys",), ("keys", HP // 4 - 1))
    for n in range(NADA):
        tile(("ada", n), ("ada", n))
    for ph in PHASES:
        for j in range(0, LB, 2):
            tile((ph, "xr", j), (ph, "xr", j + 1))
            tile((ph, "xg", j), (ph, "xg", j + 1))
        for m in range(0, KD, 2):
            tile((ph, "gr", m), (ph, "gr", m + 1))
            tile((ph, "ro", m), (ph, "ro", m + 1))
        tile((ph, "k"), (ph, "kv") if ph == 0 else (ph, "k", NKV - 1))
        tile((ph, "v"), (ph, "kv") if ph == 0 else (ph, "v", NT[1] // 2 - 1))
        for h in range(0, NH, 2):
            tile((ph, "q", h), (ph, "q", h + 1))
        for m in range(0, KD, 2):
            tile((ph, "ga", m), (ph, "ga", m + 1))
            tile((ph, "ao", m), (ph, "ao", m + 1))
        for n in range(D // TC):
            tile((ph, "out", n), (ph, "mix", n, NT[ph] - 1))
        for i in range(0, HP, 2):
            tile((ph, "pq", i), (ph, "pq", i + 1))
    slot = {key: i % WR for i, key in enumerate(tiles)}
    fill = {key: i // WR + 1 for i, key in enumerate(tiles)}

    def tile_source(key):
        if key == ("keys",):
            return ins["peer_keys"][0].rearrange("h t n d -> n (h t) d")
        if key[0] == "ada":
            w, c = ins["w_ada"][0], key[1] * TC
        else:
            ph, what, i = (*key, 0)[:3]
            w_in = ins["w_in"][0]
            w, c = {
                "xr": (w_in, C_XR + i * P), "xg": (w_in, C_XG + i * P),
                "gr": (w_in, C_GR + i * P), "ga": (w_in, C_GA + i * P),
                "k": (w_in, C_K), "v": (w_in, C_V), "q": (w_in, C_Q + i * P),
                "ro": (ins["w_rnn_o"][0], i * P), "ao": (ins["w_attn_o"][0], i * P),
                "out": (ins["w_out"][0], i * TC), "pq": (ins["peer_w_q"][0], i * P),
            }[what]
        return w.rearrange("(k p) n -> p k n", p=P)[:, :, c:c + TC]

    GS, NG = 4, 4
    RING = GS * NG
    steps = [[("u", 0)]] + [[("u", c + 1), ("v", c)] for c in range(NCH - 1)] + [[("v", NCH - 1)]]

    with ExitStack() as ctx:
        def sb(name, shape, dt=F32):
            return ctx.enter_context(nc.sbuf_tensor(name, shape, dt))

        def sem(name):
            return ctx.enter_context(nc.semaphore(name))

        N1 = TOK[1]
        TILE = KD * TC
        big = sb("big", [P, WR * TILE + 2 * KD * N1])
        w_tile = [big[:, s * TILE:(s + 1) * TILE].rearrange("p (k n) -> p k n", k=KD) for s in range(WR)]
        keys_tile = big[:, slot[("keys",)] * TILE:(slot[("keys",)] + 1) * TILE].rearrange("p (i d) -> p i d", i=HP)
        o_h = WR * TILE
        hT = big[:, o_h:o_h + KD * N1].rearrange("p (k n) -> p k n", k=KD)
        featT = big[:, o_h + KD * N1:o_h + 2 * KD * N1].rearrange("p (k n) -> p k n", k=KD)
        assert RING * D <= WR * TILE + 2 * KD * N1
        ring = [big[:, r * D:(r + 1) * D] for r in range(RING)]

        mix_region = sb("mix_region", [P, KD * N1])
        mixT = mix_region[:, :].rearrange("p (k n) -> p k n", k=KD)
        lru_w = mix_region[:, :].rearrange("p (w n e) -> p w n e", w=4, n=LB)
        top_v = mix_region[:, 0:4 * HP * TOPK].rearrange("p (t h k) -> p t h k", t=4, h=HP)
        top_i = mix_region[:, 4 * HP * TOPK:8 * HP * TOPK].bitcast(U32).rearrange("p (t h k) -> p t h k", t=4, h=HP)
        acc = [mix_region[:, i * D:(i + 1) * D] for i in range(4)]

        work = sb("work", [P, 12 * N1])

        def wk(i, n=1):
            return work[:, i * N1:(i + n) * N1]
        xc = [wk(0), wk(1)]
        lt, la, le, lth, lti = ([wk(2 + 2 * i), wk(3 + 2 * i)] for i in range(5))
        qT = wk(0, 4).rearrange("p (h n) -> p h n", h=G)
        sm = wk(4, 4).rearrange("p (h n) -> p h n", h=G)
        pT = [wk(8), wk(9)]
        o_sb = wk(10)
        rope_tmp = wk(11)
        xn = [wk(0, 2), wk(2, 2)]
        gate_row, scale_row, shift_row, ffn_row = wk(4, 2), wk(6, 2), wk(8, 2), wk(10, 2)
        mix_tmp = wk(0)
        pq_sb = [wk(0), wk(1)]
        cut = wk(2)
        cand = wk(4, 4)
        hot = wk(8, 4)
        b_ada = work[0:2, 0:NADA * TC]
        ada_sb = big[0:2, o_h:o_h + NADA * TC]
        assert NADA * TC <= 12 * N1 and NADA * TC <= 2 * KD * N1

        x_all = sb("x_all", [P, NCH, D])
        h2_all = sb("h2_all", [P, NCH, D])
        kT = sb("kT", [P, NKV, N1 + P])
        v_sb = sb("v_sb", [P, NT[1] + 1, KVW])
        ktok = sb("ktok", [P, KVW])
        keysT = sb("keysT", [P, HP, NKEY])
        cos_sb = sb("cos_sb", [P, N1])
        sin_sb = sb("sin_sb", [P, N1])
        mask = sb("mask", [P, 7, P])
        ident = sb("ident", [P, P])
        vrows = sb("vrows", [P, P])
        vcols = sb("vcols", [P, P])
        mod_rows = sb("mod_rows", [4 * KD, P])
        mod_b = sb("mod_b", [P, 2, KD])
        mod_a = sb("mod_a", [P, 2, KD])
        gf_row = sb("gf_row", [P, 2, D])
        final_row = sb("final_row", [P, D])
        sink = sb("sink", [P, NH])
        silu_t = sb("silu_t", [P, 2 * KD])
        siluT = sb("siluT", [P, 2 * KD])
        sp = sb("sp", [P, 8, 2 * LB])
        half_b = sb("half_b", [P, 4 * LB])
        nq = NKV * (NT[0] + NT[1])
        q_max, q_neg, q_dif, q_sum, q_es, q_tot, q_inv = (
            sb(n, [P, nq, G]) for n in ("q_max", "q_neg", "q_dif", "q_sum", "q_es", "q_tot", "q_inv"))
        nrm = sb("nrm", [P, 3 * NCH, 8])
        state = sb("state", [P, 2 * LB])
        state_out = sb("state_out", [2 * LB, P])
        eidx = sb("eidx", [P, NCH, SLOTS], U32)
        gw = sb("gw", [P, NCH, SLOTS])
        iota16 = sb("iota16", [P, TOPK])
        best = sb("best", [P, 3, SLOTS])
        pos = sb("pos", [P, 3, SLOTS], U32)
        sel = sb("sel", [P, 4, SLOTS])
        it_f = sb("it_f", [P, HP, TOPK])
        sred = sb("sred", [P, 2, PH])
        dots_ring = sb("dots_ring", [P, RING])
        dots = sb("dots", [P, SLOTS])
        gel = sb("gel", [P, SLOTS])
        idx_ring = sb("idx_ring", [P, RING], U32)
        pad = sb("pad", [P, 1])

        psum = [ctx.enter_context(nc.psum_tensor(f"bank{b}", [P, 512], F32)) for b in range(8)]

        def ps(key):
            return psum[bank[key]]

        bank_full = [sem(f"bank_full{b}") for b in range(8)]
        bank_free = [sem(f"bank_free{b}") for b in range(8)]
        tile_full = [sem(f"tile_full{s}") for s in range(WR)]
        act_chain, dve_chain = sem("act_chain"), sem("dve_chain")
        act_stage, dve_stage, pe_stage = sem("act_stage"), sem("dve_stage"), sem("pe_stage")
        consts_in, vrows_in, kctx_in, bada_in, x_in, rows_in, final_in, lru_in = map(
            sem, ("consts_in", "vrows_in", "kctx_in", "bada_in", "x_in", "rows_in", "final_in", "lru_in"))
        ada_saved, mod_in = sem("ada_saved"), sem("mod_in")
        vcols_ready, keysT_ready, kctx_ready, silu_half, silu_ready, ada_ready, mod_ready = map(
            sem, ("vcols_ready", "keysT_ready", "kctx_ready", "silu_half", "silu_ready", "ada_ready", "mod_ready"))
        lam_abs, lam_exp = sem("lam_abs"), sem("lam_exp")
        var_ready, std_ready, xn_ready, hT_ready = map(sem, ("var_ready", "std_ready", "xn_ready", "hT_ready"))
        xc_ready, sq_ready, cub_ready, gtanh_ready, feat_ready = map(
            sem, ("xc_ready", "sq_ready", "cub_ready", "gtanh_ready", "feat_ready"))
        ti_ready, e2_ready, w_ready, root_ready = map(sem, ("ti_ready", "e2_ready", "w_ready", "root_ready"))
        lru_done = sem("lru_done")
        rg_ready, mix_ready = sem("rg_ready"), sem("mix_ready")
        kt_ready, v_ready, kv_ready, q_ready = map(sem, ("kt_ready", "v_ready", "kv_ready", "q_ready"))
        neg_ready, prob_ready, sums_ready, o_part, o_ready, attn_ready = map(
            sem, ("neg_ready", "prob_ready", "sums_ready", "o_part", "o_ready", "attn_ready"))
        pT_ready = [sem("pT_even_ready"), sem("pT_odd_ready")]
        h2T_ready, pq_ready, topk_done = sem("h2T_ready"), sem("pq_ready"), sem("topk_done")
        state_ready, state_turned = sem("state_ready"), sem("state_turned")
        soft_ready, route_ready = sem("soft_ready"), sem("route_ready")
        bestdiff = sem("bestdiff")
        row_in = [sem(f"row_in{r}") for r in range(RING)]
        group_used, idx_set, idx_seen = sem("group_used"), sem("idx_set"), sem("idx_seen")
        dots_ready, gsq_ready, gcub_ready, gt_ready = map(sem, ("dots_ready", "gsq_ready", "gcub_ready", "gt_ready"))
        peer_dve = sem("peer_dve")
        fvar_ready, fstd_ready, y_ready = sem("fvar_ready"), sem("fstd_ready"), sem("y_ready")
        saved = sem("saved")

        block = ctx.enter_context(nc.Block())

        V_C, V_G, V_LAM, V_BA, V_BI, V_CW, V_CB, V_SF = 0, 16, 24, 40, 56, 72, 104, 112

        def var(ph, t):
            return sum(NT[:ph]) * 2 + t

        o_units = [(ph, "o", q) for ph in PHASES for q in quads(ph)]
        ot_units = [(ph, "ot", q) for ph in PHASES for q in quads(ph)]

        def values_done(eng, Q, h):
            if h >= 2:
                eng.wait_ge(o_part, (G - 1) * Q + h - 1)
            elif Q:
                eng.wait_ge(bank_full[bank[o_units[Q - 1]]], use[o_units[Q - 1]])

        @block.sync
        def _(sp_):
            for r0, src in (
                (V_C, ins["c_ctx"].rearrange("(r x) -> r x", x=P)),
                (V_C + KD, ins["c"].rearrange("o (r x) -> (o r) x", x=P)),
                (V_G, ins["norm_attn_g"].rearrange("o (r x) -> (o r) x", x=P)),
                (V_LAM, ins["lru_lambda"].rearrange("o d (r x) -> (o d r) x", x=P)),
                (V_BA, ins["lru_b_a"].rearrange("o d (r x) -> (o d r) x", x=P)),
                (V_BI, ins["lru_b_i"].rearrange("o d (r x) -> (o d r) x", x=P)),
                (V_CW, ins["conv_w"].rearrange("o d (r x) -> (o d r) x", x=P)),
                (V_CB, ins["conv_b"].rearrange("o (r x) -> (o r) x", x=P)),
                (V_SF, ins["state_h_fwd"].rearrange("b o (r x) -> (b o r) x", x=P)),
                (V_SF + KD, ins["state_h_bwd"].rearrange("b o (r x) -> (b o r) x", x=P)),
            ):
                sp_.dma_start(vrows[r0:r0 + src.shape[0], :], src).then_inc(vrows_in, 16)
            sp_.dma_start(ident[:, :], ins["ident"]).then_inc(consts_in, 16)

            def load_tile(key):
                i = tiles.index(key)
                if i >= WR:
                    u = last_unit[tiles[i - WR]]
                    sp_.wait_ge(bank_full[bank[u]], use[u])
                dst = keys_tile if key == ("keys",) else w_tile[slot[key]]
                sp_.dma_start(dst, tile_source(key)).then_inc(tile_full[slot[key]], 16)

            load_tile(("keys",))
            sp_.dma_start(cos_sb[:, :], ins["rope_cos"]).then_inc(consts_in, 16)
            sp_.dma_start(sin_sb[:, :], ins["rope_sin"]).then_inc(consts_in, 16)
            sp_.dma_start(mask[:, :, :], ins["mask"].rearrange("p (i n) -> p i n", n=P)).then_inc(consts_in, 16)
            sp_.dma_start(iota16[:, :], ins["iota16"]).then_inc(consts_in, 16)
            sp_.dma_start(sink[:, :], ins["attn_sink"].partition_broadcast(P).rearrange("p o h -> p (o h)")).then_inc(consts_in, 16)
            sp_.dma_start(ktok[:, :], ins["cache_k"][0, 0].rearrange("s h d -> s (h d)")).then_inc(kctx_in, 16)
            sp_.dma_start(v_sb[:, NT[1], :], ins["cache_v"][0, 0].rearrange("s h d -> s (h d)")).then_inc(kctx_in, 16)
            sp_.dma_start(b_ada, ins["b_ada"][0:1, :].partition_broadcast(2).rearrange("p o n -> p (o n)")).then_inc(bada_in, 16)
            sp_.dma_start(x_all[:, 0:NT[0], :], ins["x_prompt"][0].rearrange("(t p) d -> p t d", p=P)).then_inc(x_in, 16)
            sp_.dma_start(x_all[:, NT[0]:NCH, :], ins["x_sample"][0].rearrange("(t p) d -> p t d", p=P)).then_inc(x_in, 16)
            for n in range(NADA):
                load_tile(("ada", n))
            sp_.dma_start(final_row[:, :], ins["final_g"].partition_broadcast(P)).then_inc(final_in, 16)
            sp_.wait_ge(ada_ready, NADA)
            sp_.dma_start(ada_scratch, ada_sb).then_inc(ada_saved, 16)
            sp_.wait_ge(ada_saved, 16)
            for ci in range(2):
                sp_.dma_start(mod_rows[2 * KD * ci:2 * KD * (ci + 1), :],
                              ada_scratch[ci, 0:2 * D].rearrange("(r x) -> r x", x=P)).then_inc(mod_in, 16)
            for ci in range(2):
                sp_.dma_start(gf_row[:, ci, :], ada_scratch[ci, 5 * D:6 * D].partition_broadcast(P)).then_inc(final_in, 16)

            for ph in PHASES:
                for w, name in enumerate(("lru_w_a", "lru_w_i")):
                    if ph and w == 0:
                        sp_.wait_ge(route_ready, CH0[ph])
                    for d in range(2):
                        sp_.dma_start(lru_w[:, 2 * w + d, :, :],
                                      ins[name][0, d].rearrange("n d e -> d n e")).then_inc(lru_in, 16)
                for key in [k for k in tiles if k[0] == ph]:
                    if key == (ph, "out", 0):
                        sp_.wait_ge(attn_ready, NKV * sum(NT[:ph + 1]))
                        for row, c in ((gate_row, 2), (scale_row, 4), (shift_row, 3)):
                            sp_.dma_start(row, ada_scratch[ph, c * D:(c + 1) * D].partition_broadcast(P)).then_inc(rows_in, 16)
                        sp_.dma_start(ffn_row, ins["norm_ffn_g"][0].partition_broadcast(P)).then_inc(rows_in, 16)
                    load_tile(key)
                    if key == (0, "ga", 0):
                        sp_.wait_ge(v_ready, 2)
                        sp_.dma_start(new_k[0, 0].rearrange("s h d -> s (h d)"), ktok[:, :]).then_inc(saved, 16)
                        sp_.dma_start(new_v[0, 0].rearrange("s h d -> s (h d)"), v_sb[:, 0, :]).then_inc(saved, 16)
                        sp_.wait_ge(saved, 32)
            sp_.wait_ge(state_turned, 1)
            sp_.dma_start(new_hf[0, 0].rearrange("(r x) -> r x", x=P), state_out[0:LB, :]).then_inc(saved, 16)
            sp_.dma_start(new_hb[0, 0].rearrange("(r x) -> r x", x=P), state_out[LB:2 * LB, :]).then_inc(saved, 16)
            for c in range(NCH):
                dst = y_prompt[0, c * P:(c + 1) * P, :] if c < NT[0] else y_sample[0, (c - NT[0]) * P:(c - NT[0] + 1) * P, :]
                sp_.wait_ge(y_ready, c + 1)
                sp_.dma_start(dst, x_all[:, c, :]).then_inc(saved, 16)
            sp_.wait_ge(saved, 16 * (4 + NCH))

        @block.tensor
        def _(pe):
            todo = list(order)
            stage = [0]

            def open_unit(key):
                assert todo.pop(0) == key, key
                if use[key] > 1:
                    pe.wait_ge(bank_free[bank[key]], use[key] - 1)
                return ps(key)

            def close_unit(key, last):
                last.then_inc(bank_full[bank[key]], 1)

            def arrived(key):
                pe.wait_ge(tile_full[slot[key]], 16 * fill[key])
                return w_tile[slot[key]]

            def end_stage():
                stage[0] += 1
                pe.drain().then_inc(pe_stage, 1)
                pe.wait_ge(act_stage, stage[0])
                pe.wait_ge(dve_stage, stage[0])

            pe.wait_ge(vrows_in, 160)
            pe.wait_ge(consts_in, 16 * 6)
            u = open_unit(("vcols",))
            close_unit(("vcols",), nc.tensor.transpose(u[:, 0:P], vrows[:, :], ident[:, :]))
            arrived(("keys",))
            for i in range(HP // 4):
                u = open_unit(("keys", i))
                for k in range(4):
                    last = nc.tensor.transpose(u[:, k * P:(k + 1) * P], keys_tile[:, 4 * i + k, :], ident[:, :])
                close_unit(("keys", i), last)
            pe.wait_ge(kctx_in, 32)
            u = open_unit(("kctx",))
            for kv in range(NKV):
                last = nc.tensor.transpose(u[:, kv * P:(kv + 1) * P], ktok[:, kv * P:(kv + 1) * P], ident[:, :])
            close_unit(("kctx",), last)
            pe.wait_ge(silu_ready, 1)
            cond = siluT[:, :].rearrange("p (c k) -> p k c", c=2)
            for n in range(NADA):
                w = arrived(("ada", n))
                u = open_unit(("ada", n))
                for k in range(KD):
                    last = nc.tensor.matmul(u[0:2, 0:TC], cond[:, k, :], w[:, k, :], start=(k == 0), stop=(k == KD - 1))
                close_unit(("ada", n), last)
            pe.wait_ge(mod_in, 32)
            u = open_unit(("mod",))
            close_unit(("mod",), nc.tensor.transpose(u[:, 0:4 * KD], mod_rows[:, :], ident[0:4 * KD, 0:4 * KD]))
            end_stage()

            for ph in PHASES:
                N = TOK[ph]

                def feature_unit(key, w, col, src, n=N):
                    u = open_unit(key)
                    for k in range(KD):
                        last = nc.tensor.matmul(u[:, 0:n], w[:, k, col:col + P], src[:, k, 0:n],
                                                start=(k == 0), stop=(k == KD - 1))
                    close_unit(key, last)

                for t in range(NT[ph]):
                    pe.wait_ge(xn_ready, var(ph, t) + 1)
                    for i in range(2):
                        u = open_unit((ph, "xt", t, i))
                        for k in range(4):
                            last = nc.tensor.transpose(u[:, k * P:(k + 1) * P],
                                                       xn[t % 2][:, (4 * i + k) * P:(4 * i + k + 1) * P], ident[:, :])
                        close_unit((ph, "xt", t, i), last)
                pe.wait_ge(hT_ready, 2 * CH0[ph] + 2 * NT[ph])
                end_stage()

                pe.wait_ge(lru_in, 64 * (ph + 1))

                def gates(j):
                    pe.wait_ge(xc_ready, LB * ph + j + 1)
                    for g in range(4):
                        d, w = g // 2, g % 2
                        u = open_unit((ph, "gate", j, g))
                        close_unit((ph, "gate", j, g), nc.tensor.matmul(
                            u[:, 0:N], lru_w[:, 2 * w + d, j, :], xc[j % 2][:, 0:N], start=True, stop=True))
                for j in range(LB):
                    wr, wg = arrived((ph, "xr", j - j % 2)), arrived((ph, "xg", j - j % 2))
                    feature_unit((ph, "xr", j), wr, (j % 2) * P, hT)
                    feature_unit((ph, "xg", j), wg, (j % 2) * P, hT)
                    if j:
                        gates(j - 1)
                gates(LB - 1)
                end_stage()

                for m in range(KD):
                    wg, wo = arrived((ph, "gr", m - m % 2)), arrived((ph, "ro", m - m % 2))
                    feature_unit((ph, "gr", m), wg, (m % 2) * P, hT)
                    feature_unit((ph, "ro", m), wo, (m % 2) * P, featT)

                wk_, wv_ = arrived((ph, "k")), arrived((ph, "v"))
                if ph == 0:
                    u = open_unit((ph, "kv"))
                    for w, o in ((wk_, 0), (wv_, KVW)):
                        for k in range(KD):
                            last = nc.tensor.matmul(u[:, o:o + KVW], hT[:, k, 0:P], w[:, k, :],
                                                    start=(k == 0), stop=(k == KD - 1))
                    close_unit((ph, "kv"), last)
                    pe.wait_ge(v_ready, 2)
                    u = open_unit((ph, "kt"))
                    for kv in range(NKV):
                        last = nc.tensor.transpose(u[:, kv * P:(kv + 1) * P], ktok[:, kv * P:(kv + 1) * P], ident[:, :])
                    close_unit((ph, "kt"), last)
                else:
                    for kv in range(NKV):
                        feature_unit((ph, "k", kv), wk_, kv * P, hT)
                    for i in range(NT[ph] // 2):
                        u = open_unit((ph, "v", i))
                        for t in range(2):
                            for k in range(KD):
                                last = nc.tensor.matmul(u[:, t * KVW:(t + 1) * KVW],
                                                        hT[:, k, (2 * i + t) * P:(2 * i + t + 1) * P], wv_[:, k, :],
                                                        start=(k == 0), stop=(k == KD - 1))
                        close_unit((ph, "v", i), last)
                end_stage()

                def window(n):
                    return (0, 0) if ph == 0 else (max(n - 1, 0), min(n + 1, NT[ph] - 1))

                def score_units(q):
                    n, kv = q
                    lo, hi = window(n)
                    win = (hi - lo + 1) * P
                    for h in range(G):
                        key = (ph, "s", q, h)
                        u = open_unit(key)
                        qh = qT[:, h, n * P:(n + 1) * P]
                        last = nc.tensor.matmul(u[:, 0:win], qh, kT[:, kv, lo * P:lo * P + win], start=True, stop=True)
                        if ph:
                            last = nc.tensor.matmul(u[:, win:win + P], qh, kT[:, kv, CTX:CTX + P], start=True, stop=True)
                        close_unit(key, last)

                for kv in range(NKV):
                    for h in range(kv * G, kv * G + G, 2):
                        w = arrived((ph, "q", h))
                        feature_unit((ph, "q", h), w, 0, hT)
                        feature_unit((ph, "q", h + 1), w, P, hT)
                    pe.wait_ge(q_ready, NH * ph + (kv + 1) * G)
                    qs = [q for q in quads(ph) if q[1] == kv]
                    score_units(qs[0])
                    for i, q in enumerate(qs):
                        n = q[0]
                        Q = NKV * CH0[ph] + quads(ph).index(q)
                        lo, hi = window(n)
                        blocks = list(range(lo, hi + 1)) + ([NT[1]] if ph else [])
                        if i + 1 < len(qs):
                            score_units(qs[i + 1])
                        o = open_unit((ph, "o", q))

                        def values(h):
                            pe.wait_ge(pT_ready[h % 2], G // 2 * Q + h // 2 + 1)
                            for i_, b in enumerate(blocks):
                                last = nc.tensor.matmul(o[:, h * P:(h + 1) * P], pT[h % 2][:, i_ * P:(i_ + 1) * P],
                                                        v_sb[:, b, kv * P:(kv + 1) * P],
                                                        start=(i_ == 0), stop=(i_ == len(blocks) - 1))
                            if h == G - 1:
                                close_unit((ph, "o", q), last)
                            else:
                                last.then_inc(o_part, 1)
                        for h in range(G):
                            pe.wait_ge(prob_ready, G * Q + h + 1)
                            key = (ph, "pt", q, h)
                            u = open_unit(key)
                            for i_ in range(len(blocks)):
                                last = nc.tensor.transpose(u[:, i_ * P:(i_ + 1) * P], sm[:, h, i_ * P:(i_ + 1) * P], ident[:, :])
                            close_unit(key, last)
                            if h:
                                values(h - 1)
                        values(G - 1)
                        pe.wait_ge(o_ready, Q + 1)
                        u = open_unit((ph, "ot", q))
                        for h in range(G):
                            last = nc.tensor.transpose(u[:, h * P:(h + 1) * P], o_sb[:, h * P:(h + 1) * P], ident[:, :])
                        close_unit((ph, "ot", q), last)
                pe.wait_ge(attn_ready, NKV * sum(NT[:ph + 1]))
                end_stage()

                for m in range(KD):
                    wg, wo = arrived((ph, "ga", m - m % 2)), arrived((ph, "ao", m - m % 2))
                    feature_unit((ph, "ga", m), wg, (m % 2) * P, hT)
                    feature_unit((ph, "ao", m), wo, (m % 2) * P, featT)
                pe.wait_ge(mix_ready, KD * 2 * (ph + 1))
                for n in range(D // TC):
                    w = arrived((ph, "out", n))
                    for t in range(NT[ph]):
                        key = (ph, "mix", n, t)
                        u = open_unit(key)
                        for k in range(KD):
                            last = nc.tensor.matmul(u[:, 0:TC], mixT[:, k, t * P:(t + 1) * P], w[:, k, :],
                                                    start=(k == 0), stop=(k == KD - 1))
                        close_unit(key, last)
                for t in range(NT[ph]):
                    pe.wait_ge(xn_ready, var(ph, NT[ph] + t) + 1)
                    for i in range(2):
                        u = open_unit((ph, "h2", t, i))
                        for k in range(4):
                            f = (4 * i + k) * P
                            last = nc.tensor.transpose(u[:, k * P:(k + 1) * P], h2_all[:, CH0[ph] + t, f:f + P], ident[:, :])
                        close_unit((ph, "h2", t, i), last)
                end_stage()

                pe.wait_ge(h2T_ready, 2 * CH0[ph] + 2 * NT[ph])

                def scores(hp):
                    pe.wait_ge(pq_ready, HP * ph + hp + 1)
                    u = open_unit((ph, "sc", hp))
                    for t in range(NT[ph]):
                        last = nc.tensor.matmul(u[:, t * P:(t + 1) * P], pq_sb[hp % 2][:, t * P:(t + 1) * P],
                                                keysT[:, hp, :], start=True, stop=True)
                    close_unit((ph, "sc", hp), last)
                for hp in range(HP):
                    w = arrived((ph, "pq", hp - hp % 2))
                    feature_unit((ph, "pq", hp), w, (hp % 2) * P, hT)
                    if hp:
                        scores(hp - 1)
                scores(HP - 1)
                if ph == 0:
                    pe.wait_ge(state_ready, 2 * LB)
                    u = open_unit(("state",))
                    close_unit(("state",), nc.tensor.transpose(u[0:2 * LB, 0:P], state[:, :], ident[:, :]))
                end_stage()

        @block.scalar
        def _(act):
            chain = Chain(act, act_chain)
            stage = [0]

            def full(key):
                act.wait_ge(bank_full[bank[key]], use[key])
                return ps(key)

            def end_stage():
                stage[0] += 1
                act.drain().then_inc(act_stage, 1)
                act.wait_ge(pe_stage, stage[0])
                act.wait_ge(dve_stage, stage[0])

            def run(out, in_, func, **kw):
                return nc.scalar.activation(out, in_, func, **kw)

            u = full(("vcols",))
            chain.link(run(vcols[:, :], u[:, 0:P], ACT.Identity))
            act.drain().then_inc(vcols_ready, 1)
            run(silu_t[:, :], vcols[:, 0:2 * KD], ACT.Tanh, scale=0.5).then_inc(silu_half, 1)
            act.wait_ge(lam_abs, 1)
            run(sp[:, 1, :], sp[:, 0, :], ACT.Exp, scale=-1.0).then_inc(lam_exp, 1)
            u = full(("kctx",))
            chain.mark(run(kT[:, :, CTX:CTX + P], u[:, 0:KVW].rearrange("p (h s) -> p h s", h=NKV), ACT.Identity))
            chain.wait()
            act.drain().then_inc(bank_free[bank[("kctx",)]], 1)
            act.drain().then_inc(bank_free[bank[("vcols",)]], 1)
            end_stage()

            for ph in PHASES:
                N = TOK[ph]
                for t in range(NT[ph]):
                    v = var(ph, t)
                    act.wait_ge(var_ready, v + 1)
                    run(nrm[:, v, 2:3], nrm[:, v, 1:2], ACT.Sqrt).then_inc(std_ready, 1)
                for t in range(NT[ph]):
                    for i in range(2):
                        u = full((ph, "xt", t, i))
                        for k in range(4):
                            f = 4 * i + k
                            last = run(hT[:, f, t * P:(t + 1) * P], u[:, k * P:(k + 1) * P], ACT.Identity,
                                       scale=mod_a[:, ph, f:f + 1], bias=mod_b[:, ph, f:f + 1])
                            if k < 3:
                                chain.mark(last)
                        last.then_inc(bank_free[bank[(ph, "xt", t, i)]], 1)
                        act.drain().then_inc(hT_ready, 1)
                end_stage()

                def gelu_in(j):
                    u = full((ph, "xg", j))
                    run(featT[:, j, 0:N], u[:, 0:N], ACT.Square).then_inc(sq_ready, 1)
                    act.wait_ge(cub_ready, LB * ph + j + 1)
                    run(featT[:, j, 0:N], featT[:, j, 0:N], ACT.Tanh, scale=GELU_C * GELU_S).then_inc(gtanh_ready, 1)
                gelu_in(0)
                for j in range(LB):
                    B = LB * ph + j
                    if j + 1 < LB:
                        gelu_in(j + 1)
                    if j:
                        act.wait_ge(lru_done, B)
                    for d in range(2):
                        u = full((ph, "gate", j, 2 * d))
                        run(lt[d][:, 0:N], u[:, 0:N], ACT.Tanh, scale=0.5,
                            bias=half_b[:, d * LB + j:d * LB + j + 1]).then_inc(bank_free[bank[(ph, "gate", j, 2 * d)]], 1)
                        u = full((ph, "gate", j, 2 * d + 1))
                        run(lti[d][:, 0:N], u[:, 0:N], ACT.Tanh, scale=0.5,
                            bias=half_b[:, (2 + d) * LB + j:(2 + d) * LB + j + 1])\
                            .then_inc(bank_free[bank[(ph, "gate", j, 2 * d + 1)]], 1)
                    for d in range(2):
                        i = d * LB + j
                        act.wait_ge(bank_free[bank[(ph, "gate", j, 2 * d + 1)]], use[(ph, "gate", j, 2 * d + 1)])
                        chain.mark(run(lth[d][:, 0:N], lt[d][:, 0:N], ACT.Tanh, scale=sp[:, 7, i:i + 1], bias=sp[:, 7, i:i + 1]))
                        chain.mark(run(la[d][:, 0:N], lt[d][:, 0:N], ACT.Exp, scale=sp[:, 5, i:i + 1], bias=sp[:, 5, i:i + 1]))
                        run(le[d][:, 0:N], lt[d][:, 0:N], ACT.Exp, scale=sp[:, 6, i:i + 1], bias=sp[:, 6, i:i + 1])\
                            .then_inc(e2_ready, 1)
                    for d in range(2):
                        act.wait_ge(w_ready, 2 * B + d + 1)
                        run(le[d][:, 0:N], le[d][:, 0:N], ACT.Sqrt, scale=0.25).then_inc(root_ready, 1)
                end_stage()

                def merge(a, j0):
                    for m in range(KD):
                        i = 2 * KD * ph + j0 + m
                        if m >= 2:
                            act.wait_ge(mix_ready, i - 1)
                        u = full((ph, a, m))
                        chain.link(run(wk(2 + m % 2)[:, 0:N], u[:, 0:N], ACT.Tanh, scale=0.5))
                        act.drain().then_inc(bank_free[bank[(ph, a, m)]], 1)
                        act.drain().then_inc(rg_ready, 1)
                merge("gr", 0)

                if ph == 0:
                    u = full((ph, "kt"))
                    chain.link(run(kT[:, :, 0:P], u[:, 0:KVW].rearrange("p (h s) -> p h s", h=NKV), ACT.Identity))
                    act.drain().then_inc(bank_free[bank[(ph, "kt")]], 1)
                else:
                    for i in range(NT[ph] // 2):
                        u = full((ph, "v", i))
                        run(v_sb[:, 2 * i:2 * i + 2, :], u[:, :].rearrange("p (t n) -> p t n", t=2), ACT.Identity)\
                            .then_inc(bank_free[bank[(ph, "v", i)]], 1)
                end_stage()
                for kv in range(NKV):
                    if ph == 0:
                        for h in range(kv * G, kv * G + G):
                            u = full((ph, "q", h))
                            run(qT[:, h % G, 0:N], u[:, 0:N], ACT.Identity).then_inc(bank_free[bank[(ph, "q", h)]], 1)
                            act.drain().then_inc(q_ready, 1)
                    for q in [q for q in quads(ph) if q[1] == kv]:
                        n = q[0]
                        Q = NKV * CH0[ph] + quads(ph).index(q)
                        W = P if ph == 0 else (min(n + 1, NT[ph] - 1) - max(n - 1, 0) + 2) * P
                        act.wait_ge(neg_ready, Q + 1)
                        chain.mark(run(q_es[:, Q, :], q_dif[:, Q, :], ACT.Exp))
                        for h in range(G):
                            chain.mark(run(sm[:, h, 0:W], sm[:, h, 0:W], ACT.Exp, bias=q_neg[:, Q, h:h + 1],
                                           accum_out=q_sum[:, Q, h:h + 1]))
                            act.drain().then_inc(prob_ready, 1)
                        act.drain().then_inc(sums_ready, 1)
                        for h in (1, 3):
                            u = full((ph, "pt", q, h))
                            values_done(act, Q, h)
                            chain.link(run(pT[1][:, 0:W], u[:, 0:W], ACT.Identity))
                            act.drain().then_inc(bank_free[bank[(ph, "pt", q, h)]], 1)
                            act.drain().then_inc(pT_ready[1], 1)
                        u = full((ph, "ot", q))
                        run(featT[:, kv * G:(kv + 1) * G, n * P:(n + 1) * P], u[:, :].rearrange("p (h s) -> p h s", h=G),
                            ACT.Identity).then_inc(bank_free[bank[(ph, "ot", q)]], 1)
                        act.drain().then_inc(attn_ready, 1)
                end_stage()
                merge("ga", KD)
                for t in range(NT[ph]):
                    v = var(ph, NT[ph] + t)
                    act.wait_ge(var_ready, v + 1)
                    run(nrm[:, v, 2:3], nrm[:, v, 1:2], ACT.Sqrt).then_inc(std_ready, 1)
                for t in range(NT[ph]):
                    for i in range(2):
                        u = full((ph, "h2", t, i))
                        run(hT[:, 4 * i:4 * i + 4, t * P:(t + 1) * P], u[:, :].rearrange("p (k s) -> p k s", k=4),
                            ACT.Identity).then_inc(bank_free[bank[(ph, "h2", t, i)]], 1)
                        act.drain().then_inc(h2T_ready, 1)
                end_stage()
                for hp in range(HP):
                    u = full((ph, "pq", hp))
                    if hp >= 2:
                        s = (ph, "sc", hp - 2)
                        act.wait_ge(bank_full[bank[s]], use[s])
                    chain.link(run(pq_sb[hp % 2][:, 0:N], u[:, 0:N], ACT.Identity))
                    act.drain().then_inc(bank_free[bank[(ph, "pq", hp)]], 1)
                    act.drain().then_inc(pq_ready, 1)
                end_stage()
                for t in range(NT[ph]):
                    c = CH0[ph] + t
                    act.wait_ge(bestdiff, c + 1)
                    run(best[:, 1, :], best[:, 1, :], ACT.Exp).then_inc(soft_ready, 1)
                if ph == 0:
                    pass
            for i, step in enumerate(steps):
                for table, c in step:
                    if table == "u":
                        act.wait_ge(dots_ready, c + 1)
                        run(gel[:, :], dots[:, :], ACT.Square).then_inc(gsq_ready, 1)
                        act.wait_ge(gcub_ready, c + 1)
                        run(gel[:, :], gel[:, :], ACT.Tanh, scale=GELU_C * GELU_S).then_inc(gt_ready, 1)
                for table, c in step:
                    if table == "v":
                        act.wait_ge(fvar_ready, c + 1)
                        run(nrm[:, 2 * NCH + c, 2:3], nrm[:, 2 * NCH + c, 1:2], ACT.Sqrt).then_inc(fstd_ready, 1)

        @block.vector
        def _(dve):
            V = nc.vector
            chain = Chain(dve, dve_chain)
            link, mark = chain.link, chain.mark
            stage = [0]

            def full(key):
                dve.wait_ge(bank_full[bank[key]], use[key])
                return ps(key)

            def free(key):
                dve.drain().then_inc(bank_free[bank[key]], 1)

            def end_stage():
                stage[0] += 1
                dve.drain().then_inc(dve_stage, 1)
                dve.wait_ge(pe_stage, stage[0])
                dve.wait_ge(act_stage, stage[0])

            def variance(v, src, scratch):
                link(V.tensor_tensor_reduce(scratch, src, src, 1.0, 0.0, ALU.mult, ALU.add, nrm[:, v, 0:1]))
                link(V.tensor_scalar(nrm[:, v, 1:2], nrm[:, v, 0:1], 1.0 / D, EPS, ALU.mult, ALU.add))

            def inverse_root(v):
                n = nrm[:, v, :]
                link(V.reciprocal(n[:, 3:4], n[:, 2:3]))
                link(V.tensor_tensor(n[:, 4:5], n[:, 3:4], n[:, 3:4], ALU.mult))
                link(V.tensor_tensor(n[:, 5:6], n[:, 4:5], n[:, 1:2], ALU.mult))
                link(V.tensor_scalar(n[:, 6:7], n[:, 5:6], -0.5, 1.5, ALU.mult, ALU.add))
                link(V.tensor_tensor(n[:, 7:8], n[:, 6:7], n[:, 3:4], ALU.mult))
                return n[:, 7:8]

            dve.wait_ge(vcols_ready, 1)
            lam = vcols[:, V_LAM:V_LAM + 2 * LB]
            link(V.tensor_scalar(sp[:, 2, :], lam, -1.0, None, ALU.mult))
            link(V.tensor_tensor(sp[:, 0, :], lam, sp[:, 2, :], ALU.max))
            dve.drain().then_inc(lam_abs, 1)
            link(V.tensor_scalar(sp[:, 2, :], sp[:, 2, :], 0.0, None, ALU.max))
            link(V.tensor_scalar(half_b[:, :], vcols[:, V_BA:V_BA + 4 * LB], 0.5, None, ALU.mult))
            dve.wait_ge(silu_half, 1)
            link(V.tensor_scalar(silu_t[:, :], silu_t[:, :], 0.5, 0.5, ALU.mult, ALU.add))
            V.tensor_tensor(siluT[:, :], silu_t[:, :], vcols[:, 0:2 * KD], ALU.mult).then_inc(silu_ready, 1)
            dve.wait_ge(lam_exp, 1)
            link(V.tensor_scalar(sp[:, 3, :], sp[:, 1, :], 2.0, None, ALU.add))
            link(V.reciprocal(sp[:, 4, :], sp[:, 3, :]))
            link(V.tensor_tensor(sp[:, 3, :], sp[:, 1, :], sp[:, 4, :], ALU.mult))
            link(V.tensor_tensor(sp[:, 4, :], sp[:, 3, :], sp[:, 3, :], ALU.mult))
            link(V.tensor_scalar(sp[:, 5, :], sp[:, 4, :], 1.0 / 15, 1.0 / 13, ALU.mult, ALU.add))
            for d in (11, 9, 7, 5, 3, 1):
                link(V.tensor_tensor(sp[:, 6, :], sp[:, 5, :], sp[:, 4, :], ALU.mult))
                link(V.tensor_scalar(sp[:, 5, :], sp[:, 6, :], 1.0 / d, None, ALU.add))
            link(V.tensor_tensor(sp[:, 6, :], sp[:, 5, :], sp[:, 3, :], ALU.mult))
            link(V.scalar_tensor_tensor(sp[:, 1, :], sp[:, 6, :], 2.0, sp[:, 2, :], ALU.mult, ALU.add))
            link(V.tensor_scalar(sp[:, 5, :], sp[:, 1, :], -4.0, None, ALU.mult))
            link(V.tensor_scalar(sp[:, 6, :], sp[:, 1, :], -8.0, None, ALU.mult))
            link(V.tensor_scalar(sp[:, 7, :], sp[:, 1, :], 4.0, None, ALU.mult))
            for i in range(HP // 4):
                u = full(("keys", i))
                mark(V.tensor_copy(keysT[:, 4 * i:4 * i + 4, :], u[:, :].rearrange("p (i n) -> p i n", i=4)))
                free(("keys", i))
            dve.wait_ge(bada_in, 16)
            for n in range(NADA):
                u = full(("ada", n))
                c = n * TC
                V.tensor_tensor(ada_sb[:, c:c + TC], u[0:2, 0:TC], b_ada[:, c:c + TC], ALU.add).then_inc(ada_ready, 1)
                free(("ada", n))
            u = full(("mod",))
            cols = u[:, 0:4 * KD].rearrange("p (c w k) -> p c w k", c=2, w=2)
            mark(V.tensor_copy(mod_b[:, :, :], cols[:, :, 0, :]))
            link(V.tensor_scalar(mod_a[:, :, :], cols[:, :, 1, :], 1.0, None, ALU.add))
            free(("mod",))
            for ci in range(2):
                link(V.tensor_tensor(mod_a[:, ci, :], mod_a[:, ci, :], vcols[:, V_G:V_G + KD], ALU.mult))
            end_stage()

            dve.wait_ge(x_in, 32)
            for ph in PHASES:
                N = TOK[ph]
                for t in range(NT[ph]):
                    v = var(ph, t)
                    if t >= 2:
                        u = (ph, "xt", t - 2, 1)
                        dve.wait_ge(bank_full[bank[u]], use[u])
                    x = x_all[:, CH0[ph] + t, :]
                    variance(v, x, xn[t % 2])
                    dve.drain().then_inc(var_ready, 1)
                    dve.wait_ge(std_ready, v + 1)
                    r = inverse_root(v)
                    V.tensor_scalar(xn[t % 2], x, r, None, ALU.mult).then_inc(xn_ready, 1)
                end_stage()

                def conv(j):
                    B = LB * ph + j
                    w = [vcols[:, V_CW + i * KD + j:V_CW + i * KD + j + 1] for i in range(4)]
                    b = vcols[:, V_CB + j:V_CB + j + 1]
                    u, y = full((ph, "xr", j)), xc[j % 2]
                    if j >= 2:
                        s = (ph, "gate", j - 2, 3)
                        dve.wait_ge(bank_full[bank[s]], use[s])
                    link(V.tensor_scalar(y[:, 0:N], u[:, 0:N], w[2], b, ALU.mult, ALU.add))
                    link(V.scalar_tensor_tensor(y[:, 2:N], u[:, 0:N - 2], w[0], y[:, 2:N], ALU.mult, ALU.add))
                    link(V.scalar_tensor_tensor(y[:, 1:N], u[:, 0:N - 1], w[1], y[:, 1:N], ALU.mult, ALU.add))
                    link(V.scalar_tensor_tensor(y[:, 0:N - 1], u[:, 1:N], w[3], y[:, 0:N - 1], ALU.mult, ALU.add))
                    free((ph, "xr", j))
                    dve.drain().then_inc(xc_ready, 1)
                    g, f = full((ph, "xg", j)), featT[:, j, 0:N]
                    dve.wait_ge(sq_ready, B + 1)
                    V.scalar_tensor_tensor(f, f, 1.0 / GELU_C, g[:, 0:N], ALU.add, ALU.mult).then_inc(cub_ready, 1)
                    dve.wait_ge(gtanh_ready, B + 1)
                    link(V.scalar_tensor_tensor(f, f, 1.0, g[:, 0:N], ALU.add, ALU.mult))
                    free((ph, "xg", j))
                conv(0)
                for j in range(LB):
                    B = LB * ph + j
                    if j + 1 < LB:
                        conv(j + 1)
                    y = xc[j % 2][:, 0:N]
                    for d in range(2):
                        dve.wait_ge(e2_ready, 2 * B + d + 1)
                        V.scalar_tensor_tensor(le[d][:, 0:N], le[d][:, 0:N], 1.0, lth[d][:, 0:N],
                                               ALU.add, ALU.mult).then_inc(w_ready, 1)
                        mark(V.scalar_tensor_tensor(lti[d][:, 0:N], lti[d][:, 0:N], 1.0, y, ALU.add, ALU.mult))
                    chain.wait()
                    for d in range(2):
                        dve.wait_ge(root_ready, 2 * B + d + 1)
                        link(V.tensor_tensor(lti[d][:, 0:N], lti[d][:, 0:N], le[d][:, 0:N], ALU.mult))
                        h0 = 0.0 if ph == 0 else vcols[:, V_SF + d * KD + j:V_SF + d * KD + j + 1]
                        rev = slice(None, None, -1) if d else slice(None)
                        a_, b_, o_ = (t_[:, 0:N][:, rev] for t_ in (la[d], lti[d], lt[d]))
                        link(V.tensor_tensor_scan(o_, a_, b_, h0, ALU.mult, ALU.add))
                    if ph == 0:
                        V.tensor_copy(state[:, j:j + 1], lt[0][:, N - 1:N]).then_inc(state_ready, 1)
                        V.tensor_copy(state[:, LB + j:LB + j + 1], lt[1][:, 0:1]).then_inc(state_ready, 1)
                        dve.wait_ge(state_ready, 2 * j + 2)
                    link(V.tensor_tensor(lt[0][:, 0:N], lt[0][:, 0:N], lt[1][:, 0:N], ALU.add))
                    f = featT[:, j, 0:N]
                    link(V.scalar_tensor_tensor(f, lt[0][:, 0:N], 0.5, f, ALU.mult, ALU.mult))
                    dve.drain().then_inc(lru_done, 1)
                end_stage()

                def merge(a, o, j0):
                    for m in range(KD):
                        i = 2 * KD * ph + j0 + m
                        dve.wait_ge(rg_ready, i + 1)
                        u = full((ph, o, m))
                        t_ = wk(2 + m % 2)[:, 0:N]
                        if a == "gr":
                            link(V.scalar_tensor_tensor(mixT[:, m, 0:N], t_, 1.0, u[:, 0:N], ALU.add, ALU.mult))
                        else:
                            link(V.scalar_tensor_tensor(t_, t_, 1.0, u[:, 0:N], ALU.add, ALU.mult))
                            link(V.tensor_tensor(mixT[:, m, 0:N], mixT[:, m, 0:N], t_, ALU.add))
                        free((ph, o, m))
                        dve.drain().then_inc(mix_ready, 1)
                merge("gr", "ro", 0)

                def rope(key, dst):
                    u = full(key)
                    mark(V.tensor_tensor(dst, u[:, 0:N], cos_sb[:, 0:N], ALU.mult))
                    mark(V.tensor_tensor(rope_tmp[0:64, 0:N], u[64:128, 0:N], sin_sb[64:128, 0:N], ALU.mult))
                    link(V.tensor_tensor(rope_tmp[64:128, 0:N], u[0:64, 0:N], sin_sb[0:64, 0:N], ALU.mult))
                    free(key)
                    link(V.tensor_tensor(dst, dst, rope_tmp[:, 0:N], ALU.add))
                if ph == 0:
                    u = full((ph, "kv"))
                    V.tensor_copy(ktok[:, :], u[:, 0:KVW]).then_inc(v_ready, 1)
                    V.tensor_copy(v_sb[:, 0, :], u[:, KVW:2 * KVW]).then_inc(v_ready, 1)
                    free((ph, "kv"))
                else:
                    for kv in range(NKV):
                        rope((ph, "k", kv), kT[:, kv, 0:N])
                end_stage()
                for kv in range(NKV):
                    if ph:
                        for h in range(kv * G, kv * G + G):
                            rope((ph, "q", h), qT[:, h % G, 0:N])
                            dve.drain().then_inc(q_ready, 1)

                    def soft(q):
                        n = q[0]
                        Q = NKV * CH0[ph] + quads(ph).index(q)
                        W = P if ph == 0 else (min(n + 1, NT[ph] - 1) - max(n - 1, 0) + 2) * P
                        for h in range(G):
                            u = full((ph, "s", q, h))
                            if ph == 0:
                                mark(V.tensor_scalar(sm[:, h, 0:W], u[:, 0:W], SCALE, None, ALU.mult))
                            else:
                                m0 = 1 if n == 0 else 0 if n < NT[ph] - 1 else 4
                                mk = mask[:, m0:m0 + W // P, :].rearrange("p i n -> p (i n)")
                                mark(V.scalar_tensor_tensor(sm[:, h, 0:W], u[:, 0:W], SCALE, mk, ALU.mult, ALU.add))
                            free((ph, "s", q, h))
                        chain.wait()
                        link(V.tensor_reduce(q_max[:, Q, :], sm[:, :, 0:W], AX_X, ALU.max))
                        sk = sink[:, kv * G:(kv + 1) * G]
                        link(V.tensor_tensor(q_max[:, Q, :], q_max[:, Q, :], sk, ALU.max))
                        link(V.tensor_tensor(q_dif[:, Q, :], sk, q_max[:, Q, :], ALU.subtract))
                        link(V.tensor_scalar(q_neg[:, Q, :], q_max[:, Q, :], -1.0, None, ALU.mult))
                        dve.drain().then_inc(neg_ready, 1)

                    qs = [q for q in quads(ph) if q[1] == kv]
                    soft(qs[0])
                    for i, q in enumerate(qs):
                        n = q[0]
                        Q = NKV * CH0[ph] + quads(ph).index(q)
                        W = P if ph == 0 else (min(n + 1, NT[ph] - 1) - max(n - 1, 0) + 2) * P
                        for h in (0, 2):
                            u = full((ph, "pt", q, h))
                            values_done(dve, Q, h)
                            link(V.tensor_copy(pT[0][:, 0:W], u[:, 0:W]))
                            free((ph, "pt", q, h))
                            dve.drain().then_inc(pT_ready[0], 1)
                        dve.wait_ge(sums_ready, Q + 1)
                        link(V.tensor_tensor(q_tot[:, Q, :], q_sum[:, Q, :], q_es[:, Q, :], ALU.add))
                        link(V.reciprocal(q_inv[:, Q, :], q_tot[:, Q, :]))
                        u = full((ph, "o", q))
                        if Q:
                            prev = ot_units[Q - 1]
                            dve.wait_ge(bank_full[bank[prev]], use[prev])
                        link(V.tensor_tensor(o_sb[:, :].rearrange("p (h d) -> p h d", h=G),
                                             u[:, :].rearrange("p (h d) -> p h d", h=G),
                                             q_inv[:, Q, :].unsqueeze(2).to_broadcast([P, G, P]), ALU.mult))
                        free((ph, "o", q))
                        dve.drain().then_inc(o_ready, 1)
                        if i + 1 < len(qs):
                            soft(qs[i + 1])
                end_stage()
                merge("ga", "ao", KD)
                dve.wait_ge(rows_in, 64 * (ph + 1))
                for n in range(D // TC):
                    for t in range(NT[ph]):
                        u = full((ph, "mix", n, t))
                        x = x_all[:, CH0[ph] + t, n * TC:(n + 1) * TC]
                        link(V.scalar_tensor_tensor(mix_tmp[:, 0:TC], u[:, 0:TC], 0.5, gate_row[:, n * TC:(n + 1) * TC],
                                                    ALU.mult, ALU.mult))
                        free((ph, "mix", n, t))
                        link(V.tensor_tensor(x, x, mix_tmp[:, 0:TC], ALU.add))
                link(V.scalar_tensor_tensor(scale_row, scale_row, 1.0, ffn_row, ALU.add, ALU.mult))
                for t in range(NT[ph]):
                    c = CH0[ph] + t
                    v = var(ph, NT[ph] + t)
                    variance(v, x_all[:, c, :], h2_all[:, c, :])
                    dve.drain().then_inc(var_ready, 1)
                    dve.wait_ge(std_ready, v + 1)
                    r = inverse_root(v)
                    link(V.scalar_tensor_tensor(h2_all[:, c, :], x_all[:, c, :], r, scale_row, ALU.mult, ALU.mult))
                    V.tensor_tensor(h2_all[:, c, :], h2_all[:, c, :], shift_row, ALU.add).then_inc(xn_ready, 1)
                end_stage()
                for hp in range(HP):
                    u = full((ph, "sc", hp))
                    for t in range(NT[ph]):
                        s = u[:, t * P:(t + 1) * P]
                        tv, ti = top_v[:, t, hp, :], top_i[:, t, hp, :]
                        cu = cut[:, (t % 4) * P:(t % 4 + 1) * P]
                        link(V.max(tv[:, 0:8], s))
                        mark(V.max_index(ti[:, 0:8], tv[:, 0:8], s))
                        link(V.match_replace(cu, tv[:, 0:8], s, NEG_BIG))
                        link(V.max(tv[:, 8:16], cu))
                        link(V.max_index(ti[:, 8:16], tv[:, 8:16], cu))
                    free((ph, "sc", hp))
                if ph == 0:
                    u = full(("state",))
                    link(V.tensor_copy(state_out[:, :], u[0:2 * LB, 0:P]))
                    free(("state",))
                    dve.drain().then_inc(state_turned, 1)
                end_stage()
                for t in range(NT[ph]):
                    c = CH0[ph] + t
                    tv = top_v[:, t, :, :].rearrange("p (h s) k -> p h s k", s=2)
                    shape = [P, PH, TOPK, TOPK]
                    sums = cand.rearrange("p (h i j) -> p h i j", h=PH, i=TOPK)
                    link(V.tensor_tensor(sums, tv[:, :, 0, :].unsqueeze(3).to_broadcast(shape),
                                         tv[:, :, 1, :].unsqueeze(2).to_broadcast(shape), ALU.add))
                    bv = best[:, 0, :].rearrange("p (h k) -> p h k", h=PH)
                    bp = pos[:, 0, :].rearrange("p (h k) -> p h k", h=PH)
                    for h in range(PH):
                        s = cand[:, h * TOPK * TOPK:(h + 1) * TOPK * TOPK]
                        link(V.max(bv[:, h, 0:8], s))
                        link(V.max_index(bp[:, h, 0:8], bv[:, h, 0:8], s))
                        link(V.match_replace(s, bv[:, h, 0:8], s, NEG_BIG))
                        link(V.max(bv[:, h, 8:16], s))
                        link(V.max_index(bp[:, h, 8:16], bv[:, h, 8:16], s))
                    link(V.tensor_tensor(best[:, 1, :].rearrange("p (h k) -> p h k", h=PH), bv,
                                         bv[:, :, 0:1].to_broadcast([P, PH, TOPK]), ALU.subtract))
                    dve.drain().then_inc(bestdiff, 1)
                    link(V.tensor_scalar(pos[:, 1, :], pos[:, 0, :], 4, None, ALU.logical_shift_right))
                    link(V.tensor_scalar(pos[:, 2, :], pos[:, 0, :], TOPK - 1, None, ALU.bitwise_and))
                    link(V.tensor_copy(sel[:, 0:2, :], pos[:, 1:3, :]))
                    link(V.tensor_copy(it_f[:, :, :], top_i[:, t, :, :]))
                    itf = it_f[:, :, :].rearrange("p (h s) k -> p h s k", s=2)
                    onehot = hot.rearrange("p (h k i) -> p h k i", h=PH, k=TOPK)
                    for s in range(2):
                        ps_ = sel[:, s, :].rearrange("p (h k) -> p h k", h=PH)
                        link(V.tensor_tensor(onehot, ps_.unsqueeze(3).to_broadcast(shape),
                                             iota16[:, :].unsqueeze(1).unsqueeze(1).to_broadcast(shape), ALU.is_equal))
                        link(V.tensor_tensor(onehot, onehot, itf[:, :, s, :].unsqueeze(2).to_broadcast(shape), ALU.mult))
                        link(V.tensor_reduce(sel[:, 2 + s, :].rearrange("p (h k) -> p h k", h=PH), onehot, AX_X, ALU.add))
                    link(V.scalar_tensor_tensor(sel[:, 0, :], sel[:, 2, :], float(NKEY), sel[:, 3, :], ALU.mult, ALU.add))
                    link(V.tensor_copy(eidx[:, c, :], sel[:, 0, :]))
                    dve.wait_ge(soft_ready, c + 1)
                    e = best[:, 1, :].rearrange("p (h k) -> p h k", h=PH)
                    link(V.tensor_reduce(sred[:, 0, :], e, AX_X, ALU.add))
                    link(V.reciprocal(sred[:, 1, :], sred[:, 0, :]))
                    link(V.tensor_tensor(gw[:, c, :].rearrange("p (h k) -> p h k", h=PH), e,
                                         sred[:, 1, :].unsqueeze(2).to_broadcast([P, PH, TOPK]), ALU.mult))
                    dve.drain().then_inc(route_ready, 1)
            dve.wait_ge(final_in, 48)

            dve.wait_ge(pe_stage, stage[0])
            dve.drain().then_inc(group_used, NG)
            groups = [0]
            turns = [0]
            done = [1]
            V.memset(dots_ring[:, :], 0.0).then_inc(peer_dve, 1)
            for step in steps:
                iters = len(step) * SLOTS // RING
                per = RING // len(step)
                for table, c in step:
                    if table == "v":
                        for i in range(2):
                            V.memset(acc[i], 0.0).then_inc(peer_dve, 1)
                            done[0] += 1
                dve.wait_ge(peer_dve, done[0])
                nv = per if len(step) == 2 or step[0][0] == "v" else 0
                has_u = step[0][0] == "u"
                each = nv + (1 if has_u else 0)
                with dve.Fori(0, iters) as it:
                    k = 0
                    for r in range(RING):
                        table, c = step[r % len(step)]
                        q = r // len(step)
                        end = r % GS == GS - 1
                        if r == 0:
                            dve.wait_ge(peer_dve, it * each + done[0])
                        dve.wait_ge(row_in[r], (it + (turns[0] + 1)) * 16)
                        if table == "u":
                            ins_ = V.tensor_tensor_reduce(ring[r], ring[r], h2_all[:, c, :], 1.0, 0.0,
                                                          ALU.mult, ALU.add, dots_ring[:, r:r + 1])
                        else:
                            if k >= 2:
                                dve.wait_ge(peer_dve, it * each + (done[0] + k - 1))
                            ins_ = V.scalar_tensor_tensor(acc[k % 2], ring[r], gw[:, c, bass.ds(it * per + q, 1)],
                                                          acc[k % 2], ALU.mult, ALU.add)
                            ins_.then_inc(peer_dve, 1)
                            k += 1
                        if end:
                            if table == "u":
                                ins_.then_inc(group_used, 1)
                            else:
                                dve.drain().then_inc(group_used, 1)
                    if has_u:
                        dve.wait_ge(group_used, it * NG + (NG + groups[0] + NG))
                        src = dots_ring[:, :].rearrange("p (q s) -> p q s", s=len(step))[:, :, 0]
                        V.tensor_copy(dots[:, bass.ds(it * per, per)], src).then_inc(peer_dve, 1)
                groups[0] += iters * NG
                turns[0] += iters
                done[0] += iters * each
                dve.wait_ge(peer_dve, done[0])
                for table, c in step:
                    if table == "u":
                        dve.drain().then_inc(dots_ready, 1)
                        dve.wait_ge(gsq_ready, c + 1)
                        V.scalar_tensor_tensor(gel[:, :], gel[:, :], 1.0 / GELU_C, dots[:, :], ALU.add, ALU.mult)\
                            .then_inc(gcub_ready, 1)
                        dve.wait_ge(gt_ready, c + 1)
                        link(V.scalar_tensor_tensor(gel[:, :], gel[:, :], 1.0, dots[:, :], ALU.add, ALU.mult))
                        link(V.scalar_tensor_tensor(gw[:, c, :], gw[:, c, :], 0.5, gel[:, :], ALU.mult, ALU.mult))
                for table, c in step:
                    if table == "v":
                        x = x_all[:, c, :]
                        link(V.tensor_tensor(acc[0], acc[0], acc[1], ALU.add))
                        link(V.tensor_tensor(acc[0], acc[0], gf_row[:, 0 if c < NT[0] else 1, :], ALU.mult))
                        link(V.tensor_tensor(x, x, acc[0], ALU.add))
                        v = 2 * NCH + c
                        variance(v, x, acc[1])
                        dve.drain().then_inc(fvar_ready, 1)
                        dve.wait_ge(fstd_ready, c + 1)
                        r = inverse_root(v)
                        V.scalar_tensor_tensor(x, x, r, final_row[:, :], ALU.mult, ALU.mult).then_inc(y_ready, 1)
                        dve.wait_ge(y_ready, c + 1)

        @block.gpsimd
        def _(pool):
            g = nc.gpsimd
            g.memset(pad[:, :], 0.0).then_inc(idx_seen, 1)
            pool.wait_ge(idx_seen, 1)
            groups = sets = 0
            pool.wait_ge(route_ready, NCH)
            for step in steps:
                iters = len(step) * SLOTS // RING
                per = GS // len(step)
                with pool.Fori(0, iters) as it:
                    for n in range(NG):
                        pool.wait_ge(group_used, it * NG + (groups + n + 1))
                        for s, (table, c) in enumerate(step):
                            dst = idx_ring[:, n * GS:(n + 1) * GS].rearrange("p (q s) -> p q s", s=len(step))[:, :, s]
                            src = eidx[:, c, bass.ds(it * (per * NG) + n * per, per)]
                            g.tensor_copy(dst, src).then_inc(idx_set, 1)
                        pool.wait_ge(idx_set, it * (NG * len(step)) + (sets + (n + 1) * len(step)))
                        g.tensor_tensor(pad[:, :], pad[:, :], pad[:, :], ALU.add).then_inc(idx_seen, 1)
                        for i in range(GS):
                            r = n * GS + i
                            table, c = step[r % len(step)]
                            g.indirect_dma_start(ring[r], None, ins["peer_u" if table == "u" else "peer_v"][0],
                                                 bass.IndirectOffsetOnAxis(ap=idx_ring[:, r:r + 1], axis=0))\
                                .then_inc(row_in[r], 16)
                groups += iters * NG
                sets += iters * NG * len(step)



_INS = ['x_prompt', 'x_sample', 'c', 'cache_k', 'cache_v', 'state_h_fwd', 'state_h_bwd', 'c_ctx', 'norm_attn_g',
        'norm_ffn_g', 'final_g', 'w_ada', 'b_ada', 'w_in', 'attn_sink', 'conv_w', 'conv_b', 'lru_w_a', 'lru_b_a',
        'lru_w_i', 'lru_b_i', 'lru_lambda', 'w_attn_o', 'w_rnn_o', 'w_out', 'peer_w_q', 'peer_keys', 'peer_u',
        'peer_v']
_OUTS = [((1, 128, 1024), 'float32'), ((1, 512, 1024), 'float32'), ((1, 1, 128, 2, 128), 'float32'),
         ((1, 1, 128, 2, 128), 'float32'), ((1, 1, 1024), 'float32'), ((1, 1, 1024), 'float32')]


def _constants(np, tokens, head_dim, block, grid_w, topk):
    freqs = head_dim // 4
    rows = tokens // grid_w
    row = np.repeat(np.arange(rows, dtype=np.float32), grid_w)
    col = np.tile(np.arange(grid_w, dtype=np.float32), rows)
    inv = (np.float32(10000.0) ** (-np.arange(freqs, dtype=np.float32) / np.float32(freqs))).astype(np.float32)
    ang = np.concatenate([row[:, None] * inv, col[:, None] * inv], axis=-1).T
    cos, sin = np.cos(ang).astype(np.float32), np.sin(ang).astype(np.float32)
    q, k = np.arange(block)[:, None], np.arange(block)[None, :]
    before = np.where(k >= q, 0.0, -1e30).astype(np.float32)
    after = np.where(k <= q, 0.0, -1e30).astype(np.float32)
    none = np.zeros_like(before)
    return {
        "rope_cos": np.concatenate([cos, cos]), "rope_sin": np.concatenate([sin, -sin]),
        "mask": np.concatenate([before, none, after, none, before, none, none], axis=1),
        "ident": np.eye(block, dtype=np.float32),
        "iota16": np.broadcast_to(np.arange(topk, dtype=np.float32), (block, topk)).copy(),
    }


def kernel(**inputs):
    import numpy as _np
    import concourse.bacc as _bacc
    from concourse import mybir as _mybir
    from concourse.bass_utils import run_bass_kernel_spmd as _run

    nc = _bacc.Bacc("TRN2", target_bir_lowering=False, num_devices=1)
    arrays, ins, outs = {}, {}, []
    given = {name: _np.ascontiguousarray(inputs[name]) for name in _INS}
    given.update(_constants(_np, 512, 128, 128, 64, 16))
    for name, a in given.items():
        arrays[f"in_{name}_dram"] = a
        ins[name] = nc.dram_tensor(f"in_{name}_dram", a.shape, _mybir.dt.from_np(a.dtype), kind="ExternalInput").ap()
    for i, (shape, dtype) in enumerate(_OUTS):
        dt = _mybir.dt.from_np(_np.dtype(dtype))
        outs.append(nc.dram_tensor(f"out_{i}_dram", shape, dt, kind="ExternalOutput").ap())
    scratch = nc.dram_tensor("ada_scratch", (2, 6144), _mybir.dt.float32, kind="Internal").ap()
    hybrid_step(nc, ins, outs, scratch)
    r = _run(nc, [arrays], core_ids=[0])
    return tuple(r.results[0][f"out_{i}_dram"] for i in range(len(_OUTS)))
```

```python
from contextlib import ExitStack

import concourse.bass as bass
from concourse import mybir

ALU = mybir.AluOpType
ACT = mybir.ActivationFunctionType
AX_X = mybir.AxisListType.X
F32 = mybir.dt.float32
U32 = mybir.dt.uint32

P = 128
GELU_C = 0.044715
GELU_S = 0.7978845608028654
NEG_BIG = -3.0e38


class Chain:

    def __init__(self, eng, sem):
        self.eng, self.sem, self.n = eng, sem, 0

    def mark(self, ins):
        self.n += 1
        ins.then_inc(self.sem, 1)
        return self.n

    def wait(self, n=None):
        self.eng.wait_ge(self.sem, self.n if n is None else n)

    def link(self, ins):
        self.mark(ins)
        self.wait()


def hybrid_step(nc, ins, outs, ada_scratch):
    y_prompt, y_sample, new_k, new_v, new_hf, new_hb = outs
    D = ins["w_in"].shape[1]
    KD = D // P
    HD = ins["cache_k"].shape[-1]
    NKV = ins["cache_k"].shape[-2]
    NH = ins["attn_sink"].shape[-1]
    G = NH // NKV
    KVW = NKV * HD
    LB = ins["lru_w_a"].shape[2]
    HP = ins["peer_keys"].shape[1] * 2
    PH = HP // 2
    NKEY = ins["peer_keys"].shape[3]
    TOPK = 16
    SLOTS = PH * TOPK
    EPS = 1e-6
    SCALE = float(HD) ** -0.5
    TC = 256
    C_Q, C_K, C_V = 0, NH * HD, NH * HD + KVW
    C_XR = C_V + KVW
    C_XG, C_GA = C_XR + D, C_XR + 2 * D
    C_GR = C_GA + D
    assert HD == P and NKEY == P and SLOTS == P and LB == KD

    TOK = [ins["x_prompt"].shape[1], ins["x_sample"].shape[1]]
    NT = [n // P for n in TOK]
    CH0 = [0, NT[0]]
    NCH = sum(NT)
    PHASES = (0, 1)
    CTX = TOK[1]

    bank, use, order = {}, {}, []
    bank_uses = [0] * 8

    def unit(key, b):
        bank[key] = b
        bank_uses[b] += 1
        use[key] = bank_uses[b]
        order.append(key)

    def quads(ph):
        return [(n, kv) for kv in range(NKV) for n in range(NT[ph])]

    unit(("vcols",), 0)
    for i in range(HP // 4):
        unit(("keys", i), 1 + i % 3)
    unit(("kctx",), 4)
    NADA = ins["w_ada"].shape[2] // TC
    for n in range(NADA):
        unit(("ada", n), n % 4)
    unit(("mod",), 4)
    def norm1_units(ph):
        for t in range(NT[ph]):
            for i in range(2):
                unit((ph, "xt", t, i), 2 * (t % 2) + i)

    for ph in PHASES:
        if ph == 0:
            norm1_units(0)

        def gates(j):
            for g in range(4):
                unit((ph, "gate", j, g), 4 + g)
        for j in range(LB):
            unit((ph, "xr", j), 2 * (j % 2))
            unit((ph, "xg", j), 2 * (j % 2) + 1)
            if j:
                gates(j - 1)
        gates(LB - 1)
        for m in range(KD):
            unit((ph, "gr", m), 2 * (m % 4))
            unit((ph, "ro", m), 2 * (m % 4) + 1)
        if ph == 0:
            unit((ph, "kv"), 0)
            unit((ph, "kt"), 1)
        else:
            for kv in range(NKV):
                unit((ph, "k", kv), kv)
            for i in range(NT[ph] // 2):
                unit((ph, "v", i), 2 + i)
        for h in range(NH):
            unit((ph, "q", h), 4 + h % G)
        qs = quads(ph)
        for h in range(G):
            unit((ph, "s", qs[0], h), h)
        for i, q in enumerate(qs):
            if i + 1 < len(qs):
                for h in range(G):
                    unit((ph, "s", qs[i + 1], h), h)
            unit((ph, "o", q), 6)
            for h in range(G):
                unit((ph, "pt", q, h), 4 + h % 2)
            if i:
                unit((ph, "ot", qs[i - 1]), 7)
        unit((ph, "ot", qs[-1]), 7)
        for m in range(KD):
            unit((ph, "ga", m), 2 * (m % 4))
            unit((ph, "ao", m), 2 * (m % 4) + 1)
        for n in range(D // TC):
            for t in range(NT[ph]):
                unit((ph, "mix", n, t), (n * NT[ph] + t) % 8)
        for t in range(NT[ph]):
            for i in range(2):
                unit((ph, "h2", t, i), 2 * (t % 2) + i)
        if ph == 0:
            norm1_units(1)
        for hp in range(HP):
            unit((ph, "pq", hp), 4 + hp % 2)
            if hp:
                unit((ph, "sc", hp - 1), (hp - 1) % 2)
        unit((ph, "sc", HP - 1), (HP - 1) % 2)
        if ph == 0:
            unit(("state",), 7)

    WR = 4
    tiles, last_unit = [], {}

    def tile(key, unit_key):
        tiles.append(key)
        last_unit[key] = unit_key

    tile(("keys",), ("keys", HP // 4 - 1))
    for n in range(NADA):
        tile(("ada", n), ("ada", n))
    for ph in PHASES:
        for j in range(0, LB, 2):
            tile((ph, "xr", j), (ph, "xr", j + 1))
            tile((ph, "xg", j), (ph, "xg", j + 1))
        for m in range(0, KD, 2):
            tile((ph, "gr", m), (ph, "gr", m + 1))
            tile((ph, "ro", m), (ph, "ro", m + 1))
        tile((ph, "k"), (ph, "kv") if ph == 0 else (ph, "k", NKV - 1))
        tile((ph, "v"), (ph, "kv") if ph == 0 else (ph, "v", NT[1] // 2 - 1))
        for h in range(0, NH, 2):
            tile((ph, "q", h), (ph, "q", h + 1))
        for m in range(0, KD, 2):
            tile((ph, "ga", m), (ph, "ga", m + 1))
            tile((ph, "ao", m), (ph, "ao", m + 1))
        for n in range(D // TC):
            tile((ph, "out", n), (ph, "mix", n, NT[ph] - 1))
        for i in range(0, HP, 2):
            tile((ph, "pq", i), (ph, "pq", i + 1))
    slot = {key: i % WR for i, key in enumerate(tiles)}
    fill = {key: i // WR + 1 for i, key in enumerate(tiles)}

    def tile_source(key):
        if key == ("keys",):
            return ins["peer_keys"][0].rearrange("h t n d -> n (h t) d")
        if key[0] == "ada":
            w, c = ins["w_ada"][0], key[1] * TC
        else:
            ph, what, i = (*key, 0)[:3]
            w_in = ins["w_in"][0]
            w, c = {
                "xr": (w_in, C_XR + i * P), "xg": (w_in, C_XG + i * P),
                "gr": (w_in, C_GR + i * P), "ga": (w_in, C_GA + i * P),
                "k": (w_in, C_K), "v": (w_in, C_V), "q": (w_in, C_Q + i * P),
                "ro": (ins["w_rnn_o"][0], i * P), "ao": (ins["w_attn_o"][0], i * P),
                "out": (ins["w_out"][0], i * TC), "pq": (ins["peer_w_q"][0], i * P),
            }[what]
        return w.rearrange("(k p) n -> p k n", p=P)[:, :, c:c + TC]

    GS, NG = 4, 4
    RING = GS * NG
    C1 = CH0[1]
    steps = [[("u", C1)]] + [[("u", c + 1), ("v", c)] for c in range(C1, NCH - 1)] + [[("v", NCH - 1)]]
    PARTS = 4
    GS0, RING0 = 2, 6
    assert NT[0] == 1

    with ExitStack() as ctx:
        def sb(name, shape, dt=F32):
            return ctx.enter_context(nc.sbuf_tensor(name, shape, dt))

        def sem(name):
            return ctx.enter_context(nc.semaphore(name))

        N1 = TOK[1]
        TILE = KD * TC
        big = sb("big", [P, WR * TILE + 2 * KD * N1])
        w_tile = [big[:, s * TILE:(s + 1) * TILE].rearrange("p (k n) -> p k n", k=KD) for s in range(WR)]
        keys_tile = big[:, slot[("keys",)] * TILE:(slot[("keys",)] + 1) * TILE].rearrange("p (i d) -> p i d", i=HP)
        o_h = WR * TILE
        hT = big[:, o_h:o_h + KD * N1].rearrange("p (k n) -> p k n", k=KD)
        featT = big[:, o_h + KD * N1:o_h + 2 * KD * N1].rearrange("p (k n) -> p k n", k=KD)
        assert RING * D <= WR * TILE + 2 * KD * N1
        ring = [big[:, r * D:(r + 1) * D] for r in range(RING)]

        mix_region = sb("mix_region", [P, KD * N1])
        mixT = mix_region[:, :].rearrange("p (k n) -> p k n", k=KD)
        lru_w = mix_region[:, :].rearrange("p (w n e) -> p w n e", w=4, n=LB)
        top_v = mix_region[:, 0:4 * HP * TOPK].rearrange("p (t h k) -> p t h k", t=4, h=HP)
        top_i = mix_region[:, 4 * HP * TOPK:8 * HP * TOPK].bitcast(U32).rearrange("p (t h k) -> p t h k", t=4, h=HP)
        acc = [mix_region[:, (2 + i) * D:(3 + i) * D] for i in range(2)]
        assert 8 * HP * TOPK <= 2 * D

        work = sb("work", [P, 12 * N1])

        def wk(i, n=1):
            return work[:, i * N1:(i + n) * N1]
        xc = [wk(0), wk(1)]
        lt, la, le, lth, lti = ([wk(2 + 2 * i), wk(3 + 2 * i)] for i in range(5))
        sm_pair = [wk(4 * i, 4).rearrange("p (h n) -> p h n", h=G) for i in range(2)]
        pT = [wk(8), wk(9)]
        o_sb = [wk(10), wk(11)]
        rope_tmp = wk(11)
        xn = [wk(0, 2), wk(2, 2)]
        gate_row, scale_row, shift_row, ffn_row = wk(4, 2), wk(6, 2), wk(8, 2), wk(10, 2)
        mix_tmp = wk(0)
        pq_sb = [wk(0), wk(1)]
        cut = wk(2)
        cand = wk(4, 4)
        hot = wk(8, 4)
        b_ada = work[0:2, 0:NADA * TC]
        ada_sb = big[0:2, o_h:o_h + NADA * TC]
        assert NADA * TC <= 12 * N1 and NADA * TC <= 2 * KD * N1

        x_all = sb("x_all", [P, NCH, D])
        h2_all = sb("h2_all", [P, NCH, D])
        kT = sb("kT", [P, NKV, N1 + P])
        v_sb = sb("v_sb", [P, NT[1] + 1, KVW])
        ktok = sb("ktok", [P, KVW])
        keysT = sb("keysT", [P, HP, NKEY])
        cos_sb = sb("cos_sb", [P, N1])
        sin_sb = sb("sin_sb", [P, N1])
        mask = sb("mask", [P, 7, P])
        ident = sb("ident", [P, P])
        vrows = sb("vrows", [P, P])
        vcols = sb("vcols", [P, P])
        mod_rows = sb("mod_rows", [4 * KD, P])
        mod_b = sb("mod_b", [P, 2, KD])
        mod_a = sb("mod_a", [P, 2, KD])
        gf_row = sb("gf_row", [P, 2, D])
        final_row = sb("final_row", [P, D])
        sink = sb("sink", [P, NH])
        silu_t = sb("silu_t", [P, 2 * KD])
        siluT = sb("siluT", [P, 2 * KD])
        sp = sb("sp", [P, 8, 2 * LB])
        half_b = sb("half_b", [P, 4 * LB])
        nq = NKV * (NT[0] + NT[1])
        q_max, q_neg, q_dif, q_sum, q_es, q_tot, q_inv = (
            sb(n, [P, nq, G]) for n in ("q_max", "q_neg", "q_dif", "q_sum", "q_es", "q_tot", "q_inv"))
        nrm = sb("nrm", [P, 3 * NCH, 8])
        state = sb("state", [P, 2 * LB])
        state_out = sb("state_out", [2 * LB, P])
        eidx = sb("eidx", [P, NCH, SLOTS], U32)
        gw = sb("gw", [P, NCH, SLOTS])
        iota16 = sb("iota16", [P, TOPK])
        best = sb("best", [P, 3, SLOTS])
        pos = sb("pos", [P, 3, SLOTS], U32)
        sel = sb("sel", [P, 4, SLOTS])
        it_f = sb("it_f", [P, HP, TOPK])
        sred = sb("sred", [P, 2, PH])
        dots_ring = sb("dots_ring", [P, RING])
        dots = sb("dots", [P, SLOTS])
        gel = sb("gel", [P, SLOTS])
        idx_ring = sb("idx_ring", [P, RING], U32)
        pad = sb("pad", [P, 1])
        ring0_more = sb("ring0_more", [P, 2, D])
        ring0 = [h2_all[:, c, :] for c in range(C1, NCH)] + [ring0_more[:, i, :] for i in range(2)]
        assert len(ring0) == RING0
        acc0 = [gf_row[:, 1, :], final_row[:, :]]

        psum = [ctx.enter_context(nc.psum_tensor(f"bank{b}", [P, 512], F32)) for b in range(8)]

        def ps(key):
            return psum[bank[key]]

        bank_full = [sem(f"bank_full{b}") for b in range(8)]
        bank_free = [sem(f"bank_free{b}") for b in range(8)]
        tile_full = [sem(f"tile_full{s}") for s in range(WR)]
        act_chain, dve_chain = sem("act_chain"), sem("dve_chain")
        act_stage, dve_stage, pe_stage = sem("act_stage"), sem("dve_stage"), sem("pe_stage")
        consts_in, vrows_in, kctx_in, bada_in, x_in, rows_in, final_in, lru_in = map(
            sem, ("consts_in", "vrows_in", "kctx_in", "bada_in", "x_in", "rows_in", "final_in", "lru_in"))
        ada_saved, mod_in = sem("ada_saved"), sem("mod_in")
        vcols_ready, keysT_ready, kctx_ready, silu_half, silu_ready, ada_ready, mod_ready = map(
            sem, ("vcols_ready", "keysT_ready", "kctx_ready", "silu_half", "silu_ready", "ada_ready", "mod_ready"))
        lam_abs, lam_exp = sem("lam_abs"), sem("lam_exp")
        var_ready, std_ready, xn_ready, hT_ready = map(sem, ("var_ready", "std_ready", "xn_ready", "hT_ready"))
        xc_ready, sq_ready, cub_ready, gtanh_ready, feat_ready = map(
            sem, ("xc_ready", "sq_ready", "cub_ready", "gtanh_ready", "feat_ready"))
        ti_ready, e2_ready, w_ready, root_ready = map(sem, ("ti_ready", "e2_ready", "w_ready", "root_ready"))
        lru_done = sem("lru_done")
        rg_ready, mix_ready = sem("rg_ready"), sem("mix_ready")
        kt_ready, v_ready, kv_ready, q_ready = map(sem, ("kt_ready", "v_ready", "kv_ready", "q_ready"))
        neg_ready, prob_ready, sums_ready, o_part, o_ready, attn_ready = map(
            sem, ("neg_ready", "prob_ready", "sums_ready", "o_part", "o_ready", "attn_ready"))
        pT_ready = [sem("pT_even_ready"), sem("pT_odd_ready")]
        h2T_ready, pq_ready, topk_done = sem("h2T_ready"), sem("pq_ready"), sem("topk_done")
        state_ready, state_turned = sem("state_ready"), sem("state_turned")
        soft_ready, route_ready = sem("soft_ready"), sem("route_ready")
        bestdiff = sem("bestdiff")
        row_in = [sem(f"row_in{r}") for r in range(RING)]
        row0_in = [sem(f"row0_in{r}") for r in range(RING0)]
        slot0_used, sums0_done = sem("slot0_used"), sem("sums0_done")
        group_used, idx_set, idx_seen = sem("group_used"), sem("idx_set"), sem("idx_seen")
        dots_ready, gsq_ready, gcub_ready, gt_ready = map(sem, ("dots_ready", "gsq_ready", "gcub_ready", "gt_ready"))
        peer_dve = sem("peer_dve")
        fvar_ready, fstd_ready, y_ready = sem("fvar_ready"), sem("fstd_ready"), sem("y_ready")
        saved = sem("saved")

        block = ctx.enter_context(nc.Block())

        V_C, V_G, V_LAM, V_BA, V_BI, V_CW, V_CB, V_SF = 0, 16, 24, 40, 56, 72, 104, 112

        def var1(ph, t):
            return t if ph == 0 else 2 * NT[0] + t

        def var2(ph, t):
            return NT[0] + t if ph == 0 else 2 * NT[0] + NT[1] + t

        o_units = [(ph, "o", q) for ph in PHASES for q in quads(ph)]
        ot_units = [(ph, "ot", q) for ph in PHASES for q in quads(ph)]

        def values_done(eng, Q, h):
            if h >= 2:
                eng.wait_ge(o_part, (G - 1) * Q + h - 1)
            elif Q:
                eng.wait_ge(bank_full[bank[o_units[Q - 1]]], use[o_units[Q - 1]])

        @block.sync
        def _(sp_):
            for r0, src in (
                (V_C, ins["c_ctx"].rearrange("(r x) -> r x", x=P)),
                (V_C + KD, ins["c"].rearrange("o (r x) -> (o r) x", x=P)),
                (V_G, ins["norm_attn_g"].rearrange("o (r x) -> (o r) x", x=P)),
                (V_LAM, ins["lru_lambda"].rearrange("o d (r x) -> (o d r) x", x=P)),
                (V_BA, ins["lru_b_a"].rearrange("o d (r x) -> (o d r) x", x=P)),
                (V_BI, ins["lru_b_i"].rearrange("o d (r x) -> (o d r) x", x=P)),
                (V_CW, ins["conv_w"].rearrange("o d (r x) -> (o d r) x", x=P)),
                (V_CB, ins["conv_b"].rearrange("o (r x) -> (o r) x", x=P)),
                (V_SF, ins["state_h_fwd"].rearrange("b o (r x) -> (b o r) x", x=P)),
                (V_SF + KD, ins["state_h_bwd"].rearrange("b o (r x) -> (b o r) x", x=P)),
            ):
                sp_.dma_start(vrows[r0:r0 + src.shape[0], :], src).then_inc(vrows_in, 16)
            sp_.dma_start(ident[:, :], ins["ident"]).then_inc(consts_in, 16)

            def load_tile(key):
                i = tiles.index(key)
                if i >= WR:
                    u = last_unit[tiles[i - WR]]
                    sp_.wait_ge(bank_full[bank[u]], use[u])
                dst = keys_tile if key == ("keys",) else w_tile[slot[key]]
                sp_.dma_start(dst, tile_source(key)).then_inc(tile_full[slot[key]], 16)

            load_tile(("keys",))
            sp_.dma_start(cos_sb[:, :], ins["rope_cos"]).then_inc(consts_in, 16)
            sp_.dma_start(sin_sb[:, :], ins["rope_sin"]).then_inc(consts_in, 16)
            sp_.dma_start(mask[:, :, :], ins["mask"].rearrange("p (i n) -> p i n", n=P)).then_inc(consts_in, 16)
            sp_.dma_start(iota16[:, :], ins["iota16"]).then_inc(consts_in, 16)
            sp_.dma_start(sink[:, :], ins["attn_sink"].partition_broadcast(P).rearrange("p o h -> p (o h)")).then_inc(consts_in, 16)
            sp_.dma_start(ktok[:, :], ins["cache_k"][0, 0].rearrange("s h d -> s (h d)")).then_inc(kctx_in, 16)
            sp_.dma_start(v_sb[:, NT[1], :], ins["cache_v"][0, 0].rearrange("s h d -> s (h d)")).then_inc(kctx_in, 16)
            sp_.dma_start(b_ada, ins["b_ada"][0:1, :].partition_broadcast(2).rearrange("p o n -> p (o n)")).then_inc(bada_in, 16)
            sp_.dma_start(x_all[:, 0:NT[0], :], ins["x_prompt"][0].rearrange("(t p) d -> p t d", p=P)).then_inc(x_in, 16)
            sp_.dma_start(x_all[:, NT[0]:NCH, :], ins["x_sample"][0].rearrange("(t p) d -> p t d", p=P)).then_inc(x_in, 16)
            for n in range(NADA):
                load_tile(("ada", n))
            sp_.wait_ge(ada_ready, NADA)
            sp_.dma_start(ada_scratch, ada_sb).then_inc(ada_saved, 16)
            sp_.wait_ge(ada_saved, 16)
            for ci in range(2):
                sp_.dma_start(mod_rows[2 * KD * ci:2 * KD * (ci + 1), :],
                              ada_scratch[ci, 0:2 * D].rearrange("(r x) -> r x", x=P)).then_inc(mod_in, 16)
            sp_.dma_start(gf_row[:, 0, :], ada_scratch[0, 5 * D:6 * D].partition_broadcast(P)).then_inc(final_in, 16)

            for ph in PHASES:
                for key in [k for k in tiles if k[0] == ph]:
                    if key == (ph, "xr", 0 if ph == 0 else 4):
                        if ph:
                            sp_.wait_ge(route_ready, CH0[ph])
                        for w, name in enumerate(("lru_w_a", "lru_w_i")):
                            for d in range(2):
                                sp_.dma_start(lru_w[:, 2 * w + d, :, :],
                                              ins[name][0, d].rearrange("n d e -> d n e")).then_inc(lru_in, 16)
                    if key == (ph, "out", 0):
                        sp_.wait_ge(attn_ready, NKV * sum(NT[:ph + 1]))
                        for row, c in ((gate_row, 2), (scale_row, 4), (shift_row, 3)):
                            sp_.dma_start(row, ada_scratch[ph, c * D:(c + 1) * D].partition_broadcast(P)).then_inc(rows_in, 16)
                        sp_.dma_start(ffn_row, ins["norm_ffn_g"][0].partition_broadcast(P)).then_inc(rows_in, 16)
                    load_tile(key)
                    if key == (0, "ga", 0):
                        sp_.wait_ge(v_ready, 2)
                        sp_.dma_start(new_k[0, 0].rearrange("s h d -> s (h d)"), ktok[:, :]).then_inc(saved, 16)
                        sp_.dma_start(new_v[0, 0].rearrange("s h d -> s (h d)"), v_sb[:, 0, :]).then_inc(saved, 16)
                        sp_.wait_ge(saved, 32)
            sp_.wait_ge(sums0_done, 1)
            sp_.dma_start(gf_row[:, 1, :], ada_scratch[1, 5 * D:6 * D].partition_broadcast(P)).then_inc(final_in, 16)
            sp_.dma_start(final_row[:, :], ins["final_g"].partition_broadcast(P)).then_inc(final_in, 16)
            sp_.wait_ge(state_turned, 1)
            sp_.dma_start(new_hf[0, 0].rearrange("(r x) -> r x", x=P), state_out[0:LB, :]).then_inc(saved, 16)
            sp_.dma_start(new_hb[0, 0].rearrange("(r x) -> r x", x=P), state_out[LB:2 * LB, :]).then_inc(saved, 16)
            for c in range(NCH):
                dst = y_prompt[0, c * P:(c + 1) * P, :] if c < NT[0] else y_sample[0, (c - NT[0]) * P:(c - NT[0] + 1) * P, :]
                sp_.wait_ge(y_ready, c + 1)
                sp_.dma_start(dst, x_all[:, c, :]).then_inc(saved, 16)
            sp_.wait_ge(saved, 16 * (4 + NCH))

        @block.tensor
        def _(pe):
            todo = list(order)
            stage = [0]

            def open_unit(key):
                assert todo.pop(0) == key, key
                if use[key] > 1:
                    pe.wait_ge(bank_free[bank[key]], use[key] - 1)
                return ps(key)

            def close_unit(key, last):
                last.then_inc(bank_full[bank[key]], 1)

            def arrived(key):
                pe.wait_ge(tile_full[slot[key]], 16 * fill[key])
                return w_tile[slot[key]]

            def end_stage():
                stage[0] += 1
                pe.drain().then_inc(pe_stage, 1)
                pe.wait_ge(act_stage, stage[0])
                pe.wait_ge(dve_stage, stage[0])

            pe.wait_ge(vrows_in, 160)
            pe.wait_ge(consts_in, 16 * 6)
            u = open_unit(("vcols",))
            close_unit(("vcols",), nc.tensor.transpose(u[:, 0:P], vrows[:, :], ident[:, :]))
            arrived(("keys",))
            for i in range(HP // 4):
                u = open_unit(("keys", i))
                for k in range(4):
                    last = nc.tensor.transpose(u[:, k * P:(k + 1) * P], keys_tile[:, 4 * i + k, :], ident[:, :])
                close_unit(("keys", i), last)
            pe.wait_ge(kctx_in, 32)
            u = open_unit(("kctx",))
            for kv in range(NKV):
                last = nc.tensor.transpose(u[:, kv * P:(kv + 1) * P], ktok[:, kv * P:(kv + 1) * P], ident[:, :])
            close_unit(("kctx",), last)
            pe.wait_ge(silu_ready, 1)
            cond = siluT[:, :].rearrange("p (c k) -> p k c", c=2)
            for n in range(NADA):
                w = arrived(("ada", n))
                u = open_unit(("ada", n))
                for k in range(KD):
                    last = nc.tensor.matmul(u[0:2, 0:TC], cond[:, k, :], w[:, k, :], start=(k == 0), stop=(k == KD - 1))
                close_unit(("ada", n), last)
            pe.wait_ge(mod_in, 32)
            u = open_unit(("mod",))
            close_unit(("mod",), nc.tensor.transpose(u[:, 0:4 * KD], mod_rows[:, :], ident[0:4 * KD, 0:4 * KD]))
            end_stage()

            for ph in PHASES:
                N = TOK[ph]

                def feature_unit(key, w, col, src, n=N):
                    u = open_unit(key)
                    for k in range(KD):
                        last = nc.tensor.matmul(u[:, 0:n], w[:, k, col:col + P], src[:, k, 0:n],
                                                start=(k == 0), stop=(k == KD - 1))
                    close_unit(key, last)

                def norm1(ph):
                    for t in range(NT[ph]):
                        pe.wait_ge(xn_ready, var1(ph, t) + 1)
                        for i in range(2):
                            u = open_unit((ph, "xt", t, i))
                            for k in range(4):
                                last = nc.tensor.transpose(u[:, k * P:(k + 1) * P],
                                                           xn[t % 2][:, (4 * i + k) * P:(4 * i + k + 1) * P], ident[:, :])
                            close_unit((ph, "xt", t, i), last)
                if ph == 0:
                    norm1(0)
                    end_stage()

                pe.wait_ge(lru_in, 64 * (ph + 1))

                def gates(j):
                    pe.wait_ge(xc_ready, LB * ph + j + 1)
                    for g in range(4):
                        d, w = g // 2, g % 2
                        u = open_unit((ph, "gate", j, g))
                        close_unit((ph, "gate", j, g), nc.tensor.matmul(
                            u[:, 0:N], lru_w[:, 2 * w + d, j, :], xc[j % 2][:, 0:N], start=True, stop=True))
                for j in range(LB):
                    wr, wg = arrived((ph, "xr", j - j % 2)), arrived((ph, "xg", j - j % 2))
                    feature_unit((ph, "xr", j), wr, (j % 2) * P, hT)
                    feature_unit((ph, "xg", j), wg, (j % 2) * P, hT)
                    if j:
                        gates(j - 1)
                gates(LB - 1)
                end_stage()

                for m in range(KD):
                    wg, wo = arrived((ph, "gr", m - m % 2)), arrived((ph, "ro", m - m % 2))
                    feature_unit((ph, "gr", m), wg, (m % 2) * P, hT)
                    feature_unit((ph, "ro", m), wo, (m % 2) * P, featT)

                wk_, wv_ = arrived((ph, "k")), arrived((ph, "v"))
                if ph == 0:
                    u = open_unit((ph, "kv"))
                    for w, o in ((wk_, 0), (wv_, KVW)):
                        for k in range(KD):
                            last = nc.tensor.matmul(u[:, o:o + KVW], hT[:, k, 0:P], w[:, k, :],
                                                    start=(k == 0), stop=(k == KD - 1))
                    close_unit((ph, "kv"), last)
                    pe.wait_ge(v_ready, 2)
                    u = open_unit((ph, "kt"))
                    for kv in range(NKV):
                        last = nc.tensor.transpose(u[:, kv * P:(kv + 1) * P], ktok[:, kv * P:(kv + 1) * P], ident[:, :])
                    close_unit((ph, "kt"), last)
                else:
                    for kv in range(NKV):
                        feature_unit((ph, "k", kv), wk_, kv * P, hT)
                    for i in range(NT[ph] // 2):
                        u = open_unit((ph, "v", i))
                        for t in range(2):
                            for k in range(KD):
                                last = nc.tensor.matmul(u[:, t * KVW:(t + 1) * KVW],
                                                        hT[:, k, (2 * i + t) * P:(2 * i + t + 1) * P], wv_[:, k, :],
                                                        start=(k == 0), stop=(k == KD - 1))
                        close_unit((ph, "v", i), last)
                for h in range(0, NH, 2):
                    w = arrived((ph, "q", h))
                    feature_unit((ph, "q", h), w, 0, hT)
                    feature_unit((ph, "q", h + 1), w, P, hT)
                end_stage()

                def window(n):
                    return (0, 0) if ph == 0 else (max(n - 1, 0), min(n + 1, NT[ph] - 1))

                def score_units(q):
                    n, kv = q
                    lo, hi = window(n)
                    win = (hi - lo + 1) * P
                    for h in range(G):
                        key = (ph, "s", q, h)
                        u = open_unit(key)
                        qh = featT[:, kv * G + h, n * P:(n + 1) * P]
                        last = nc.tensor.matmul(u[:, 0:win], qh, kT[:, kv, lo * P:lo * P + win], start=True, stop=True)
                        if ph:
                            last = nc.tensor.matmul(u[:, win:win + P], qh, kT[:, kv, CTX:CTX + P], start=True, stop=True)
                        close_unit(key, last)

                def turn_values(i):
                    q = qs[i]
                    Q = NKV * CH0[ph] + i
                    pe.wait_ge(o_ready, Q + 1)
                    u = open_unit((ph, "ot", q))
                    for h in range(G):
                        last = nc.tensor.transpose(u[:, h * P:(h + 1) * P], o_sb[Q % 2][:, h * P:(h + 1) * P], ident[:, :])
                    close_unit((ph, "ot", q), last)

                qs = quads(ph)
                score_units(qs[0])
                for i, q in enumerate(qs):
                    n, kv = q
                    Q = NKV * CH0[ph] + i
                    lo, hi = window(n)
                    blocks = list(range(lo, hi + 1)) + ([NT[1]] if ph else [])
                    if i + 1 < len(qs):
                        score_units(qs[i + 1])
                    o = open_unit((ph, "o", q))

                    def values(h):
                        pe.wait_ge(pT_ready[h % 2], G // 2 * Q + h // 2 + 1)
                        for i_, b in enumerate(blocks):
                            last = nc.tensor.matmul(o[:, h * P:(h + 1) * P], pT[h % 2][:, i_ * P:(i_ + 1) * P],
                                                    v_sb[:, b, kv * P:(kv + 1) * P],
                                                    start=(i_ == 0), stop=(i_ == len(blocks) - 1))
                        if h == G - 1:
                            close_unit((ph, "o", q), last)
                        else:
                            last.then_inc(o_part, 1)
                    for h in range(G):
                        pe.wait_ge(prob_ready, G * Q + h + 1)
                        key = (ph, "pt", q, h)
                        u = open_unit(key)
                        for i_ in range(len(blocks)):
                            last = nc.tensor.transpose(u[:, i_ * P:(i_ + 1) * P],
                                                       sm_pair[Q % 2][:, h, i_ * P:(i_ + 1) * P], ident[:, :])
                        close_unit(key, last)
                        if h:
                            values(h - 1)
                    values(G - 1)
                    if i:
                        turn_values(i - 1)
                turn_values(len(qs) - 1)
                pe.wait_ge(attn_ready, NKV * sum(NT[:ph + 1]))
                end_stage()

                for m in range(KD):
                    wg, wo = arrived((ph, "ga", m - m % 2)), arrived((ph, "ao", m - m % 2))
                    feature_unit((ph, "ga", m), wg, (m % 2) * P, hT)
                    feature_unit((ph, "ao", m), wo, (m % 2) * P, featT)
                pe.wait_ge(mix_ready, KD * 2 * (ph + 1))
                for n in range(D // TC):
                    w = arrived((ph, "out", n))
                    for t in range(NT[ph]):
                        key = (ph, "mix", n, t)
                        u = open_unit(key)
                        for k in range(KD):
                            last = nc.tensor.matmul(u[:, 0:TC], mixT[:, k, t * P:(t + 1) * P], w[:, k, :],
                                                    start=(k == 0), stop=(k == KD - 1))
                        close_unit(key, last)
                for t in range(NT[ph]):
                    pe.wait_ge(xn_ready, var2(ph, t) + 1)
                    for i in range(2):
                        u = open_unit((ph, "h2", t, i))
                        for k in range(4):
                            f = (4 * i + k) * P
                            last = nc.tensor.transpose(u[:, k * P:(k + 1) * P], h2_all[:, CH0[ph] + t, f:f + P], ident[:, :])
                        close_unit((ph, "h2", t, i), last)
                if ph == 0:
                    norm1(1)
                end_stage()

                def scores(hp):
                    pe.wait_ge(pq_ready, HP * ph + hp + 1)
                    u = open_unit((ph, "sc", hp))
                    for t in range(NT[ph]):
                        last = nc.tensor.matmul(u[:, t * P:(t + 1) * P], pq_sb[hp % 2][:, t * P:(t + 1) * P],
                                                keysT[:, hp, :], start=True, stop=True)
                    close_unit((ph, "sc", hp), last)
                for hp in range(HP):
                    w = arrived((ph, "pq", hp - hp % 2))
                    feature_unit((ph, "pq", hp), w, (hp % 2) * P, featT)
                    if hp:
                        scores(hp - 1)
                scores(HP - 1)
                if ph == 0:
                    pe.wait_ge(state_ready, 2 * LB)
                    u = open_unit(("state",))
                    close_unit(("state",), nc.tensor.transpose(u[0:2 * LB, 0:P], state[:, :], ident[:, :]))
                end_stage()

        @block.scalar
        def _(act):
            chain = Chain(act, act_chain)
            stage = [0]

            def full(key):
                act.wait_ge(bank_full[bank[key]], use[key])
                return ps(key)

            def end_stage():
                stage[0] += 1
                act.drain().then_inc(act_stage, 1)
                act.wait_ge(pe_stage, stage[0])
                act.wait_ge(dve_stage, stage[0])

            def run(out, in_, func, **kw):
                return nc.scalar.activation(out, in_, func, **kw)

            u = full(("vcols",))
            chain.link(run(vcols[:, :], u[:, 0:P], ACT.Identity))
            act.drain().then_inc(vcols_ready, 1)
            run(silu_t[:, :], vcols[:, 0:2 * KD], ACT.Tanh, scale=0.5).then_inc(silu_half, 1)
            act.wait_ge(lam_abs, 1)
            run(sp[:, 1, :], sp[:, 0, :], ACT.Exp, scale=-1.0).then_inc(lam_exp, 1)
            u = full(("kctx",))
            chain.mark(run(kT[:, :, CTX:CTX + P], u[:, 0:KVW].rearrange("p (h s) -> p h s", h=NKV), ACT.Identity))
            chain.wait()
            act.drain().then_inc(bank_free[bank[("kctx",)]], 1)
            act.drain().then_inc(bank_free[bank[("vcols",)]], 1)
            end_stage()

            def soft(c):
                act.wait_ge(bestdiff, c + 1)
                run(best[:, 1, :], best[:, 1, :], ACT.Exp).then_inc(soft_ready, 1)

            def gelu_dots(c):
                act.wait_ge(dots_ready, c + 1)
                run(gel[:, :], dots[:, :], ACT.Square).then_inc(gsq_ready, 1)
                act.wait_ge(gcub_ready, c + 1)
                run(gel[:, :], gel[:, :], ACT.Tanh, scale=GELU_C * GELU_S).then_inc(gt_ready, 1)

            def final(c):
                act.wait_ge(fvar_ready, c + 1)
                run(nrm[:, 2 * NCH + c, 2:3], nrm[:, 2 * NCH + c, 1:2], ACT.Sqrt).then_inc(fstd_ready, 1)

            for ph in PHASES:
                N = TOK[ph]
                def norm1(ph):
                    for t in range(NT[ph]):
                        v = var1(ph, t)
                        act.wait_ge(var_ready, v + 1)
                        run(nrm[:, v, 2:3], nrm[:, v, 1:2], ACT.Sqrt).then_inc(std_ready, 1)
                    for t in range(NT[ph]):
                        for i in range(2):
                            u = full((ph, "xt", t, i))
                            for k in range(4):
                                f = 4 * i + k
                                last = run(hT[:, f, t * P:(t + 1) * P], u[:, k * P:(k + 1) * P], ACT.Identity,
                                           scale=mod_a[:, ph, f:f + 1], bias=mod_b[:, ph, f:f + 1])
                            last.then_inc(bank_free[bank[(ph, "xt", t, i)]], 1)
                if ph == 0:
                    norm1(0)
                    end_stage()

                def gelu_in(j):
                    u = full((ph, "xg", j))
                    run(featT[:, j, 0:N], u[:, 0:N], ACT.Square).then_inc(sq_ready, 1)
                    act.wait_ge(cub_ready, LB * ph + j + 1)
                    run(featT[:, j, 0:N], featT[:, j, 0:N], ACT.Tanh, scale=GELU_C * GELU_S).then_inc(gtanh_ready, 1)
                gelu_in(0)
                for j in range(LB):
                    B = LB * ph + j
                    if j + 1 < LB:
                        gelu_in(j + 1)
                    if j:
                        act.wait_ge(lru_done, B)
                    for d in range(2):
                        u = full((ph, "gate", j, 2 * d))
                        run(lt[d][:, 0:N], u[:, 0:N], ACT.Tanh, scale=0.5,
                            bias=half_b[:, d * LB + j:d * LB + j + 1]).then_inc(bank_free[bank[(ph, "gate", j, 2 * d)]], 1)
                        u = full((ph, "gate", j, 2 * d + 1))
                        run(lti[d][:, 0:N], u[:, 0:N], ACT.Tanh, scale=0.5,
                            bias=half_b[:, (2 + d) * LB + j:(2 + d) * LB + j + 1])\
                            .then_inc(bank_free[bank[(ph, "gate", j, 2 * d + 1)]], 1)
                    for d in range(2):
                        i = d * LB + j
                        act.wait_ge(bank_free[bank[(ph, "gate", j, 2 * d + 1)]], use[(ph, "gate", j, 2 * d + 1)])
                        chain.mark(run(lth[d][:, 0:N], lt[d][:, 0:N], ACT.Tanh, scale=sp[:, 7, i:i + 1], bias=sp[:, 7, i:i + 1]))
                        chain.mark(run(la[d][:, 0:N], lt[d][:, 0:N], ACT.Exp, scale=sp[:, 5, i:i + 1], bias=sp[:, 5, i:i + 1]))
                        run(le[d][:, 0:N], lt[d][:, 0:N], ACT.Exp, scale=sp[:, 6, i:i + 1], bias=sp[:, 6, i:i + 1])\
                            .then_inc(e2_ready, 1)
                    for d in range(2):
                        act.wait_ge(w_ready, 2 * B + d + 1)
                        run(le[d][:, 0:N], le[d][:, 0:N], ACT.Sqrt, scale=0.25).then_inc(root_ready, 1)
                end_stage()

                def merge(a, j0):
                    for m in range(KD):
                        i = 2 * KD * ph + j0 + m
                        if m >= 2:
                            act.wait_ge(mix_ready, i - 1)
                        u = full((ph, a, m))
                        chain.link(run(wk(2 + m % 2)[:, 0:N], u[:, 0:N], ACT.Tanh, scale=0.5))
                        act.drain().then_inc(bank_free[bank[(ph, a, m)]], 1)
                        act.drain().then_inc(rg_ready, 1)
                merge("gr", 0)

                if ph == 0:
                    u = full((ph, "kt"))
                    chain.link(run(kT[:, :, 0:P], u[:, 0:KVW].rearrange("p (h s) -> p h s", h=NKV), ACT.Identity))
                    act.drain().then_inc(bank_free[bank[(ph, "kt")]], 1)
                else:
                    for i in range(NT[ph] // 2):
                        u = full((ph, "v", i))
                        run(v_sb[:, 2 * i:2 * i + 2, :], u[:, :].rearrange("p (t n) -> p t n", t=2), ACT.Identity)\
                            .then_inc(bank_free[bank[(ph, "v", i)]], 1)
                if ph == 0:
                    for h in range(NH):
                        u = full((ph, "q", h))
                        run(featT[:, h, 0:N], u[:, 0:N], ACT.Identity).then_inc(bank_free[bank[(ph, "q", h)]], 1)
                end_stage()
                if ph:
                    gelu_dots(0)
                qs = quads(ph)

                def width(n):
                    return P if ph == 0 else (min(n + 1, NT[ph] - 1) - max(n - 1, 0) + 2) * P

                def exps(i):
                    Q = NKV * CH0[ph] + i
                    W = width(qs[i][0])
                    act.wait_ge(neg_ready, Q + 1)
                    run(q_es[:, Q, :], q_dif[:, Q, :], ACT.Exp).then_inc(act_chain, 1)
                    chain.n += 1
                    for h in range(G):
                        p_ = sm_pair[Q % 2][:, h, 0:W]
                        run(p_, p_, ACT.Exp, bias=q_neg[:, Q, h:h + 1], accum_out=q_sum[:, Q, h:h + 1])\
                            .then_inc(prob_ready, 1)
                exps(0)
                for i, q in enumerate(qs):
                    n, kv = q
                    Q = NKV * CH0[ph] + i
                    W = width(n)
                    if i + 1 < len(qs):
                        exps(i + 1)
                    for h in (1, 3):
                        u = full((ph, "pt", q, h))
                        values_done(act, Q, h)
                        run(pT[1][:, 0:W], u[:, 0:W], ACT.Identity).then_inc(pT_ready[1], 1)
                        act.wait_ge(pT_ready[1], G // 2 * Q + h // 2 + 1)
                        act.drain().then_inc(bank_free[bank[(ph, "pt", q, h)]], 1)
                    for j in ([i - 1] if i else []) + ([i] if i == len(qs) - 1 else []):
                        q = qs[j]
                        u = full((ph, "ot", q))
                        run(featT[:, q[1] * G:(q[1] + 1) * G, q[0] * P:(q[0] + 1) * P],
                            u[:, :].rearrange("p (h s) -> p h s", h=G), ACT.Identity).then_inc(attn_ready, 1)
                        act.drain().then_inc(bank_free[bank[(ph, "ot", q)]], 1)
                end_stage()
                merge("ga", KD)
                for t in range(NT[ph]):
                    v = var2(ph, t)
                    act.wait_ge(var_ready, v + 1)
                    run(nrm[:, v, 2:3], nrm[:, v, 1:2], ACT.Sqrt).then_inc(std_ready, 1)
                for t in range(NT[ph]):
                    for i in range(2):
                        u = full((ph, "h2", t, i))
                        run(featT[:, 4 * i:4 * i + 4, t * P:(t + 1) * P], u[:, :].rearrange("p (k s) -> p k s", k=4),
                            ACT.Identity).then_inc(bank_free[bank[(ph, "h2", t, i)]], 1)
                if ph == 0:
                    norm1(1)
                end_stage()
                for hp in range(HP):
                    u = full((ph, "pq", hp))
                    if hp >= 2:
                        s = (ph, "sc", hp - 2)
                        act.wait_ge(bank_full[bank[s]], use[s])
                    chain.link(run(pq_sb[hp % 2][:, 0:N], u[:, 0:N], ACT.Identity))
                    act.drain().then_inc(bank_free[bank[(ph, "pq", hp)]], 1)
                    act.drain().then_inc(pq_ready, 1)
                end_stage()
                if ph == 0:
                    soft(0)
            soft(C1)
            for step in steps:
                if step[0][0] == "u" and step[0][1] + 1 < NCH:
                    soft(step[0][1] + 1)
                for table, c in step:
                    if table == "u":
                        gelu_dots(c)
                if step is steps[0]:
                    final(0)
                for table, c in step:
                    if table == "v":
                        final(c)

        @block.vector
        def _(dve):
            V = nc.vector
            chain = Chain(dve, dve_chain)
            link, mark = chain.link, chain.mark
            stage = [0]

            def full(key):
                dve.wait_ge(bank_full[bank[key]], use[key])
                return ps(key)

            def free(key):
                dve.drain().then_inc(bank_free[bank[key]], 1)

            def end_stage():
                stage[0] += 1
                dve.drain().then_inc(dve_stage, 1)
                dve.wait_ge(pe_stage, stage[0])
                dve.wait_ge(act_stage, stage[0])

            def variance(v, src, scratch):
                link(V.tensor_tensor_reduce(scratch, src, src, 1.0, 0.0, ALU.mult, ALU.add, nrm[:, v, 0:1]))
                link(V.tensor_scalar(nrm[:, v, 1:2], nrm[:, v, 0:1], 1.0 / D, EPS, ALU.mult, ALU.add))

            def inverse_root(v):
                n = nrm[:, v, :]
                link(V.reciprocal(n[:, 3:4], n[:, 2:3]))
                link(V.tensor_tensor(n[:, 4:5], n[:, 3:4], n[:, 3:4], ALU.mult))
                link(V.tensor_tensor(n[:, 5:6], n[:, 4:5], n[:, 1:2], ALU.mult))
                link(V.tensor_scalar(n[:, 6:7], n[:, 5:6], -0.5, 1.5, ALU.mult, ALU.add))
                link(V.tensor_tensor(n[:, 7:8], n[:, 6:7], n[:, 3:4], ALU.mult))
                return n[:, 7:8]

            dve.wait_ge(vcols_ready, 1)
            lam = vcols[:, V_LAM:V_LAM + 2 * LB]
            link(V.tensor_scalar(sp[:, 2, :], lam, -1.0, None, ALU.mult))
            link(V.tensor_tensor(sp[:, 0, :], lam, sp[:, 2, :], ALU.max))
            dve.drain().then_inc(lam_abs, 1)
            link(V.tensor_scalar(sp[:, 2, :], sp[:, 2, :], 0.0, None, ALU.max))
            link(V.tensor_scalar(half_b[:, :], vcols[:, V_BA:V_BA + 4 * LB], 0.5, None, ALU.mult))
            dve.wait_ge(silu_half, 1)
            link(V.tensor_scalar(silu_t[:, :], silu_t[:, :], 0.5, 0.5, ALU.mult, ALU.add))
            V.tensor_tensor(siluT[:, :], silu_t[:, :], vcols[:, 0:2 * KD], ALU.mult).then_inc(silu_ready, 1)
            dve.wait_ge(lam_exp, 1)
            link(V.tensor_scalar(sp[:, 3, :], sp[:, 1, :], 2.0, None, ALU.add))
            link(V.reciprocal(sp[:, 4, :], sp[:, 3, :]))
            link(V.tensor_tensor(sp[:, 3, :], sp[:, 1, :], sp[:, 4, :], ALU.mult))
            link(V.tensor_tensor(sp[:, 4, :], sp[:, 3, :], sp[:, 3, :], ALU.mult))
            link(V.tensor_scalar(sp[:, 5, :], sp[:, 4, :], 1.0 / 15, 1.0 / 13, ALU.mult, ALU.add))
            for d in (11, 9, 7, 5, 3, 1):
                link(V.tensor_tensor(sp[:, 6, :], sp[:, 5, :], sp[:, 4, :], ALU.mult))
                link(V.tensor_scalar(sp[:, 5, :], sp[:, 6, :], 1.0 / d, None, ALU.add))
            link(V.tensor_tensor(sp[:, 6, :], sp[:, 5, :], sp[:, 3, :], ALU.mult))
            link(V.scalar_tensor_tensor(sp[:, 1, :], sp[:, 6, :], 2.0, sp[:, 2, :], ALU.mult, ALU.add))
            link(V.tensor_scalar(sp[:, 5, :], sp[:, 1, :], -4.0, None, ALU.mult))
            link(V.tensor_scalar(sp[:, 6, :], sp[:, 1, :], -8.0, None, ALU.mult))
            link(V.tensor_scalar(sp[:, 7, :], sp[:, 1, :], 4.0, None, ALU.mult))
            for i in range(HP // 4):
                u = full(("keys", i))
                mark(V.tensor_copy(keysT[:, 4 * i:4 * i + 4, :], u[:, :].rearrange("p (i n) -> p i n", i=4)))
                free(("keys", i))
            dve.wait_ge(bada_in, 16)
            for n in range(NADA):
                u = full(("ada", n))
                c = n * TC
                V.tensor_tensor(ada_sb[:, c:c + TC], u[0:2, 0:TC], b_ada[:, c:c + TC], ALU.add).then_inc(ada_ready, 1)
                free(("ada", n))
            u = full(("mod",))
            cols = u[:, 0:4 * KD].rearrange("p (c w k) -> p c w k", c=2, w=2)
            mark(V.tensor_copy(mod_b[:, :, :], cols[:, :, 0, :]))
            link(V.tensor_scalar(mod_a[:, :, :], cols[:, :, 1, :], 1.0, None, ALU.add))
            free(("mod",))
            for ci in range(2):
                link(V.tensor_tensor(mod_a[:, ci, :], mod_a[:, ci, :], vcols[:, V_G:V_G + KD], ALU.mult))
            end_stage()

            served = [None]

            def serve(n):
                for _ in range(n):
                    s_ = served[0]
                    if s_ is None or s_ == 2 * SLOTS or (s_ == SLOTS and not gelu0[0]):
                        return
                    r = s_ % RING0
                    dve.wait_ge(row0_in[r], 16 * (s_ // RING0 + 1))
                    if s_ < SLOTS:
                        V.tensor_tensor_reduce(ring0[r], ring0[r], h2_all[:, 0, :], 1.0, 0.0, ALU.mult, ALU.add,
                                               dots[:, s_:s_ + 1]).then_inc(slot0_used, 1)
                    else:
                        a_, w_ = acc0[s_ % 2], gw[:, 0, s_ - SLOTS:s_ - SLOTS + 1]
                        if s_ < SLOTS + 2:
                            V.tensor_scalar(a_, ring0[r], w_, None, ALU.mult).then_inc(slot0_used, 1)
                        else:
                            dve.wait_ge(slot0_used, RING0 + s_ - 1)
                            V.scalar_tensor_tensor(a_, ring0[r], w_, a_, ALU.mult, ALU.add).then_inc(slot0_used, 1)
                    served[0] += 1
            gelu0 = [False]

            def gelu_dots(c):
                if c == 0:
                    serve(SLOTS)
                    dve.wait_ge(slot0_used, RING0 + SLOTS)
                    gelu0[0] = True
                dve.drain().then_inc(dots_ready, 1)
                dve.wait_ge(gsq_ready, c + 1)
                V.scalar_tensor_tensor(gel[:, :], gel[:, :], 1.0 / GELU_C, dots[:, :], ALU.add, ALU.mult)\
                    .then_inc(gcub_ready, 1)
                dve.wait_ge(gt_ready, c + 1)
                link(V.scalar_tensor_tensor(gel[:, :], gel[:, :], 1.0, dots[:, :], ALU.add, ALU.mult))
                link(V.scalar_tensor_tensor(gw[:, c, :], gw[:, c, :], 0.5, gel[:, :], ALU.mult, ALU.mult))

            def add_sums(c, acc_):
                x = x_all[:, c, :]
                link(V.tensor_tensor(acc_[0], acc_[0], acc_[1], ALU.add))
                link(V.tensor_tensor(acc_[0], acc_[0], gf_row[:, 0 if c < NT[0] else 1, :], ALU.mult))
                link(V.tensor_tensor(x, x, acc_[0], ALU.add))

            def final(c, scratch):
                x, v = x_all[:, c, :], 2 * NCH + c
                variance(v, x, scratch)
                dve.drain().then_inc(fvar_ready, 1)
                dve.wait_ge(fstd_ready, c + 1)
                r = inverse_root(v)
                V.scalar_tensor_tensor(x, x, r, final_row[:, :], ALU.mult, ALU.mult).then_inc(y_ready, 1)
                dve.wait_ge(y_ready, c + 1)

            def route(c, part):
                tv = top_v[:, max(c - C1, 0), :, :].rearrange("p (h s) k -> p h s k", s=2)
                shape = [P, PH, TOPK, TOPK]
                bv = best[:, 0, :].rearrange("p (h k) -> p h k", h=PH)
                bp = pos[:, 0, :].rearrange("p (h k) -> p h k", h=PH)
                if part == 0:
                    sums = cand.rearrange("p (h i j) -> p h i j", h=PH, i=TOPK)
                    link(V.tensor_tensor(sums, tv[:, :, 0, :].unsqueeze(3).to_broadcast(shape),
                                         tv[:, :, 1, :].unsqueeze(2).to_broadcast(shape), ALU.add))
                if part < 2:
                    for h in range(part * PH // 2, (part + 1) * PH // 2):
                        s = cand[:, h * TOPK * TOPK:(h + 1) * TOPK * TOPK]
                        link(V.max(bv[:, h, 0:8], s))
                        link(V.max_index(bp[:, h, 0:8], bv[:, h, 0:8], s))
                        link(V.match_replace(s, bv[:, h, 0:8], s, NEG_BIG))
                        link(V.max(bv[:, h, 8:16], s))
                        link(V.max_index(bp[:, h, 8:16], bv[:, h, 8:16], s))
                    return
                onehot = hot.rearrange("p (h k i) -> p h k i", h=PH, k=TOPK)
                if part == 2:
                    link(V.tensor_tensor(best[:, 1, :].rearrange("p (h k) -> p h k", h=PH), bv,
                                         bv[:, :, 0:1].to_broadcast([P, PH, TOPK]), ALU.subtract))
                    dve.drain().then_inc(bestdiff, 1)
                    link(V.tensor_scalar(pos[:, 1, :], pos[:, 0, :], 4, None, ALU.logical_shift_right))
                    link(V.tensor_scalar(pos[:, 2, :], pos[:, 0, :], TOPK - 1, None, ALU.bitwise_and))
                    link(V.tensor_copy(sel[:, 0:2, :], pos[:, 1:3, :]))
                    link(V.tensor_copy(it_f[:, :, :], top_i[:, max(c - C1, 0), :, :]))
                itf = it_f[:, :, :].rearrange("p (h s) k -> p h s k", s=2)
                s = part - 2
                at = sel[:, s, :].rearrange("p (h k) -> p h k", h=PH)
                link(V.tensor_tensor(onehot, at.unsqueeze(3).to_broadcast(shape),
                                     iota16[:, :].unsqueeze(1).unsqueeze(1).to_broadcast(shape), ALU.is_equal))
                link(V.tensor_tensor(onehot, onehot, itf[:, :, s, :].unsqueeze(2).to_broadcast(shape), ALU.mult))
                link(V.tensor_reduce(sel[:, 2 + s, :].rearrange("p (h k) -> p h k", h=PH), onehot, AX_X, ALU.add))
                if part == PARTS - 1:
                    link(V.scalar_tensor_tensor(sel[:, 0, :], sel[:, 2, :], float(NKEY), sel[:, 3, :], ALU.mult, ALU.add))
                    link(V.tensor_copy(eidx[:, c, :], sel[:, 0, :]))
                    dve.wait_ge(soft_ready, c + 1)
                    e = best[:, 1, :].rearrange("p (h k) -> p h k", h=PH)
                    link(V.tensor_reduce(sred[:, 0, :], e, AX_X, ALU.add))
                    link(V.reciprocal(sred[:, 1, :], sred[:, 0, :]))
                    link(V.tensor_tensor(gw[:, c, :].rearrange("p (h k) -> p h k", h=PH), e,
                                         sred[:, 1, :].unsqueeze(2).to_broadcast([P, PH, TOPK]), ALU.mult))
                    dve.drain().then_inc(route_ready, 1)

            dve.wait_ge(x_in, 32)
            for ph in PHASES:
                N = TOK[ph]
                def norm1(ph):
                    for t in range(NT[ph]):
                        v = var1(ph, t)
                        if t >= 2:
                            u = (ph, "xt", t - 2, 1)
                            dve.wait_ge(bank_full[bank[u]], use[u])
                        x = x_all[:, CH0[ph] + t, :]
                        variance(v, x, xn[t % 2])
                        dve.drain().then_inc(var_ready, 1)
                        dve.wait_ge(std_ready, v + 1)
                        r = inverse_root(v)
                        V.tensor_scalar(xn[t % 2], x, r, None, ALU.mult).then_inc(xn_ready, 1)
                if ph == 0:
                    norm1(0)
                    end_stage()

                def conv(j):
                    B = LB * ph + j
                    w = [vcols[:, V_CW + i * KD + j:V_CW + i * KD + j + 1] for i in range(4)]
                    b = vcols[:, V_CB + j:V_CB + j + 1]
                    u, y = full((ph, "xr", j)), xc[j % 2]
                    if j >= 2:
                        s = (ph, "gate", j - 2, 3)
                        dve.wait_ge(bank_full[bank[s]], use[s])
                    link(V.tensor_scalar(y[:, 0:N], u[:, 0:N], w[2], b, ALU.mult, ALU.add))
                    link(V.scalar_tensor_tensor(y[:, 2:N], u[:, 0:N - 2], w[0], y[:, 2:N], ALU.mult, ALU.add))
                    link(V.scalar_tensor_tensor(y[:, 1:N], u[:, 0:N - 1], w[1], y[:, 1:N], ALU.mult, ALU.add))
                    link(V.scalar_tensor_tensor(y[:, 0:N - 1], u[:, 1:N], w[3], y[:, 0:N - 1], ALU.mult, ALU.add))
                    free((ph, "xr", j))
                    dve.drain().then_inc(xc_ready, 1)
                    g, f = full((ph, "xg", j)), featT[:, j, 0:N]
                    dve.wait_ge(sq_ready, B + 1)
                    V.scalar_tensor_tensor(f, f, 1.0 / GELU_C, g[:, 0:N], ALU.add, ALU.mult).then_inc(cub_ready, 1)
                    dve.wait_ge(gtanh_ready, B + 1)
                    link(V.scalar_tensor_tensor(f, f, 1.0, g[:, 0:N], ALU.add, ALU.mult))
                    free((ph, "xg", j))
                conv(0)
                for j in range(LB):
                    B = LB * ph + j
                    if j + 1 < LB:
                        conv(j + 1)
                    serve(2)
                    y = xc[j % 2][:, 0:N]
                    for d in range(2):
                        dve.wait_ge(e2_ready, 2 * B + d + 1)
                        V.scalar_tensor_tensor(le[d][:, 0:N], le[d][:, 0:N], 1.0, lth[d][:, 0:N],
                                               ALU.add, ALU.mult).then_inc(w_ready, 1)
                        mark(V.scalar_tensor_tensor(lti[d][:, 0:N], lti[d][:, 0:N], 1.0, y, ALU.add, ALU.mult))
                    chain.wait()
                    for d in range(2):
                        dve.wait_ge(root_ready, 2 * B + d + 1)
                        link(V.tensor_tensor(lti[d][:, 0:N], lti[d][:, 0:N], le[d][:, 0:N], ALU.mult))
                        h0 = 0.0 if ph == 0 else vcols[:, V_SF + d * KD + j:V_SF + d * KD + j + 1]
                        rev = slice(None, None, -1) if d else slice(None)
                        a_, b_, o_ = (t_[:, 0:N][:, rev] for t_ in (la[d], lti[d], lt[d]))
                        link(V.tensor_tensor_scan(o_, a_, b_, h0, ALU.mult, ALU.add))
                    if ph == 0:
                        V.tensor_copy(state[:, j:j + 1], lt[0][:, N - 1:N]).then_inc(state_ready, 1)
                        V.tensor_copy(state[:, LB + j:LB + j + 1], lt[1][:, 0:1]).then_inc(state_ready, 1)
                        dve.wait_ge(state_ready, 2 * j + 2)
                    serve(2)
                    link(V.tensor_tensor(lt[0][:, 0:N], lt[0][:, 0:N], lt[1][:, 0:N], ALU.add))
                    f = featT[:, j, 0:N]
                    link(V.scalar_tensor_tensor(f, lt[0][:, 0:N], 0.5, f, ALU.mult, ALU.mult))
                    dve.drain().then_inc(lru_done, 1)
                    serve(2)
                end_stage()

                def merge(a, o, j0):
                    for m in range(KD):
                        i = 2 * KD * ph + j0 + m
                        dve.wait_ge(rg_ready, i + 1)
                        u = full((ph, o, m))
                        t_ = wk(2 + m % 2)[:, 0:N]
                        if a == "gr":
                            link(V.scalar_tensor_tensor(mixT[:, m, 0:N], t_, 1.0, u[:, 0:N], ALU.add, ALU.mult))
                        else:
                            link(V.scalar_tensor_tensor(t_, t_, 1.0, u[:, 0:N], ALU.add, ALU.mult))
                            link(V.tensor_tensor(mixT[:, m, 0:N], mixT[:, m, 0:N], t_, ALU.add))
                        free((ph, o, m))
                        dve.drain().then_inc(mix_ready, 1)
                        serve(10 if a == "gr" else 8)
                merge("gr", "ro", 0)

                def rope(key, dst):
                    u = full(key)
                    mark(V.tensor_tensor(dst, u[:, 0:N], cos_sb[:, 0:N], ALU.mult))
                    mark(V.tensor_tensor(rope_tmp[0:64, 0:N], u[64:128, 0:N], sin_sb[64:128, 0:N], ALU.mult))
                    link(V.tensor_tensor(rope_tmp[64:128, 0:N], u[0:64, 0:N], sin_sb[0:64, 0:N], ALU.mult))
                    free(key)
                    link(V.tensor_tensor(dst, dst, rope_tmp[:, 0:N], ALU.add))
                if ph == 0:
                    u = full((ph, "kv"))
                    V.tensor_copy(ktok[:, :], u[:, 0:KVW]).then_inc(v_ready, 1)
                    V.tensor_copy(v_sb[:, 0, :], u[:, KVW:2 * KVW]).then_inc(v_ready, 1)
                    free((ph, "kv"))
                else:
                    for kv in range(NKV):
                        rope((ph, "k", kv), kT[:, kv, 0:N])
                    for h in range(NH):
                        rope((ph, "q", h), featT[:, h, 0:N])
                end_stage()
                if ph:
                    gelu_dots(0)
                qs = quads(ph)
                if True:
                    def soft(q):
                        n = q[0]
                        kv = q[1]
                        Q = NKV * CH0[ph] + quads(ph).index(q)
                        W = P if ph == 0 else (min(n + 1, NT[ph] - 1) - max(n - 1, 0) + 2) * P
                        for h in range(G):
                            u = full((ph, "s", q, h))
                            sm = sm_pair[Q % 2]
                            if ph == 0:
                                mark(V.tensor_scalar(sm[:, h, 0:W], u[:, 0:W], SCALE, None, ALU.mult))
                            else:
                                m0 = 1 if n == 0 else 0 if n < NT[ph] - 1 else 4
                                mk = mask[:, m0:m0 + W // P, :].rearrange("p i n -> p (i n)")
                                mark(V.scalar_tensor_tensor(sm[:, h, 0:W], u[:, 0:W], SCALE, mk, ALU.mult, ALU.add))
                            free((ph, "s", q, h))
                        chain.wait()
                        link(V.tensor_reduce(q_max[:, Q, :], sm[:, :, 0:W], AX_X, ALU.max))
                        sk = sink[:, kv * G:(kv + 1) * G]
                        link(V.tensor_tensor(q_max[:, Q, :], q_max[:, Q, :], sk, ALU.max))
                        link(V.tensor_tensor(q_dif[:, Q, :], sk, q_max[:, Q, :], ALU.subtract))
                        link(V.tensor_scalar(q_neg[:, Q, :], q_max[:, Q, :], -1.0, None, ALU.mult))
                        dve.drain().then_inc(neg_ready, 1)

                    soft(qs[0])
                    for i, q in enumerate(qs):
                        Q = NKV * CH0[ph] + i
                        n = q[0]
                        W = P if ph == 0 else (min(n + 1, NT[ph] - 1) - max(n - 1, 0) + 2) * P
                        if i + 1 < len(qs):
                            soft(qs[i + 1])
                        serve(2)
                        for h in (0, 2):
                            u = full((ph, "pt", q, h))
                            values_done(dve, Q, h)
                            V.tensor_copy(pT[0][:, 0:W], u[:, 0:W]).then_inc(pT_ready[0], 1)
                            dve.wait_ge(pT_ready[0], G // 2 * Q + h // 2 + 1)
                            free((ph, "pt", q, h))
                            serve(1)
                        dve.wait_ge(prob_ready, G * Q + G)
                        link(V.tensor_tensor(q_tot[:, Q, :], q_sum[:, Q, :], q_es[:, Q, :], ALU.add))
                        link(V.reciprocal(q_inv[:, Q, :], q_tot[:, Q, :]))
                        u = full((ph, "o", q))
                        if Q >= 2:
                            prev = ot_units[Q - 2]
                            dve.wait_ge(bank_full[bank[prev]], use[prev])
                        V.tensor_tensor(o_sb[Q % 2].rearrange("p (h d) -> p h d", h=G),
                                        u[:, :].rearrange("p (h d) -> p h d", h=G),
                                        q_inv[:, Q, :].unsqueeze(2).to_broadcast([P, G, P]), ALU.mult).then_inc(o_ready, 1)
                        dve.wait_ge(o_ready, Q + 1)
                        free((ph, "o", q))
                        serve(2)
                end_stage()
                merge("ga", "ao", KD)
                dve.wait_ge(rows_in, 64 * (ph + 1))
                for n in range(D // TC):
                    for t in range(NT[ph]):
                        u = full((ph, "mix", n, t))
                        x = x_all[:, CH0[ph] + t, n * TC:(n + 1) * TC]
                        link(V.scalar_tensor_tensor(mix_tmp[:, 0:TC], u[:, 0:TC], 0.5, gate_row[:, n * TC:(n + 1) * TC],
                                                    ALU.mult, ALU.mult))
                        free((ph, "mix", n, t))
                        link(V.tensor_tensor(x, x, mix_tmp[:, 0:TC], ALU.add))
                        serve(1)
                if ph:
                    serve(2 * SLOTS)
                    dve.wait_ge(slot0_used, RING0 + 2 * SLOTS)
                    add_sums(0, acc0)
                    dve.drain().then_inc(sums0_done, 1)
                link(V.scalar_tensor_tensor(scale_row, scale_row, 1.0, ffn_row, ALU.add, ALU.mult))
                for t in range(NT[ph]):
                    c = CH0[ph] + t
                    v = var2(ph, t)
                    variance(v, x_all[:, c, :], h2_all[:, c, :])
                    dve.drain().then_inc(var_ready, 1)
                    dve.wait_ge(std_ready, v + 1)
                    r = inverse_root(v)
                    link(V.scalar_tensor_tensor(h2_all[:, c, :], x_all[:, c, :], r, scale_row, ALU.mult, ALU.mult))
                    V.tensor_tensor(h2_all[:, c, :], h2_all[:, c, :], shift_row, ALU.add).then_inc(xn_ready, 1)
                if ph == 0:
                    norm1(1)
                end_stage()
                for hp in range(HP):
                    u = full((ph, "sc", hp))
                    for t in range(NT[ph]):
                        s = u[:, t * P:(t + 1) * P]
                        tv, ti = top_v[:, t, hp, :], top_i[:, t, hp, :]
                        cu = cut[:, (t % 4) * P:(t % 4 + 1) * P]
                        link(V.max(tv[:, 0:8], s))
                        mark(V.max_index(ti[:, 0:8], tv[:, 0:8], s))
                        link(V.match_replace(cu, tv[:, 0:8], s, NEG_BIG))
                        link(V.max(tv[:, 8:16], cu))
                        link(V.max_index(ti[:, 8:16], tv[:, 8:16], cu))
                    free((ph, "sc", hp))
                if ph == 0:
                    u = full(("state",))
                    link(V.tensor_copy(state_out[:, :], u[0:2 * LB, 0:P]))
                    free(("state",))
                    dve.drain().then_inc(state_turned, 1)
                end_stage()
                if ph == 0:
                    for part in range(PARTS):
                        route(0, part)
                    dve.drain().then_inc(slot0_used, RING0)
                    served[0] = 0

            for part in range(PARTS):
                route(C1, part)
            dve.drain().then_inc(group_used, NG)
            groups = turns = 0
            V.memset(dots_ring[:, :], 0.0).then_inc(peer_dve, 1)
            done = 1
            for step in steps:
                per = RING // len(step)
                has_u = step[0][0] == "u"
                has_v = step[-1][0] == "v"
                if has_v:
                    for a_ in acc:
                        V.memset(a_, 0.0).then_inc(peer_dve, 1)
                    done += 2
                    dve.wait_ge(peer_dve, done)
                each = (per if has_v else 0) + (1 if has_u else 0)
                turns_all = len(step) * SLOTS // RING
                iters = turns_all // PARTS
                for part in range(PARTS):
                    with dve.Fori(0, iters) as it:
                        k = 0
                        for r in range(RING):
                            table, c = step[r % len(step)]
                            q = r // len(step)
                            if r == 0:
                                dve.wait_ge(peer_dve, it * each + done)
                            dve.wait_ge(row_in[r], (it + (turns + 1)) * 16)
                            if table == "u":
                                ins_ = V.tensor_tensor_reduce(ring[r], ring[r], h2_all[:, c, :], 1.0, 0.0,
                                                              ALU.mult, ALU.add, dots_ring[:, r:r + 1])
                            else:
                                if k >= 2:
                                    dve.wait_ge(peer_dve, it * each + (done + k - 1))
                                w_ = gw[:, c, bass.ds(it * per + (part * iters * per + q), 1)]
                                ins_ = V.scalar_tensor_tensor(acc[k % 2], ring[r], w_, acc[k % 2], ALU.mult, ALU.add)
                                ins_.then_inc(peer_dve, 1)
                                k += 1
                            if r % GS == GS - 1:
                                if table == "u":
                                    ins_.then_inc(group_used, 1)
                                else:
                                    dve.drain().then_inc(group_used, 1)
                        if has_u:
                            dve.wait_ge(group_used, it * NG + (NG + groups + NG))
                            src = dots_ring[:, :].rearrange("p (q s) -> p q s", s=len(step))[:, :, 0]
                            V.tensor_copy(dots[:, bass.ds(it * per + part * iters * per, per)], src).then_inc(peer_dve, 1)
                    groups += iters * NG
                    turns += iters
                    done += iters * each
                    if has_u and step[0][1] + 1 < NCH:
                        route(step[0][1] + 1, part)
                dve.wait_ge(peer_dve, done)
                for table, c in step:
                    if table == "u":
                        gelu_dots(c)
                if step is steps[0]:
                    dve.wait_ge(final_in, 48)
                    final(0, ring0_more[:, 0, :])
                for table, c in step:
                    if table == "v":
                        add_sums(c, acc)
                        final(c, acc[1])

        @block.gpsimd
        def _(pool):
            g = nc.gpsimd
            g.memset(pad[:, :], 0.0).then_inc(idx_seen, 1)
            pool.wait_ge(idx_seen, 1)
            pool.wait_ge(route_ready, 1)
            sets = 0

            def rows0(table, first_slot, first_row, turn_slots, turn):
                r, used, sets_ = first_slot % RING0, turn * RING0 + first_slot, turn * (RING0 // GS0) + sets
                pool.wait_ge(slot0_used, used + GS0)
                src = eidx[:, 0, bass.ds(turn * RING0 + first_row, GS0)]
                g.tensor_copy(idx_ring[:, r:r + GS0], src).then_inc(idx_set, 1)
                pool.wait_ge(idx_set, sets_ + 1 + turn_slots)
                g.tensor_tensor(pad[:, :], pad[:, :], pad[:, :], ALU.add).then_inc(idx_seen, 1)
                for i in range(GS0):
                    g.indirect_dma_start(ring0[r + i], None, ins["peer_" + table][0],
                                         bass.IndirectOffsetOnAxis(ap=idx_ring[:, r + i:r + i + 1], axis=0))\
                        .then_inc(row0_in[r + i], 16)

            slot_ = 0
            for table in "uv":
                row = 0
                while row < SLOTS:
                    whole = (SLOTS - row) // RING0 if slot_ % RING0 == 0 else 0
                    if whole:
                        with pool.Fori(0, whole) as turn:
                            for n in range(RING0 // GS0):
                                rows0(table, slot_ + n * GS0, row + n * GS0, n, turn)
                        n = whole * RING0
                    else:
                        rows0(table, slot_, row, 0, 0)
                        n = GS0
                    slot_, row, sets = slot_ + n, row + n, sets + n // GS0

            groups = 0
            for step in steps:
                pool.wait_ge(route_ready, step[0][1] + 1)
                iters = len(step) * SLOTS // RING
                per = GS // len(step)
                with pool.Fori(0, iters) as it:
                    for n in range(NG):
                        pool.wait_ge(group_used, it * NG + (groups + n + 1))
                        for s, (table, c) in enumerate(step):
                            dst = idx_ring[:, n * GS:(n + 1) * GS].rearrange("p (q s) -> p q s", s=len(step))[:, :, s]
                            src = eidx[:, c, bass.ds(it * (per * NG) + n * per, per)]
                            g.tensor_copy(dst, src).then_inc(idx_set, 1)
                        pool.wait_ge(idx_set, it * (NG * len(step)) + (sets + (n + 1) * len(step)))
                        g.tensor_tensor(pad[:, :], pad[:, :], pad[:, :], ALU.add).then_inc(idx_seen, 1)
                        for i in range(GS):
                            r = n * GS + i
                            table, c = step[r % len(step)]
                            g.indirect_dma_start(ring[r], None, ins["peer_u" if table == "u" else "peer_v"][0],
                                                 bass.IndirectOffsetOnAxis(ap=idx_ring[:, r:r + 1], axis=0))\
                                .then_inc(row_in[r], 16)
                groups += iters * NG
                sets += iters * NG * len(step)



_INS = ['x_prompt', 'x_sample', 'c', 'cache_k', 'cache_v', 'state_h_fwd', 'state_h_bwd', 'c_ctx', 'norm_attn_g',
        'norm_ffn_g', 'final_g', 'w_ada', 'b_ada', 'w_in', 'attn_sink', 'conv_w', 'conv_b', 'lru_w_a', 'lru_b_a',
        'lru_w_i', 'lru_b_i', 'lru_lambda', 'w_attn_o', 'w_rnn_o', 'w_out', 'peer_w_q', 'peer_keys', 'peer_u',
        'peer_v']
_OUTS = [((1, 128, 1024), 'float32'), ((1, 512, 1024), 'float32'), ((1, 1, 128, 2, 128), 'float32'),
         ((1, 1, 128, 2, 128), 'float32'), ((1, 1, 1024), 'float32'), ((1, 1, 1024), 'float32')]


def _constants(np, tokens, head_dim, block, grid_w, topk):
    freqs = head_dim // 4
    rows = tokens // grid_w
    row = np.repeat(np.arange(rows, dtype=np.float32), grid_w)
    col = np.tile(np.arange(grid_w, dtype=np.float32), rows)
    inv = (np.float32(10000.0) ** (-np.arange(freqs, dtype=np.float32) / np.float32(freqs))).astype(np.float32)
    ang = np.concatenate([row[:, None] * inv, col[:, None] * inv], axis=-1).T
    cos, sin = np.cos(ang).astype(np.float32), np.sin(ang).astype(np.float32)
    q, k = np.arange(block)[:, None], np.arange(block)[None, :]
    before = np.where(k >= q, 0.0, -1e30).astype(np.float32)
    after = np.where(k <= q, 0.0, -1e30).astype(np.float32)
    none = np.zeros_like(before)
    return {
        "rope_cos": np.concatenate([cos, cos]), "rope_sin": np.concatenate([sin, -sin]),
        "mask": np.concatenate([before, none, after, none, before, none, none], axis=1),
        "ident": np.eye(block, dtype=np.float32),
        "iota16": np.broadcast_to(np.arange(topk, dtype=np.float32), (block, topk)).copy(),
    }


def kernel(**inputs):
    import numpy as _np
    import concourse.bacc as _bacc
    from concourse import mybir as _mybir
    from concourse.bass_utils import run_bass_kernel_spmd as _run

    nc = _bacc.Bacc("TRN2", target_bir_lowering=False, num_devices=1)
    arrays, ins, outs = {}, {}, []
    given = {name: _np.ascontiguousarray(inputs[name]) for name in _INS}
    given.update(_constants(_np, 512, 128, 128, 64, 16))
    for name, a in given.items():
        arrays[f"in_{name}_dram"] = a
        ins[name] = nc.dram_tensor(f"in_{name}_dram", a.shape, _mybir.dt.from_np(a.dtype), kind="ExternalInput").ap()
    for i, (shape, dtype) in enumerate(_OUTS):
        dt = _mybir.dt.from_np(_np.dtype(dtype))
        outs.append(nc.dram_tensor(f"out_{i}_dram", shape, dt, kind="ExternalOutput").ap())
    scratch = nc.dram_tensor("ada_scratch", (2, 6144), _mybir.dt.float32, kind="Internal").ap()
    hybrid_step(nc, ins, outs, scratch)
    r = _run(nc, [arrays], core_ids=[0])
    return tuple(r.results[0][f"out_{i}_dram"] for i in range(len(_OUTS)))
```

```python
from contextlib import ExitStack

import concourse.bass as bass
from concourse import mybir

ALU = mybir.AluOpType
ACT = mybir.ActivationFunctionType
AX_X = mybir.AxisListType.X
F32 = mybir.dt.float32
U32 = mybir.dt.uint32

P = 128
GELU_C = 0.044715
GELU_S = 0.7978845608028654
NEG_BIG = -3.0e38


class Chain:

    def __init__(self, eng, sem):
        self.eng, self.sem, self.n = eng, sem, 0

    def mark(self, ins):
        self.n += 1
        ins.then_inc(self.sem, 1)
        return self.n

    def wait(self, n=None):
        self.eng.wait_ge(self.sem, self.n if n is None else n)

    def link(self, ins):
        self.mark(ins)
        self.wait()


def hybrid_step(nc, ins, outs, ada_scratch):
    y_prompt, y_sample, new_k, new_v, new_hf, new_hb = outs
    D = ins["w_in"].shape[1]
    KD = D // P
    HD = ins["cache_k"].shape[-1]
    NKV = ins["cache_k"].shape[-2]
    NH = ins["attn_sink"].shape[-1]
    G = NH // NKV
    KVW = NKV * HD
    LB = ins["lru_w_a"].shape[2]
    HP = ins["peer_keys"].shape[1] * 2
    PH = HP // 2
    NKEY = ins["peer_keys"].shape[3]
    TOPK = 16
    SLOTS = PH * TOPK
    EPS = 1e-6
    SCALE = float(HD) ** -0.5
    TC = 256
    C_Q, C_K, C_V = 0, NH * HD, NH * HD + KVW
    C_XR = C_V + KVW
    C_XG, C_GA = C_XR + D, C_XR + 2 * D
    C_GR = C_GA + D
    assert KVW == TC
    assert HD == P and NKEY == P and SLOTS == P and LB == KD

    TOK = [ins["x_prompt"].shape[1], ins["x_sample"].shape[1]]
    NT = [n // P for n in TOK]
    CH0 = [0, NT[0]]
    NCH = sum(NT)
    PHASES = (0, 1)
    CTX = TOK[1]

    bank, use, order = {}, {}, []
    bank_uses = [0] * 8

    def unit(key, b):
        bank[key] = b
        bank_uses[b] += 1
        use[key] = bank_uses[b]
        order.append(key)

    AHEAD = 4

    def quads(ph):
        return [(n, kv) for kv in range(NKV) for n in range(NT[ph])]

    unit(("vcols",), 0)
    for i in range(HP // 4):
        unit(("keys", i), 1 + i % 3)
    unit(("kctx",), 4)
    NADA = ins["w_ada"].shape[2] // TC
    per_c = NADA // 6
    ada_first = [*range(2 * per_c), *range(4 * per_c, 5 * per_c)]
    ada_lru, ada_topk = list(range(2 * per_c, 4 * per_c)), list(range(5 * per_c, NADA))
    assert len(ada_lru) == LB
    for i, n in enumerate(ada_first):
        unit(("ada", n), i % 4)
    unit(("mod",), 4)
    def norm1_units(ph):
        for t in range(NT[ph]):
            for i in range(2):
                unit((ph, "xt", t, i), 2 * (t % 2) + i)

    for ph in PHASES:
        if ph == 0:
            norm1_units(0)

        def gates(j):
            for g in range(4):
                unit((ph, "gate", j, g), 4 + g)

        def output_units(a, o):
            for m in range(KD):
                unit((ph, o, m), 4 + m % 4)
                if m + AHEAD < KD:
                    unit((ph, a, m + AHEAD), m % AHEAD)
        for j in range(LB):
            unit((ph, "xr", j), 2 * (j % 2))
            unit((ph, "xg", j), 2 * (j % 2) + 1)
            if ph and j >= LB - NKV:
                unit((ph, "k", j - LB + NKV), 2 * ((j + 1) % 2))
                unit((ph, "v", j - LB + NKV), 2 * ((j + 1) % 2) + 1)
            if ph == 0:
                unit(("ada", ada_lru[j]), 7)
            if j:
                gates(j - 1)
        gates(LB - 1)
        for m in range(AHEAD):
            unit((ph, "gr", m), m % AHEAD)
        output_units("gr", "ro")
        if ph == 0:
            unit((ph, "kv"), 0)
            unit((ph, "kt"), 1)
        for h in range(NH):
            unit((ph, "q", h), 4 + h % G)
        qs = quads(ph)
        for h in range(G):
            unit((ph, "s", qs[0], h), h)
        for i, q in enumerate(qs):
            if i + 1 < len(qs):
                for h in range(G):
                    unit((ph, "s", qs[i + 1], h), h)
            unit((ph, "o", q), 6)
            if i == len(qs) - 1:
                unit((ph, "ga", 0), 0)
            for h in range(G):
                unit((ph, "pt", q, h), 4 + h % 2)
            if i:
                unit((ph, "ot", qs[i - 1]), 7)
        unit((ph, "ga", 1), 1)
        unit((ph, "ot", qs[-1]), 7)
        for m in range(2, AHEAD):
            unit((ph, "ga", m), m)
        output_units("ga", "ao")
        def h2_units(t):
            for i in range(2):
                unit((ph, "h2", t, i), 4 + 2 * (t % 2) + i)
        for t in range(NT[ph]):
            for n in range(D // TC):
                unit((ph, "mix", n, t), n)
            if t:
                h2_units(t - 1)
        h2_units(NT[ph] - 1)
        if ph == 0:
            norm1_units(1)
        ada_after = {3 * i + 3: n for i, n in enumerate(ada_topk)}
        for hp in range(HP):
            unit((ph, "pq", hp), 4 + hp % 2)
            if hp:
                unit((ph, "sc", hp - 1), (hp - 1) % 2)
                if ph == 0 and hp in ada_after:
                    unit(("ada", ada_after[hp]), 2)
        unit((ph, "sc", HP - 1), (HP - 1) % 2)
        if ph == 0:
            unit(("state",), 7)

    WR = 4
    tiles, last_unit = [], {}

    def tile(key, unit_key):
        tiles.append(key)
        last_unit[key] = unit_key

    tile(("keys",), ("keys", HP // 4 - 1))
    for n in ada_first:
        tile(("ada", n), ("ada", n))
    for ph in PHASES:
        def output_tiles(a, o):
            for m in range(0, AHEAD, 2):
                tile((ph, a, m), (ph, a, m + 1))
            for m in range(0, KD, 2):
                tile((ph, o, m), (ph, o, m + 1))
                if m + AHEAD < KD:
                    tile((ph, a, m + AHEAD), (ph, a, m + AHEAD + 1))
        for j in range(0, LB, 2):
            tile((ph, "xr", j), (ph, "xr", j + 1))
            tile((ph, "xg", j), (ph, "xg", j + 1))
            if ph == 0:
                for n in ada_lru[j:j + 2]:
                    tile(("ada", n), ("ada", n))
        if ph:
            tile((ph, "k"), (ph, "k", NKV - 1))
            tile((ph, "v"), (ph, "v", NT[1] // 2 - 1))
        output_tiles("gr", "ro")
        if ph == 0:
            tile((ph, "k"), (ph, "kv"))
            tile((ph, "v"), (ph, "kv"))
        for h in range(0, NH, 2):
            tile((ph, "q", h), (ph, "q", h + 1))
        output_tiles("ga", "ao")
        for n in range(D // TC):
            tile((ph, "out", n), (ph, "mix", n, NT[ph] - 1))
        for i in range(0, HP, 2):
            tile((ph, "pq", i), (ph, "pq", i + 1))
            for hp in (i, i + 1):
                if ph == 0 and hp in ada_after:
                    tile(("ada", ada_after[hp]), ("ada", ada_after[hp]))
    slot = {key: i % WR for i, key in enumerate(tiles)}
    fill = {key: i // WR + 1 for i, key in enumerate(tiles)}

    def tile_source(key):
        if key == ("keys",):
            return ins["peer_keys"][0].rearrange("h t n d -> n (h t) d")
        if key[0] == "ada":
            w, c = ins["w_ada"][0], key[1] * TC
        else:
            ph, what, i = (*key, 0)[:3]
            w_in = ins["w_in"][0]
            w, c = {
                "xr": (w_in, C_XR + i * P), "xg": (w_in, C_XG + i * P),
                "gr": (w_in, C_GR + i * P), "ga": (w_in, C_GA + i * P),
                "k": (w_in, C_K), "v": (w_in, C_V), "q": (w_in, C_Q + i * P),
                "ro": (ins["w_rnn_o"][0], i * P), "ao": (ins["w_attn_o"][0], i * P),
                "out": (ins["w_out"][0], i * TC), "pq": (ins["peer_w_q"][0], i * P),
            }[what]
        return w.rearrange("(k p) n -> p k n", p=P)[:, :, c:c + TC]

    GS, NG = 4, 4
    RING = GS * NG
    C1 = CH0[1]
    steps = [[("u", C1)]] + [[("u", c + 1), ("v", c)] for c in range(C1, NCH - 1)] + [[("v", NCH - 1)]]
    PARTS = 4
    GS0, RING0 = 1, 5
    assert NT[0] == 1

    with ExitStack() as ctx:
        def sb(name, shape, dt=F32):
            return ctx.enter_context(nc.sbuf_tensor(name, shape, dt))

        def sem(name):
            return ctx.enter_context(nc.semaphore(name))

        N1 = TOK[1]
        TILE = KD * TC
        big = sb("big", [P, WR * TILE + 2 * KD * N1])
        w_tile = [big[:, s * TILE:(s + 1) * TILE].rearrange("p (k n) -> p k n", k=KD) for s in range(WR)]
        keys_tile = big[:, slot[("keys",)] * TILE:(slot[("keys",)] + 1) * TILE].rearrange("p (i d) -> p i d", i=HP)
        o_h = WR * TILE
        hT = big[:, o_h:o_h + KD * N1].rearrange("p (k n) -> p k n", k=KD)
        featT = big[:, o_h + KD * N1:o_h + 2 * KD * N1].rearrange("p (k n) -> p k n", k=KD)
        assert RING * D <= WR * TILE + 2 * KD * N1
        ring = [big[:, r * D:(r + 1) * D] for r in range(RING)]

        mix_region = sb("mix_region", [P, KD * N1])
        mixT = mix_region[:, :].rearrange("p (k n) -> p k n", k=KD)
        lru_w = mix_region[:, :].rearrange("p (w n e) -> p w n e", w=4, n=LB)
        top_v = mix_region[:, 0:4 * HP * TOPK].rearrange("p (t h k) -> p t h k", t=4, h=HP)
        top_i = mix_region[:, 4 * HP * TOPK:8 * HP * TOPK].bitcast(U32).rearrange("p (t h k) -> p t h k", t=4, h=HP)
        acc = [mix_region[:, (2 + i) * D:(3 + i) * D] for i in range(2)]
        assert 8 * HP * TOPK <= 2 * D

        work = sb("work", [P, 12 * N1])

        def wk(i, n=1):
            return work[:, i * N1:(i + n) * N1]
        xc = [wk(0), wk(1)]
        lt, la, le, lth, lti = ([wk(2 + 2 * i), wk(3 + 2 * i)] for i in range(5))
        sm_pair = [wk(4 * i, 4).rearrange("p (h n) -> p h n", h=G) for i in range(2)]
        pT = [wk(8), wk(9)]
        o_sb = [wk(10), wk(11)]
        rope_tmp = wk(11)
        xn = [wk(0, 2), wk(2, 2)]
        gate_row, scale_row, shift_row, ffn_row = wk(4, 2), wk(6, 2), wk(8, 2), wk(10, 2)
        mix_tmp = wk(0)
        pq_sb = [wk(0), wk(1)]
        cut = wk(2)
        cand = wk(4, 4)
        hot = wk(8, 4)
        b_ada = work[0:2, 0:NADA * TC]
        ada_sb = big[0:2, o_h:o_h + NADA * TC]
        assert NADA * TC <= 12 * N1 and NADA * TC <= 2 * KD * N1

        x_all = sb("x_all", [P, NCH, D])
        h2_all = sb("h2_all", [P, NCH, D])
        ada_late = {2: h2_all[0:2, C1 + 1:C1 + 3, :], 5: h2_all[0:2, C1:C1 + 1, :]}
        kT = sb("kT", [P, NKV, N1 + P])
        v_sb = sb("v_sb", [P, NT[1] + 1, KVW])
        ktok = sb("ktok", [P, KVW])
        keysT = sb("keysT", [P, HP, NKEY])
        cos_sb = sb("cos_sb", [P, N1])
        sin_sb = sb("sin_sb", [P, N1])
        mask = sb("mask", [P, 7, P])
        ident = sb("ident", [P, P])
        vrows = sb("vrows", [P, P])
        vcols = sb("vcols", [P, P])
        mod_rows = sb("mod_rows", [4 * KD, P])
        mod_b = sb("mod_b", [P, 2, KD])
        mod_a = sb("mod_a", [P, 2, KD])
        gf_row = sb("gf_row", [P, 2, D])
        final_row = sb("final_row", [P, D])
        sink = sb("sink", [P, NH])
        silu_t = sb("silu_t", [P, 2 * KD])
        siluT = sb("siluT", [P, 2 * KD])
        sp = sb("sp", [P, 8, 2 * LB])
        half_b = sb("half_b", [P, 4 * LB])
        nq = NKV * (NT[0] + NT[1])
        q_max, q_neg, q_dif, q_sum, q_es, q_tot, q_inv = (
            sb(n, [P, nq, G]) for n in ("q_max", "q_neg", "q_dif", "q_sum", "q_es", "q_tot", "q_inv"))
        nrm = sb("nrm", [P, 3 * NCH, 8])
        state = sb("state", [P, 2 * LB])
        state_out = sb("state_out", [2 * LB, P])
        eidx = sb("eidx", [P, NCH, SLOTS], U32)
        gw = sb("gw", [P, NCH, SLOTS])
        iota16 = sb("iota16", [P, TOPK])
        best = sb("best", [P, 3, SLOTS])
        pos = sb("pos", [P, 3, SLOTS], U32)
        sel = sb("sel", [P, 4, SLOTS])
        it_f = sb("it_f", [P, HP, TOPK])
        sred = sb("sred", [P, 2, PH])
        dots_ring = sb("dots_ring", [P, RING])
        dots = sb("dots", [P, SLOTS])
        gel = sb("gel", [P, SLOTS])
        idx_ring = sb("idx_ring", [P, RING], U32)
        pad = sb("pad", [P, 1])
        ring0_more = sb("ring0_more", [P, 2, D])
        ring0 = [h2_all[:, c, :] for c in range(C1 + 1, NCH)] + [ring0_more[:, i, :] for i in range(2)]
        assert len(ring0) == RING0
        acc0 = [gf_row[:, 1, :], final_row[:, :]]

        psum = [ctx.enter_context(nc.psum_tensor(f"bank{b}", [P, 512], F32)) for b in range(8)]

        def ps(key):
            return psum[bank[key]]

        bank_full = [sem(f"bank_full{b}") for b in range(8)]
        bank_free = [sem(f"bank_free{b}") for b in range(8)]
        tile_full = [sem(f"tile_full{s}") for s in range(WR)]
        act_chain, dve_chain = sem("act_chain"), sem("dve_chain")
        act_stage, dve_stage, pe_stage = sem("act_stage"), sem("dve_stage"), sem("pe_stage")
        consts_in, vrows_in, kctx_in, bada_in, x_in, rows_in, final_in, lru_in = map(
            sem, ("consts_in", "vrows_in", "kctx_in", "bada_in", "x_in", "rows_in", "final_in", "lru_in"))
        ada_saved, mod_in = sem("ada_saved"), sem("mod_in")
        vcols_ready, silu_half, silu_ready, ada_ready = map(
            sem, ("vcols_ready", "silu_half", "silu_ready", "ada_ready"))
        lam_abs, lam_exp = sem("lam_abs"), sem("lam_exp")
        var_ready, std_ready, xn_ready = map(sem, ("var_ready", "std_ready", "xn_ready"))
        xc_ready, sq_ready, cub_ready, gtanh_ready = map(sem, ("xc_ready", "sq_ready", "cub_ready", "gtanh_ready"))
        e2_ready, w_ready, root_ready = map(sem, ("e2_ready", "w_ready", "root_ready"))
        lru_done = sem("lru_done")
        rg_ready, mix_ready = sem("rg_ready"), sem("mix_ready")
        v_ready = sem("v_ready")
        neg_ready, prob_ready, o_part, o_ready, attn_ready = map(
            sem, ("neg_ready", "prob_ready", "o_part", "o_ready", "attn_ready"))
        pT_ready = [sem("pT_even_ready"), sem("pT_odd_ready")]
        pq_ready = sem("pq_ready")
        state_ready, state_turned = sem("state_ready"), sem("state_turned")
        soft_ready, route_ready = sem("soft_ready"), sem("route_ready")
        bestdiff = sem("bestdiff")
        row_in = [sem(f"row_in{r}") for r in range(RING)]
        row0_in = [sem(f"row0_in{r}") for r in range(RING0)]
        slot0_used, sums0_done = sem("slot0_used"), sem("sums0_done")
        group_used, idx_set, idx_seen = sem("group_used"), sem("idx_set"), sem("idx_seen")
        dots_ready, gsq_ready, gcub_ready, gt_ready = map(sem, ("dots_ready", "gsq_ready", "gcub_ready", "gt_ready"))
        peer_dve = sem("peer_dve")
        fvar_ready, fstd_ready, y_ready = sem("fvar_ready"), sem("fstd_ready"), sem("y_ready")
        saved = sem("saved")

        block = ctx.enter_context(nc.Block())

        V_C, V_G, V_LAM, V_BA, V_BI, V_CW, V_CB, V_SF = 0, 16, 24, 40, 56, 72, 104, 112

        def var1(ph, t):
            return t if ph == 0 else 2 * NT[0] + t

        def var2(ph, t):
            return NT[0] + t if ph == 0 else 2 * NT[0] + NT[1] + t

        o_units = [(ph, "o", q) for ph in PHASES for q in quads(ph)]
        ot_units = [(ph, "ot", q) for ph in PHASES for q in quads(ph)]

        def values_done(eng, Q, h):
            if h >= 2:
                eng.wait_ge(o_part, (G - 1) * Q + h - 1)
            elif Q:
                eng.wait_ge(bank_full[bank[o_units[Q - 1]]], use[o_units[Q - 1]])

        @block.sync
        def _(sp_):
            for r0, src in (
                (V_C, ins["c_ctx"].rearrange("(r x) -> r x", x=P)),
                (V_C + KD, ins["c"].rearrange("o (r x) -> (o r) x", x=P)),
                (V_G, ins["norm_attn_g"].rearrange("o (r x) -> (o r) x", x=P)),
                (V_LAM, ins["lru_lambda"].rearrange("o d (r x) -> (o d r) x", x=P)),
                (V_BA, ins["lru_b_a"].rearrange("o d (r x) -> (o d r) x", x=P)),
                (V_BI, ins["lru_b_i"].rearrange("o d (r x) -> (o d r) x", x=P)),
                (V_CW, ins["conv_w"].rearrange("o d (r x) -> (o d r) x", x=P)),
                (V_CB, ins["conv_b"].rearrange("o (r x) -> (o r) x", x=P)),
                (V_SF, ins["state_h_fwd"].rearrange("b o (r x) -> (b o r) x", x=P)),
                (V_SF + KD, ins["state_h_bwd"].rearrange("b o (r x) -> (b o r) x", x=P)),
            ):
                sp_.dma_start(vrows[r0:r0 + src.shape[0], :], src).then_inc(vrows_in, 16)
            sp_.dma_start(ident[:, :], ins["ident"]).then_inc(consts_in, 16)

            def load_tile(key):
                i = tiles.index(key)
                if i >= WR:
                    u = last_unit[tiles[i - WR]]
                    sp_.wait_ge(bank_full[bank[u]], use[u])
                dst = keys_tile if key == ("keys",) else w_tile[slot[key]]
                sp_.dma_start(dst, tile_source(key)).then_inc(tile_full[slot[key]], 16)

            load_tile(("keys",))
            sp_.dma_start(cos_sb[:, :], ins["rope_cos"]).then_inc(consts_in, 16)
            sp_.dma_start(sin_sb[:, :], ins["rope_sin"]).then_inc(consts_in, 16)
            sp_.dma_start(mask[:, :, :], ins["mask"].rearrange("p (i n) -> p i n", n=P)).then_inc(consts_in, 16)
            sp_.dma_start(iota16[:, :], ins["iota16"]).then_inc(consts_in, 16)
            sp_.dma_start(sink[:, :], ins["attn_sink"].partition_broadcast(P).rearrange("p o h -> p (o h)")).then_inc(consts_in, 16)
            sp_.dma_start(ktok[:, :], ins["cache_k"][0, 0].rearrange("s h d -> s (h d)")).then_inc(kctx_in, 16)
            sp_.dma_start(v_sb[:, NT[1], :], ins["cache_v"][0, 0].rearrange("s h d -> s (h d)")).then_inc(kctx_in, 16)
            sp_.dma_start(b_ada, ins["b_ada"][0:1, :].partition_broadcast(2).rearrange("p o n -> p (o n)")).then_inc(bada_in, 16)
            sp_.dma_start(ada_late[2], ins["b_ada"][0:1, 2 * D:4 * D].partition_broadcast(2)
                          .rearrange("p o (c n) -> p (o c) n", c=2)).then_inc(bada_in, 16)
            sp_.dma_start(ada_late[5], ins["b_ada"][0:1, 5 * D:6 * D].partition_broadcast(2)).then_inc(bada_in, 16)
            sp_.dma_start(x_all[:, 0:NT[0], :], ins["x_prompt"][0].rearrange("(t p) d -> p t d", p=P)).then_inc(x_in, 16)
            sp_.dma_start(x_all[:, NT[0]:NCH, :], ins["x_sample"][0].rearrange("(t p) d -> p t d", p=P)).then_inc(x_in, 16)
            def load_lru():
                for w, name in enumerate(("lru_w_a", "lru_w_i")):
                    for d in range(2):
                        sp_.dma_start(lru_w[:, 2 * w + d, :, :],
                                      ins[name][0, d].rearrange("n d e -> d n e")).then_inc(lru_in, 16)

            for n in ada_first:
                load_tile(("ada", n))
            load_lru()
            sp_.wait_ge(ada_ready, 2 * per_c)
            sp_.dma_start(ada_scratch[:, 0:2 * D], ada_sb[:, 0:2 * D]).then_inc(ada_saved, 16)
            sp_.wait_ge(ada_saved, 16)
            for ci in range(2):
                sp_.dma_start(mod_rows[2 * KD * ci:2 * KD * (ci + 1), :],
                              ada_scratch[ci, 0:2 * D].rearrange("(r x) -> r x", x=P)).then_inc(mod_in, 16)
            load_tile((0, "xr", 0))
            sp_.wait_ge(ada_ready, len(ada_first))
            sp_.dma_start(ada_scratch[:, 4 * D:5 * D], ada_sb[:, 4 * D:5 * D]).then_inc(ada_saved, 16)
            sp_.wait_ge(ada_saved, 32)

            for ph in PHASES:
                lo = tiles.index((0, "xr", 0)) + 1 if ph == 0 else tiles.index((1, "xr", 0))
                hi = tiles.index((1, "xr", 0)) if ph == 0 else len(tiles)
                for key in tiles[lo:hi]:
                    if key == (1, "xr", 4):
                        sp_.wait_ge(route_ready, CH0[ph])
                        load_lru()
                        sp_.wait_ge(ada_ready, NADA)
                        sp_.dma_start(ada_scratch[:, 5 * D:6 * D], h2_all[0:2, C1, :]).then_inc(ada_saved, 16)
                        sp_.wait_ge(ada_saved, 64)
                        sp_.dma_start(gf_row[:, 0, :], ada_scratch[0, 5 * D:6 * D].partition_broadcast(P)).then_inc(final_in, 16)
                    if key == (0, "ro", 2):
                        sp_.wait_ge(ada_ready, len(ada_first) + len(ada_lru))
                        sp_.dma_start(ada_scratch[:, 2 * D:4 * D].rearrange("p (c n) -> p c n", c=2), ada_late[2])\
                            .then_inc(ada_saved, 16)
                    if key == (ph, "out", 0):
                        sp_.wait_ge(attn_ready, NKV * sum(NT[:ph + 1]))
                        if ph == 0:
                            sp_.wait_ge(ada_saved, 48)
                        for row, c in ((gate_row, 2), (scale_row, 4), (shift_row, 3)):
                            sp_.dma_start(row, ada_scratch[ph, c * D:(c + 1) * D].partition_broadcast(P)).then_inc(rows_in, 16)
                        sp_.dma_start(ffn_row, ins["norm_ffn_g"][0].partition_broadcast(P)).then_inc(rows_in, 16)
                    load_tile(key)
                    if key == (0, "ga", 0):
                        sp_.wait_ge(v_ready, 2)
                        sp_.dma_start(new_k[0, 0].rearrange("s h d -> s (h d)"), ktok[:, :]).then_inc(saved, 16)
                        sp_.dma_start(new_v[0, 0].rearrange("s h d -> s (h d)"), v_sb[:, 0, :]).then_inc(saved, 16)
                        sp_.wait_ge(saved, 32)
            sp_.wait_ge(sums0_done, 1)
            sp_.dma_start(gf_row[:, 1, :], ada_scratch[1, 5 * D:6 * D].partition_broadcast(P)).then_inc(final_in, 16)
            sp_.dma_start(final_row[:, :], ins["final_g"].partition_broadcast(P)).then_inc(final_in, 16)
            sp_.wait_ge(state_turned, 1)
            sp_.dma_start(new_hf[0, 0].rearrange("(r x) -> r x", x=P), state_out[0:LB, :]).then_inc(saved, 16)
            sp_.dma_start(new_hb[0, 0].rearrange("(r x) -> r x", x=P), state_out[LB:2 * LB, :]).then_inc(saved, 16)
            for c in range(NCH):
                dst = y_prompt[0, c * P:(c + 1) * P, :] if c < NT[0] else y_sample[0, (c - NT[0]) * P:(c - NT[0] + 1) * P, :]
                sp_.wait_ge(y_ready, c + 1)
                sp_.dma_start(dst, x_all[:, c, :]).then_inc(saved, 16)
            sp_.wait_ge(saved, 16 * (4 + NCH))

        @block.tensor
        def _(pe):
            todo = list(order)
            stage = [0]

            def open_unit(key):
                assert todo.pop(0) == key, key
                if use[key] > 1:
                    pe.wait_ge(bank_free[bank[key]], use[key] - 1)
                return ps(key)

            def close_unit(key, last):
                last.then_inc(bank_full[bank[key]], 1)

            def arrived(key):
                pe.wait_ge(tile_full[slot[key]], 16 * fill[key])
                return w_tile[slot[key]]

            def stage_left():
                stage[0] += 1
                pe.drain().then_inc(pe_stage, 1)

            def others_left():
                pe.wait_ge(act_stage, stage[0])
                pe.wait_ge(dve_stage, stage[0])

            def end_stage():
                stage_left()
                others_left()

            pe.wait_ge(vrows_in, 160)
            pe.wait_ge(consts_in, 16 * 6)
            u = open_unit(("vcols",))
            close_unit(("vcols",), nc.tensor.transpose(u[:, 0:P], vrows[:, :], ident[:, :]))
            arrived(("keys",))
            for i in range(HP // 4):
                u = open_unit(("keys", i))
                for k in range(4):
                    last = nc.tensor.transpose(u[:, k * P:(k + 1) * P], keys_tile[:, 4 * i + k, :], ident[:, :])
                close_unit(("keys", i), last)
            pe.wait_ge(kctx_in, 32)
            u = open_unit(("kctx",))
            for kv in range(NKV):
                last = nc.tensor.transpose(u[:, kv * P:(kv + 1) * P], ktok[:, kv * P:(kv + 1) * P], ident[:, :])
            close_unit(("kctx",), last)
            pe.wait_ge(silu_ready, 1)
            cond = siluT[:, :].rearrange("p (c k) -> p k c", c=2)

            def adaln(n):
                w = arrived(("ada", n))
                u = open_unit(("ada", n))
                for k in range(KD):
                    last = nc.tensor.matmul(u[0:2, 0:TC], cond[:, k, :], w[:, k, :], start=(k == 0), stop=(k == KD - 1))
                close_unit(("ada", n), last)
            for n in ada_first:
                adaln(n)
            pe.wait_ge(mod_in, 32)
            u = open_unit(("mod",))
            close_unit(("mod",), nc.tensor.transpose(u[:, 0:4 * KD], mod_rows[:, :], ident[0:4 * KD, 0:4 * KD]))
            end_stage()

            for ph in PHASES:
                N = TOK[ph]

                def feature_unit(key, w, col, src, n=N):
                    u = open_unit(key)
                    for k in range(KD):
                        last = nc.tensor.matmul(u[:, 0:n], w[:, k, col:col + P], src[:, k, 0:n],
                                                start=(k == 0), stop=(k == KD - 1))
                    close_unit(key, last)

                def norm1(ph):
                    for t in range(NT[ph]):
                        pe.wait_ge(xn_ready, var1(ph, t) + 1)
                        for i in range(2):
                            u = open_unit((ph, "xt", t, i))
                            for k in range(4):
                                last = nc.tensor.transpose(u[:, k * P:(k + 1) * P],
                                                           xn[t % 2][:, (4 * i + k) * P:(4 * i + k + 1) * P], ident[:, :])
                            close_unit((ph, "xt", t, i), last)
                if ph == 0:
                    norm1(0)
                    end_stage()

                def gates(j):
                    if j == 0:
                        pe.wait_ge(lru_in, 64 * (ph + 1))
                    pe.wait_ge(xc_ready, LB * ph + j + 1)
                    for g in range(4):
                        d, w = g // 2, g % 2
                        u = open_unit((ph, "gate", j, g))
                        close_unit((ph, "gate", j, g), nc.tensor.matmul(
                            u[:, 0:N], lru_w[:, 2 * w + d, j, :], xc[j % 2][:, 0:N], start=True, stop=True))
                for j in range(LB):
                    wr, wg = arrived((ph, "xr", j - j % 2)), arrived((ph, "xg", j - j % 2))
                    feature_unit((ph, "xr", j), wr, (j % 2) * P, hT)
                    feature_unit((ph, "xg", j), wg, (j % 2) * P, hT)
                    if ph and j >= LB - NKV:
                        i = j - LB + NKV
                        feature_unit((ph, "k", i), arrived((ph, "k")), i * P, hT)
                        wv_ = arrived((ph, "v"))
                        u = open_unit((ph, "v", i))
                        for t in range(2):
                            for k in range(KD):
                                last = nc.tensor.matmul(u[:, t * KVW:(t + 1) * KVW],
                                                        hT[:, k, (2 * i + t) * P:(2 * i + t + 1) * P], wv_[:, k, :],
                                                        start=(k == 0), stop=(k == KD - 1))
                        close_unit((ph, "v", i), last)
                    if ph == 0:
                        adaln(ada_lru[j])
                    if j:
                        gates(j - 1)
                gates(LB - 1)
                stage_left()

                def merge_gate(a, m):
                    feature_unit((ph, a, m), arrived((ph, a, m - m % 2)), (m % 2) * P, hT)

                def outputs(a, o):
                    for m in range(KD):
                        feature_unit((ph, o, m), arrived((ph, o, m - m % 2)), (m % 2) * P, featT)
                        if m + AHEAD < KD:
                            merge_gate(a, m + AHEAD)
                for m in range(AHEAD):
                    merge_gate("gr", m)
                others_left()
                outputs("gr", "ro")

                if ph == 0:
                    wk_, wv_ = arrived((ph, "k")), arrived((ph, "v"))
                    u = open_unit((ph, "kv"))
                    for w, o in ((wk_, 0), (wv_, KVW)):
                        for k in range(KD):
                            last = nc.tensor.matmul(u[:, o:o + KVW], hT[:, k, 0:P], w[:, k, :],
                                                    start=(k == 0), stop=(k == KD - 1))
                    close_unit((ph, "kv"), last)
                    pe.wait_ge(v_ready, 2)
                    u = open_unit((ph, "kt"))
                    for kv in range(NKV):
                        last = nc.tensor.transpose(u[:, kv * P:(kv + 1) * P], ktok[:, kv * P:(kv + 1) * P], ident[:, :])
                    close_unit((ph, "kt"), last)
                for h in range(0, NH, 2):
                    w = arrived((ph, "q", h))
                    feature_unit((ph, "q", h), w, 0, hT)
                    feature_unit((ph, "q", h + 1), w, P, hT)
                end_stage()

                def window(n):
                    return (0, 0) if ph == 0 else (max(n - 1, 0), min(n + 1, NT[ph] - 1))

                def score_units(q):
                    n, kv = q
                    lo, hi = window(n)
                    win = (hi - lo + 1) * P
                    for h in range(G):
                        key = (ph, "s", q, h)
                        u = open_unit(key)
                        qh = featT[:, kv * G + h, n * P:(n + 1) * P]
                        last = nc.tensor.matmul(u[:, 0:win], qh, kT[:, kv, lo * P:lo * P + win], start=True, stop=True)
                        if ph:
                            last = nc.tensor.matmul(u[:, win:win + P], qh, kT[:, kv, CTX:CTX + P], start=True, stop=True)
                        close_unit(key, last)

                def turn_values(i):
                    q = qs[i]
                    Q = NKV * CH0[ph] + i
                    pe.wait_ge(o_ready, Q + 1)
                    u = open_unit((ph, "ot", q))
                    for h in range(G):
                        last = nc.tensor.transpose(u[:, h * P:(h + 1) * P], o_sb[Q % 2][:, h * P:(h + 1) * P], ident[:, :])
                    close_unit((ph, "ot", q), last)

                qs = quads(ph)
                score_units(qs[0])
                for i, q in enumerate(qs):
                    n, kv = q
                    Q = NKV * CH0[ph] + i
                    lo, hi = window(n)
                    blocks = list(range(lo, hi + 1)) + ([NT[1]] if ph else [])
                    if i + 1 < len(qs):
                        score_units(qs[i + 1])
                    o = open_unit((ph, "o", q))
                    if i == len(qs) - 1:
                        merge_gate("ga", 0)

                    def values(h):
                        pe.wait_ge(pT_ready[h % 2], G // 2 * Q + h // 2 + 1)
                        for i_, b in enumerate(blocks):
                            last = nc.tensor.matmul(o[:, h * P:(h + 1) * P], pT[h % 2][:, i_ * P:(i_ + 1) * P],
                                                    v_sb[:, b, kv * P:(kv + 1) * P],
                                                    start=(i_ == 0), stop=(i_ == len(blocks) - 1))
                        if h == G - 1:
                            close_unit((ph, "o", q), last)
                        else:
                            last.then_inc(o_part, 1)
                    for h in range(G):
                        pe.wait_ge(prob_ready, G * Q + h + 1)
                        key = (ph, "pt", q, h)
                        u = open_unit(key)
                        for i_ in range(len(blocks)):
                            last = nc.tensor.transpose(u[:, i_ * P:(i_ + 1) * P],
                                                       sm_pair[Q % 2][:, h, i_ * P:(i_ + 1) * P], ident[:, :])
                        close_unit(key, last)
                        if h:
                            values(h - 1)
                    values(G - 1)
                    if i:
                        turn_values(i - 1)
                merge_gate("ga", 1)
                turn_values(len(qs) - 1)
                stage_left()
                for m in range(2, AHEAD):
                    merge_gate("ga", m)
                pe.wait_ge(attn_ready, NKV * sum(NT[:ph + 1]))
                others_left()

                outputs("ga", "ao")
                pe.wait_ge(mix_ready, KD * 2 * (ph + 1))
                def turn_h2(t):
                    pe.wait_ge(xn_ready, var2(ph, t) + 1)
                    for i in range(2):
                        u = open_unit((ph, "h2", t, i))
                        for k in range(4):
                            f = (4 * i + k) * P
                            last = nc.tensor.transpose(u[:, k * P:(k + 1) * P], h2_all[:, CH0[ph] + t, f:f + P], ident[:, :])
                        close_unit((ph, "h2", t, i), last)
                for t in range(NT[ph]):
                    for n in range(D // TC):
                        w = arrived((ph, "out", n))
                        key = (ph, "mix", n, t)
                        u = open_unit(key)
                        for k in range(KD):
                            last = nc.tensor.matmul(u[:, 0:TC], mixT[:, k, t * P:(t + 1) * P], w[:, k, :],
                                                    start=(k == 0), stop=(k == KD - 1))
                        close_unit(key, last)
                    if t:
                        turn_h2(t - 1)
                turn_h2(NT[ph] - 1)
                if ph == 0:
                    norm1(1)
                end_stage()

                def scores(hp):
                    pe.wait_ge(pq_ready, HP * ph + hp + 1)
                    u = open_unit((ph, "sc", hp))
                    for t in range(NT[ph]):
                        last = nc.tensor.matmul(u[:, t * P:(t + 1) * P], pq_sb[hp % 2][:, t * P:(t + 1) * P],
                                                keysT[:, hp, :], start=True, stop=True)
                    close_unit((ph, "sc", hp), last)
                for hp in range(HP):
                    w = arrived((ph, "pq", hp - hp % 2))
                    feature_unit((ph, "pq", hp), w, (hp % 2) * P, featT)
                    if hp:
                        scores(hp - 1)
                        if ph == 0 and hp in ada_after:
                            adaln(ada_after[hp])
                scores(HP - 1)
                if ph == 0:
                    pe.wait_ge(state_ready, 2 * LB)
                    u = open_unit(("state",))
                    close_unit(("state",), nc.tensor.transpose(u[0:2 * LB, 0:P], state[:, :], ident[:, :]))
                end_stage()

        @block.scalar
        def _(act):
            chain = Chain(act, act_chain)
            stage = [0]

            def full(key):
                act.wait_ge(bank_full[bank[key]], use[key])
                return ps(key)

            def end_stage():
                stage[0] += 1
                act.drain().then_inc(act_stage, 1)
                act.wait_ge(pe_stage, stage[0])
                act.wait_ge(dve_stage, stage[0])

            def run(out, in_, func, **kw):
                return nc.scalar.activation(out, in_, func, **kw)

            u = full(("vcols",))
            chain.link(run(vcols[:, :], u[:, 0:P], ACT.Identity))
            act.drain().then_inc(vcols_ready, 1)
            run(silu_t[:, :], vcols[:, 0:2 * KD], ACT.Tanh, scale=0.5).then_inc(silu_half, 1)
            act.wait_ge(lam_abs, 1)
            run(sp[:, 1, :], sp[:, 0, :], ACT.Exp, scale=-1.0).then_inc(lam_exp, 1)
            u = full(("kctx",))
            chain.mark(run(kT[:, :, CTX:CTX + P], u[:, 0:KVW].rearrange("p (h s) -> p h s", h=NKV), ACT.Identity))
            chain.wait()
            act.drain().then_inc(bank_free[bank[("kctx",)]], 1)
            act.drain().then_inc(bank_free[bank[("vcols",)]], 1)
            end_stage()

            def soft(c):
                act.wait_ge(bestdiff, c + 1)
                run(best[:, 1, :], best[:, 1, :], ACT.Exp).then_inc(soft_ready, 1)

            def gelu_dots(c):
                act.wait_ge(dots_ready, c + 1)
                run(gel[:, :], dots[:, :], ACT.Square).then_inc(gsq_ready, 1)
                act.wait_ge(gcub_ready, c + 1)
                run(gel[:, :], gel[:, :], ACT.Tanh, scale=GELU_C * GELU_S).then_inc(gt_ready, 1)

            def final(c):
                act.wait_ge(fvar_ready, c + 1)
                run(nrm[:, 2 * NCH + c, 2:3], nrm[:, 2 * NCH + c, 1:2], ACT.Sqrt).then_inc(fstd_ready, 1)

            for ph in PHASES:
                N = TOK[ph]
                def norm1(ph):
                    for t in range(NT[ph]):
                        v = var1(ph, t)
                        act.wait_ge(var_ready, v + 1)
                        run(nrm[:, v, 2:3], nrm[:, v, 1:2], ACT.Sqrt).then_inc(std_ready, 1)
                    for t in range(NT[ph]):
                        for i in range(2):
                            u = full((ph, "xt", t, i))
                            for k in range(4):
                                f = 4 * i + k
                                last = run(hT[:, f, t * P:(t + 1) * P], u[:, k * P:(k + 1) * P], ACT.Identity,
                                           scale=mod_a[:, ph, f:f + 1], bias=mod_b[:, ph, f:f + 1])
                            last.then_inc(bank_free[bank[(ph, "xt", t, i)]], 1)
                if ph == 0:
                    norm1(0)
                    end_stage()

                def gelu_in(j):
                    u = full((ph, "xg", j))
                    run(featT[:, j, 0:N], u[:, 0:N], ACT.Square).then_inc(sq_ready, 1)
                    act.wait_ge(cub_ready, LB * ph + j + 1)
                    run(featT[:, j, 0:N], featT[:, j, 0:N], ACT.Tanh, scale=GELU_C * GELU_S).then_inc(gtanh_ready, 1)
                gelu_in(0)
                for j in range(LB):
                    B = LB * ph + j
                    if j + 1 < LB:
                        gelu_in(j + 1)
                    i = j + 1 - (LB - NKV)
                    if ph and 0 <= i < NKV:
                        u = full((ph, "v", i))
                        run(v_sb[:, 2 * i:2 * i + 2, :], u[:, :].rearrange("p (t n) -> p t n", t=2), ACT.Identity)\
                            .then_inc(bank_free[bank[(ph, "v", i)]], 1)
                    if j:
                        act.wait_ge(lru_done, B)
                    for d in range(2):
                        u = full((ph, "gate", j, 2 * d))
                        run(lt[d][:, 0:N], u[:, 0:N], ACT.Tanh, scale=0.5,
                            bias=half_b[:, d * LB + j:d * LB + j + 1]).then_inc(bank_free[bank[(ph, "gate", j, 2 * d)]], 1)
                        u = full((ph, "gate", j, 2 * d + 1))
                        run(lti[d][:, 0:N], u[:, 0:N], ACT.Tanh, scale=0.5,
                            bias=half_b[:, (2 + d) * LB + j:(2 + d) * LB + j + 1])\
                            .then_inc(bank_free[bank[(ph, "gate", j, 2 * d + 1)]], 1)
                    for d in range(2):
                        i = d * LB + j
                        act.wait_ge(bank_free[bank[(ph, "gate", j, 2 * d + 1)]], use[(ph, "gate", j, 2 * d + 1)])
                        chain.mark(run(lth[d][:, 0:N], lt[d][:, 0:N], ACT.Tanh, scale=sp[:, 7, i:i + 1], bias=sp[:, 7, i:i + 1]))
                        chain.mark(run(la[d][:, 0:N], lt[d][:, 0:N], ACT.Exp, scale=sp[:, 5, i:i + 1], bias=sp[:, 5, i:i + 1]))
                        run(le[d][:, 0:N], lt[d][:, 0:N], ACT.Exp, scale=sp[:, 6, i:i + 1], bias=sp[:, 6, i:i + 1])\
                            .then_inc(e2_ready, 1)
                    for d in range(2):
                        act.wait_ge(w_ready, 2 * B + d + 1)
                        run(le[d][:, 0:N], le[d][:, 0:N], ACT.Sqrt, scale=0.25).then_inc(root_ready, 1)
                end_stage()

                def merge(a, j0):
                    for m in range(KD):
                        i = 2 * KD * ph + j0 + m
                        if m >= 2:
                            act.wait_ge(mix_ready, i - 1)
                        u = full((ph, a, m))
                        chain.link(run(wk(2 + m % 2)[:, 0:N], u[:, 0:N], ACT.Tanh, scale=0.5))
                        act.drain().then_inc(bank_free[bank[(ph, a, m)]], 1)
                        act.drain().then_inc(rg_ready, 1)
                merge("gr", 0)

                if ph == 0:
                    u = full((ph, "kt"))
                    chain.link(run(kT[:, :, 0:P], u[:, 0:KVW].rearrange("p (h s) -> p h s", h=NKV), ACT.Identity))
                    act.drain().then_inc(bank_free[bank[(ph, "kt")]], 1)
                    for h in range(NH):
                        u = full((ph, "q", h))
                        run(featT[:, h, 0:N], u[:, 0:N], ACT.Identity).then_inc(bank_free[bank[(ph, "q", h)]], 1)
                end_stage()
                if ph:
                    gelu_dots(0)
                qs = quads(ph)

                def width(n):
                    return P if ph == 0 else (min(n + 1, NT[ph] - 1) - max(n - 1, 0) + 2) * P

                def exps(i):
                    Q = NKV * CH0[ph] + i
                    W = width(qs[i][0])
                    act.wait_ge(neg_ready, Q + 1)
                    run(q_es[:, Q, :], q_dif[:, Q, :], ACT.Exp).then_inc(act_chain, 1)
                    chain.n += 1
                    for h in range(G):
                        p_ = sm_pair[Q % 2][:, h, 0:W]
                        run(p_, p_, ACT.Exp, bias=q_neg[:, Q, h:h + 1], accum_out=q_sum[:, Q, h:h + 1])\
                            .then_inc(prob_ready, 1)
                exps(0)
                for i, q in enumerate(qs):
                    n, kv = q
                    Q = NKV * CH0[ph] + i
                    W = width(n)
                    for h in range(G):
                        u = full((ph, "pt", q, h))
                        values_done(act, Q, h)
                        run(pT[h % 2][:, 0:W], u[:, 0:W], ACT.Identity).then_inc(pT_ready[h % 2], 1)
                        act.wait_ge(pT_ready[h % 2], G // 2 * Q + h // 2 + 1)
                        act.drain().then_inc(bank_free[bank[(ph, "pt", q, h)]], 1)
                    if i + 1 < len(qs):
                        exps(i + 1)
                    for j in ([i - 1] if i else []) + ([i] if i == len(qs) - 1 else []):
                        q = qs[j]
                        u = full((ph, "ot", q))
                        run(featT[:, q[1] * G:(q[1] + 1) * G, q[0] * P:(q[0] + 1) * P],
                            u[:, :].rearrange("p (h s) -> p h s", h=G), ACT.Identity).then_inc(attn_ready, 1)
                        act.drain().then_inc(bank_free[bank[(ph, "ot", q)]], 1)
                end_stage()
                merge("ga", KD)
                for t in range(NT[ph] + 1):
                    if t < NT[ph]:
                        v = var2(ph, t)
                        act.wait_ge(var_ready, v + 1)
                        run(nrm[:, v, 2:3], nrm[:, v, 1:2], ACT.Sqrt).then_inc(std_ready, 1)
                    for i in range(2 if t else 0):
                        u = full((ph, "h2", t - 1, i))
                        run(featT[:, 4 * i:4 * i + 4, (t - 1) * P:t * P], u[:, :].rearrange("p (k s) -> p k s", k=4),
                            ACT.Identity).then_inc(bank_free[bank[(ph, "h2", t - 1, i)]], 1)
                if ph == 0:
                    norm1(1)
                end_stage()
                for hp in range(HP):
                    u = full((ph, "pq", hp))
                    if hp >= 2:
                        s = (ph, "sc", hp - 2)
                        act.wait_ge(bank_full[bank[s]], use[s])
                    chain.link(run(pq_sb[hp % 2][:, 0:N], u[:, 0:N], ACT.Identity))
                    act.drain().then_inc(bank_free[bank[(ph, "pq", hp)]], 1)
                    act.drain().then_inc(pq_ready, 1)
                end_stage()
                if ph == 0:
                    soft(0)
            soft(C1)
            for step in steps:
                if step[0][0] == "u" and step[0][1] + 1 < NCH:
                    soft(step[0][1] + 1)
                for table, c in step:
                    if table == "u":
                        gelu_dots(c)
                if step is steps[0]:
                    final(0)
                for table, c in step:
                    if table == "v":
                        final(c)

        @block.vector
        def _(dve):
            V = nc.vector
            chain = Chain(dve, dve_chain)
            link, mark = chain.link, chain.mark
            stage = [0]

            def full(key):
                dve.wait_ge(bank_full[bank[key]], use[key])
                return ps(key)

            def free(key):
                dve.drain().then_inc(bank_free[bank[key]], 1)

            def end_stage():
                stage[0] += 1
                dve.drain().then_inc(dve_stage, 1)
                dve.wait_ge(pe_stage, stage[0])
                dve.wait_ge(act_stage, stage[0])

            def variance(v, src, scratch):
                link(V.tensor_tensor_reduce(scratch, src, src, 1.0, 0.0, ALU.mult, ALU.add, nrm[:, v, 0:1]))
                link(V.tensor_scalar(nrm[:, v, 1:2], nrm[:, v, 0:1], 1.0 / D, EPS, ALU.mult, ALU.add))

            def inverse_root(v):
                n = nrm[:, v, :]
                link(V.reciprocal(n[:, 3:4], n[:, 2:3]))
                link(V.tensor_tensor(n[:, 4:5], n[:, 3:4], n[:, 3:4], ALU.mult))
                link(V.tensor_tensor(n[:, 5:6], n[:, 4:5], n[:, 1:2], ALU.mult))
                link(V.tensor_scalar(n[:, 6:7], n[:, 5:6], -0.5, 1.5, ALU.mult, ALU.add))
                link(V.tensor_tensor(n[:, 7:8], n[:, 6:7], n[:, 3:4], ALU.mult))
                return n[:, 7:8]

            dve.wait_ge(vcols_ready, 1)
            lam = vcols[:, V_LAM:V_LAM + 2 * LB]
            link(V.tensor_scalar(sp[:, 2, :], lam, -1.0, None, ALU.mult))
            link(V.tensor_tensor(sp[:, 0, :], lam, sp[:, 2, :], ALU.max))
            dve.drain().then_inc(lam_abs, 1)
            link(V.tensor_scalar(sp[:, 2, :], sp[:, 2, :], 0.0, None, ALU.max))
            link(V.tensor_scalar(half_b[:, :], vcols[:, V_BA:V_BA + 4 * LB], 0.5, None, ALU.mult))
            dve.wait_ge(silu_half, 1)
            link(V.tensor_scalar(silu_t[:, :], silu_t[:, :], 0.5, 0.5, ALU.mult, ALU.add))
            V.tensor_tensor(siluT[:, :], silu_t[:, :], vcols[:, 0:2 * KD], ALU.mult).then_inc(silu_ready, 1)
            dve.wait_ge(lam_exp, 1)
            link(V.tensor_scalar(sp[:, 3, :], sp[:, 1, :], 2.0, None, ALU.add))
            link(V.reciprocal(sp[:, 4, :], sp[:, 3, :]))
            link(V.tensor_tensor(sp[:, 3, :], sp[:, 1, :], sp[:, 4, :], ALU.mult))
            link(V.tensor_tensor(sp[:, 4, :], sp[:, 3, :], sp[:, 3, :], ALU.mult))
            link(V.tensor_scalar(sp[:, 5, :], sp[:, 4, :], 1.0 / 15, 1.0 / 13, ALU.mult, ALU.add))
            for d in (11, 9, 7, 5, 3, 1):
                link(V.tensor_tensor(sp[:, 6, :], sp[:, 5, :], sp[:, 4, :], ALU.mult))
                link(V.tensor_scalar(sp[:, 5, :], sp[:, 6, :], 1.0 / d, None, ALU.add))
            link(V.tensor_tensor(sp[:, 6, :], sp[:, 5, :], sp[:, 3, :], ALU.mult))
            link(V.scalar_tensor_tensor(sp[:, 1, :], sp[:, 6, :], 2.0, sp[:, 2, :], ALU.mult, ALU.add))
            link(V.tensor_scalar(sp[:, 5, :], sp[:, 1, :], -4.0, None, ALU.mult))
            link(V.tensor_scalar(sp[:, 6, :], sp[:, 1, :], -8.0, None, ALU.mult))
            link(V.tensor_scalar(sp[:, 7, :], sp[:, 1, :], 4.0, None, ALU.mult))
            for i in range(HP // 4):
                u = full(("keys", i))
                mark(V.tensor_copy(keysT[:, 4 * i:4 * i + 4, :], u[:, :].rearrange("p (i n) -> p i n", i=4)))
                free(("keys", i))
            dve.wait_ge(bada_in, 48)

            def add_bias(n):
                u = full(("ada", n))
                c = n * TC
                if n in ada_first:
                    out, bias = ada_sb[:, c:c + TC], b_ada[:, c:c + TC]
                else:
                    at, c = (C1, n - 5 * per_c) if n in ada_topk else (C1 + 1 + (n // per_c - 2), n % per_c)
                    out = bias = h2_all[0:2, at, c * TC:(c + 1) * TC]
                V.tensor_tensor(out, u[0:2, 0:TC], bias, ALU.add).then_inc(ada_ready, 1)
                free(("ada", n))
            for n in ada_first:
                add_bias(n)
            u = full(("mod",))
            cols = u[:, 0:4 * KD].rearrange("p (c w k) -> p c w k", c=2, w=2)
            mark(V.tensor_copy(mod_b[:, :, :], cols[:, :, 0, :]))
            link(V.tensor_scalar(mod_a[:, :, :], cols[:, :, 1, :], 1.0, None, ALU.add))
            free(("mod",))
            for ci in range(2):
                link(V.tensor_tensor(mod_a[:, ci, :], mod_a[:, ci, :], vcols[:, V_G:V_G + KD], ALU.mult))
            end_stage()

            served = [None]
            gelu0 = [False]

            def serve(n):
                for _ in range(n):
                    s_ = served[0]
                    if s_ is None or s_ == 2 * SLOTS or (s_ == SLOTS and not gelu0[0]):
                        return
                    r = s_ % RING0
                    dve.wait_ge(row0_in[r], 16 * (s_ // RING0 + 1))
                    if s_ < SLOTS:
                        V.tensor_tensor_reduce(ring0[r], ring0[r], h2_all[:, 0, :], 1.0, 0.0, ALU.mult, ALU.add,
                                               dots[:, s_:s_ + 1]).then_inc(slot0_used, 1)
                    else:
                        a_, w_ = acc0[s_ % 2], gw[:, 0, s_ - SLOTS:s_ - SLOTS + 1]
                        if s_ < SLOTS + 2:
                            V.tensor_scalar(a_, ring0[r], w_, None, ALU.mult).then_inc(slot0_used, 1)
                        else:
                            dve.wait_ge(slot0_used, RING0 + s_ - 1)
                            V.scalar_tensor_tensor(a_, ring0[r], w_, a_, ALU.mult, ALU.add).then_inc(slot0_used, 1)
                    served[0] += 1

            def gelu_dots(c):
                if c == 0:
                    serve(SLOTS)
                    dve.wait_ge(slot0_used, RING0 + SLOTS)
                    gelu0[0] = True
                dve.drain().then_inc(dots_ready, 1)
                dve.wait_ge(gsq_ready, c + 1)
                V.scalar_tensor_tensor(gel[:, :], gel[:, :], 1.0 / GELU_C, dots[:, :], ALU.add, ALU.mult)\
                    .then_inc(gcub_ready, 1)
                dve.wait_ge(gt_ready, c + 1)
                link(V.scalar_tensor_tensor(gel[:, :], gel[:, :], 1.0, dots[:, :], ALU.add, ALU.mult))
                link(V.scalar_tensor_tensor(gw[:, c, :], gw[:, c, :], 0.5, gel[:, :], ALU.mult, ALU.mult))

            def add_sums(c, acc_):
                x = x_all[:, c, :]
                link(V.tensor_tensor(acc_[0], acc_[0], acc_[1], ALU.add))
                link(V.tensor_tensor(acc_[0], acc_[0], gf_row[:, 0 if c < NT[0] else 1, :], ALU.mult))
                link(V.tensor_tensor(x, x, acc_[0], ALU.add))

            def final(c, scratch):
                x, v = x_all[:, c, :], 2 * NCH + c
                variance(v, x, scratch)
                dve.drain().then_inc(fvar_ready, 1)
                dve.wait_ge(fstd_ready, c + 1)
                r = inverse_root(v)
                V.scalar_tensor_tensor(x, x, r, final_row[:, :], ALU.mult, ALU.mult).then_inc(y_ready, 1)
                dve.wait_ge(y_ready, c + 1)

            def best_sums(c, h):
                s = cand[:, h * TOPK * TOPK:(h + 1) * TOPK * TOPK]
                tv = top_v[:, max(c - C1, 0), 2 * h:2 * h + 2, :]
                shape = [P, TOPK, TOPK]
                link(V.tensor_tensor(s.rearrange("p (i j) -> p i j", i=TOPK), tv[:, 0, :].unsqueeze(2).to_broadcast(shape),
                                     tv[:, 1, :].unsqueeze(1).to_broadcast(shape), ALU.add))
                v0, v1 = (best[:, 0, h * TOPK + 8 * i:h * TOPK + 8 * (i + 1)] for i in range(2))
                p0, p1 = (pos[:, 0, h * TOPK + 8 * i:h * TOPK + 8 * (i + 1)] for i in range(2))
                link(V.max(v0, s))
                link(V.max_index(p0, v0, s))
                link(V.match_replace(s, v0, s, NEG_BIG))
                link(V.max(v1, s))
                link(V.max_index(p1, v1, s))

            def best_diffs(c):
                bv = best[:, 0, :].rearrange("p (h k) -> p h k", h=PH)
                link(V.tensor_tensor(best[:, 1, :].rearrange("p (h k) -> p h k", h=PH), bv,
                                     bv[:, :, 0:1].to_broadcast([P, PH, TOPK]), ALU.subtract))
                dve.drain().then_inc(bestdiff, 1)

            def experts(c, h0, h1):
                nh = h1 - h0
                S = slice(h0 * TOPK, h1 * TOPK)
                shape = [P, nh, TOPK, TOPK]
                link(V.tensor_scalar(pos[:, 1, S], pos[:, 0, S], 4, None, ALU.logical_shift_right))
                link(V.tensor_scalar(pos[:, 2, S], pos[:, 0, S], TOPK - 1, None, ALU.bitwise_and))
                link(V.tensor_copy(sel[:, 0:2, S], pos[:, 1:3, S]))
                link(V.tensor_copy(it_f[:, 2 * h0:2 * h1, :], top_i[:, max(c - C1, 0), 2 * h0:2 * h1, :]))
                itf = it_f[:, 2 * h0:2 * h1, :].rearrange("p (h s) k -> p h s k", s=2)
                onehot = hot[:, 0:nh * TOPK * TOPK].rearrange("p (h k i) -> p h k i", h=nh, k=TOPK)
                for s in range(2):
                    at = sel[:, s, S].rearrange("p (h k) -> p h k", h=nh)
                    link(V.tensor_tensor(onehot, at.unsqueeze(3).to_broadcast(shape),
                                         iota16[:, :].unsqueeze(1).unsqueeze(1).to_broadcast(shape), ALU.is_equal))
                    link(V.tensor_tensor(onehot, onehot, itf[:, :, s, :].unsqueeze(2).to_broadcast(shape), ALU.mult))
                    link(V.tensor_reduce(sel[:, 2 + s, S].rearrange("p (h k) -> p h k", h=nh), onehot, AX_X, ALU.add))

            def routed(c):
                link(V.scalar_tensor_tensor(sel[:, 0, :], sel[:, 2, :], float(NKEY), sel[:, 3, :], ALU.mult, ALU.add))
                link(V.tensor_copy(eidx[:, c, :], sel[:, 0, :]))
                dve.wait_ge(soft_ready, c + 1)
                e = best[:, 1, :].rearrange("p (h k) -> p h k", h=PH)
                link(V.tensor_reduce(sred[:, 0, :], e, AX_X, ALU.add))
                link(V.reciprocal(sred[:, 1, :], sred[:, 0, :]))
                link(V.tensor_tensor(gw[:, c, :].rearrange("p (h k) -> p h k", h=PH), e,
                                     sred[:, 1, :].unsqueeze(2).to_broadcast([P, PH, TOPK]), ALU.mult))
                dve.drain().then_inc(route_ready, 1)

            def route(c, part):
                if part < 2:
                    for h in range(part * PH // 2, (part + 1) * PH // 2):
                        best_sums(c, h)
                if part == 2:
                    best_diffs(c)
                if part >= 2:
                    experts(c, (part - 2) * PH // 2, (part - 1) * PH // 2)
                if part == 3:
                    routed(c)

            dve.wait_ge(x_in, 32)
            for ph in PHASES:
                N = TOK[ph]
                def norm1(ph):
                    for t in range(NT[ph]):
                        v = var1(ph, t)
                        if t >= 2:
                            u = (ph, "xt", t - 2, 1)
                            dve.wait_ge(bank_full[bank[u]], use[u])
                        x = x_all[:, CH0[ph] + t, :]
                        variance(v, x, xn[t % 2])
                        dve.drain().then_inc(var_ready, 1)
                        dve.wait_ge(std_ready, v + 1)
                        r = inverse_root(v)
                        V.tensor_scalar(xn[t % 2], x, r, None, ALU.mult).then_inc(xn_ready, 1)
                if ph == 0:
                    norm1(0)
                    end_stage()

                def rope(key, dst, rope_tmp_=rope_tmp):
                    u = full(key)
                    mark(V.tensor_tensor(dst, u[:, 0:N], cos_sb[:, 0:N], ALU.mult))
                    mark(V.tensor_tensor(rope_tmp_[0:64, 0:N], u[64:128, 0:N], sin_sb[64:128, 0:N], ALU.mult))
                    link(V.tensor_tensor(rope_tmp_[64:128, 0:N], u[0:64, 0:N], sin_sb[0:64, 0:N], ALU.mult))
                    free(key)
                    link(V.tensor_tensor(dst, dst, rope_tmp_[:, 0:N], ALU.add))
                def conv(j):
                    B = LB * ph + j
                    w = [vcols[:, V_CW + i * KD + j:V_CW + i * KD + j + 1] for i in range(4)]
                    b = vcols[:, V_CB + j:V_CB + j + 1]
                    u, y = full((ph, "xr", j)), xc[j % 2]
                    if j >= 2:
                        s = (ph, "gate", j - 2, 3)
                        dve.wait_ge(bank_full[bank[s]], use[s])
                    link(V.tensor_scalar(y[:, 0:N], u[:, 0:N], w[2], b, ALU.mult, ALU.add))
                    link(V.scalar_tensor_tensor(y[:, 2:N], u[:, 0:N - 2], w[0], y[:, 2:N], ALU.mult, ALU.add))
                    link(V.scalar_tensor_tensor(y[:, 1:N], u[:, 0:N - 1], w[1], y[:, 1:N], ALU.mult, ALU.add))
                    link(V.scalar_tensor_tensor(y[:, 0:N - 1], u[:, 1:N], w[3], y[:, 0:N - 1], ALU.mult, ALU.add))
                    free((ph, "xr", j))
                    dve.drain().then_inc(xc_ready, 1)
                    g, f = full((ph, "xg", j)), featT[:, j, 0:N]
                    dve.wait_ge(sq_ready, B + 1)
                    V.scalar_tensor_tensor(f, f, 1.0 / GELU_C, g[:, 0:N], ALU.add, ALU.mult).then_inc(cub_ready, 1)
                    serve(1)
                    dve.wait_ge(gtanh_ready, B + 1)
                    link(V.scalar_tensor_tensor(f, f, 1.0, g[:, 0:N], ALU.add, ALU.mult))
                    free((ph, "xg", j))
                    i = j - (LB - NKV)
                    if ph and i >= 0:
                        rope((ph, "k", i), kT[:, i, 0:N], final_row)
                    if ph == 0:
                        add_bias(ada_lru[j])
                conv(0)
                for j in range(LB):
                    B = LB * ph + j
                    if j + 1 < LB:
                        conv(j + 1)
                    serve(2)
                    y = xc[j % 2][:, 0:N]
                    for d in range(2):
                        dve.wait_ge(e2_ready, 2 * B + d + 1)
                        V.scalar_tensor_tensor(le[d][:, 0:N], le[d][:, 0:N], 1.0, lth[d][:, 0:N],
                                               ALU.add, ALU.mult).then_inc(w_ready, 1)
                        mark(V.scalar_tensor_tensor(lti[d][:, 0:N], lti[d][:, 0:N], 1.0, y, ALU.add, ALU.mult))
                        serve(1)
                    chain.wait()
                    for d in range(2):
                        dve.wait_ge(root_ready, 2 * B + d + 1)
                        link(V.tensor_tensor(lti[d][:, 0:N], lti[d][:, 0:N], le[d][:, 0:N], ALU.mult))
                        h0 = 0.0 if ph == 0 else vcols[:, V_SF + d * KD + j:V_SF + d * KD + j + 1]
                        rev = slice(None, None, -1) if d else slice(None)
                        a_, b_, o_ = (t_[:, 0:N][:, rev] for t_ in (la[d], lti[d], lt[d]))
                        link(V.tensor_tensor_scan(o_, a_, b_, h0, ALU.mult, ALU.add))
                    if ph == 0:
                        V.tensor_copy(state[:, j:j + 1], lt[0][:, N - 1:N]).then_inc(state_ready, 1)
                        V.tensor_copy(state[:, LB + j:LB + j + 1], lt[1][:, 0:1]).then_inc(state_ready, 1)
                        dve.wait_ge(state_ready, 2 * j + 2)
                    link(V.tensor_tensor(lt[0][:, 0:N], lt[0][:, 0:N], lt[1][:, 0:N], ALU.add))
                    f = featT[:, j, 0:N]
                    link(V.scalar_tensor_tensor(f, lt[0][:, 0:N], 0.5, f, ALU.mult, ALU.mult))
                    dve.drain().then_inc(lru_done, 1)
                    serve(1)
                end_stage()

                def merge(a, o, j0):
                    for m in range(KD):
                        i = 2 * KD * ph + j0 + m
                        dve.wait_ge(rg_ready, i + 1)
                        u = full((ph, o, m))
                        t_ = wk(2 + m % 2)[:, 0:N]
                        if a == "gr":
                            link(V.scalar_tensor_tensor(mixT[:, m, 0:N], t_, 1.0, u[:, 0:N], ALU.add, ALU.mult))
                        else:
                            link(V.scalar_tensor_tensor(t_, t_, 1.0, u[:, 0:N], ALU.add, ALU.mult))
                            link(V.tensor_tensor(mixT[:, m, 0:N], mixT[:, m, 0:N], t_, ALU.add))
                        free((ph, o, m))
                        dve.drain().then_inc(mix_ready, 1)
                        serve(8 if a == "gr" else 6)
                serve(8)
                merge("gr", "ro", 0)

                if ph == 0:
                    u = full((ph, "kv"))
                    V.tensor_copy(ktok[:, :], u[:, 0:KVW]).then_inc(v_ready, 1)
                    V.tensor_copy(v_sb[:, 0, :], u[:, KVW:2 * KVW]).then_inc(v_ready, 1)
                    free((ph, "kv"))
                else:
                    for h in range(NH):
                        rope((ph, "q", h), featT[:, h, 0:N])
                        serve(1)
                end_stage()
                if ph:
                    gelu_dots(0)
                qs = quads(ph)
                def soft(q):
                    n = q[0]
                    kv = q[1]
                    Q = NKV * CH0[ph] + quads(ph).index(q)
                    W = P if ph == 0 else (min(n + 1, NT[ph] - 1) - max(n - 1, 0) + 2) * P
                    for h in range(G):
                        u = full((ph, "s", q, h))
                        sm = sm_pair[Q % 2]
                        if ph == 0:
                            mark(V.tensor_scalar(sm[:, h, 0:W], u[:, 0:W], SCALE, None, ALU.mult))
                        else:
                            m0 = 1 if n == 0 else 0 if n < NT[ph] - 1 else 4
                            mk = mask[:, m0:m0 + W // P, :].rearrange("p i n -> p (i n)")
                            mark(V.scalar_tensor_tensor(sm[:, h, 0:W], u[:, 0:W], SCALE, mk, ALU.mult, ALU.add))
                        free((ph, "s", q, h))
                    chain.wait()
                    link(V.tensor_reduce(q_max[:, Q, :], sm[:, :, 0:W], AX_X, ALU.max))
                    sk = sink[:, kv * G:(kv + 1) * G]
                    link(V.tensor_tensor(q_max[:, Q, :], q_max[:, Q, :], sk, ALU.max))
                    link(V.tensor_tensor(q_dif[:, Q, :], sk, q_max[:, Q, :], ALU.subtract))
                    link(V.tensor_scalar(q_neg[:, Q, :], q_max[:, Q, :], -1.0, None, ALU.mult))
                    dve.drain().then_inc(neg_ready, 1)

                soft(qs[0])
                for i, q in enumerate(qs):
                    Q = NKV * CH0[ph] + i
                    n = q[0]
                    if i + 1 < len(qs):
                        soft(qs[i + 1])
                    serve(4)
                    dve.wait_ge(prob_ready, G * Q + G)
                    link(V.tensor_tensor(q_tot[:, Q, :], q_sum[:, Q, :], q_es[:, Q, :], ALU.add))
                    link(V.reciprocal(q_inv[:, Q, :], q_tot[:, Q, :]))
                    u = full((ph, "o", q))
                    if Q >= 2:
                        prev = ot_units[Q - 2]
                        dve.wait_ge(bank_full[bank[prev]], use[prev])
                    V.tensor_tensor(o_sb[Q % 2].rearrange("p (h d) -> p h d", h=G),
                                    u[:, :].rearrange("p (h d) -> p h d", h=G),
                                    q_inv[:, Q, :].unsqueeze(2).to_broadcast([P, G, P]), ALU.mult).then_inc(o_ready, 1)
                    dve.wait_ge(o_ready, Q + 1)
                    free((ph, "o", q))
                    serve(2)
                end_stage()
                serve(16)
                merge("ga", "ao", KD)
                dve.wait_ge(rows_in, 64 * (ph + 1))
                link(V.scalar_tensor_tensor(scale_row, scale_row, 1.0, ffn_row, ALU.add, ALU.mult))
                for t in range(NT[ph]):
                    c = CH0[ph] + t
                    for n in range(D // TC):
                        u = full((ph, "mix", n, t))
                        x = x_all[:, c, n * TC:(n + 1) * TC]
                        link(V.scalar_tensor_tensor(mix_tmp[:, 0:TC], u[:, 0:TC], 0.5, gate_row[:, n * TC:(n + 1) * TC],
                                                    ALU.mult, ALU.mult))
                        free((ph, "mix", n, t))
                        link(V.tensor_tensor(x, x, mix_tmp[:, 0:TC], ALU.add))
                        serve(2)
                    if ph and t == 1:
                        serve(2 * SLOTS)
                        dve.wait_ge(slot0_used, RING0 + 2 * SLOTS)
                        dve.wait_ge(final_in, 16)
                        add_sums(0, acc0)
                        dve.drain().then_inc(sums0_done, 1)
                    v = var2(ph, t)
                    variance(v, x_all[:, c, :], h2_all[:, c, :])
                    dve.drain().then_inc(var_ready, 1)
                    dve.wait_ge(std_ready, v + 1)
                    r = inverse_root(v)
                    link(V.scalar_tensor_tensor(h2_all[:, c, :], x_all[:, c, :], r, scale_row, ALU.mult, ALU.mult))
                    V.tensor_tensor(h2_all[:, c, :], h2_all[:, c, :], shift_row, ALU.add).then_inc(xn_ready, 1)
                if ph == 0:
                    norm1(1)
                end_stage()
                for hp in range(HP):
                    u = full((ph, "sc", hp))
                    for t in range(NT[ph]):
                        s = u[:, t * P:(t + 1) * P]
                        tv, ti = top_v[:, t, hp, :], top_i[:, t, hp, :]
                        cu = cut[:, (t % 4) * P:(t % 4 + 1) * P]
                        link(V.max(tv[:, 0:8], s))
                        mark(V.max_index(ti[:, 0:8], tv[:, 0:8], s))
                        link(V.match_replace(cu, tv[:, 0:8], s, NEG_BIG))
                        link(V.max(tv[:, 8:16], cu))
                        link(V.max_index(ti[:, 8:16], tv[:, 8:16], cu))
                    free((ph, "sc", hp))
                    if ph == 0 and hp + 1 in ada_after:
                        add_bias(ada_after[hp + 1])
                    if hp % 2:
                        best_sums(CH0[ph], hp // 2)
                        if hp == HP - 1:
                            best_diffs(CH0[ph])
                        experts(CH0[ph], hp // 2, hp // 2 + 1)
                if ph == 0:
                    u = full(("state",))
                    link(V.tensor_copy(state_out[:, :], u[0:2 * LB, 0:P]))
                    free(("state",))
                    dve.drain().then_inc(state_turned, 1)
                end_stage()
                if ph == 0:
                    routed(0)
                    dve.drain().then_inc(slot0_used, RING0)
                    served[0] = 0

            routed(C1)
            dve.drain().then_inc(group_used, NG)
            groups = turns = 0
            V.memset(dots_ring[:, :], 0.0).then_inc(peer_dve, 1)
            done = 1
            for step in steps:
                per = RING // len(step)
                has_u = step[0][0] == "u"
                has_v = step[-1][0] == "v"
                if has_v:
                    for a_ in acc:
                        V.memset(a_, 0.0).then_inc(peer_dve, 1)
                    done += 2
                    dve.wait_ge(peer_dve, done)
                each = (per if has_v else 0) + (1 if has_u else 0)
                turns_all = len(step) * SLOTS // RING
                iters = turns_all // PARTS
                for part in range(PARTS):
                    if has_u and step[0][1] + 1 < NCH:
                        route(step[0][1] + 1, part)
                    with dve.Fori(0, iters) as it:
                        k = 0
                        for r in range(RING):
                            table, c = step[r % len(step)]
                            q = r // len(step)
                            if r == 0:
                                dve.wait_ge(peer_dve, it * each + done)
                            dve.wait_ge(row_in[r], (it + (turns + 1)) * 16)
                            if table == "u":
                                ins_ = V.tensor_tensor_reduce(ring[r], ring[r], h2_all[:, c, :], 1.0, 0.0,
                                                              ALU.mult, ALU.add, dots_ring[:, r:r + 1])
                            else:
                                if k >= 2:
                                    dve.wait_ge(peer_dve, it * each + (done + k - 1))
                                w_ = gw[:, c, bass.ds(it * per + (part * iters * per + q), 1)]
                                ins_ = V.scalar_tensor_tensor(acc[k % 2], ring[r], w_, acc[k % 2], ALU.mult, ALU.add)
                                ins_.then_inc(peer_dve, 1)
                                k += 1
                            if r % GS == GS - 1:
                                if table == "u":
                                    ins_.then_inc(group_used, 1)
                                else:
                                    dve.drain().then_inc(group_used, 1)
                        if has_u:
                            dve.wait_ge(group_used, it * NG + (NG + groups + NG))
                            src = dots_ring[:, :].rearrange("p (q s) -> p q s", s=len(step))[:, :, 0]
                            V.tensor_copy(dots[:, bass.ds(it * per + part * iters * per, per)], src).then_inc(peer_dve, 1)
                    groups += iters * NG
                    turns += iters
                    done += iters * each
                dve.wait_ge(peer_dve, done)
                for table, c in step:
                    if table == "u":
                        gelu_dots(c)
                if step is steps[0]:
                    dve.wait_ge(final_in, 48)
                    final(0, ring0_more[:, 0, :])
                for table, c in step:
                    if table == "v":
                        add_sums(c, acc)
                        final(c, acc[1])

        @block.gpsimd
        def _(pool):
            g = nc.gpsimd
            g.memset(pad[:, :], 0.0).then_inc(idx_seen, 1)
            pool.wait_ge(idx_seen, 1)
            pool.wait_ge(route_ready, 1)
            sets = 0

            def rows0(table, first_slot, first_row, turn_slots, turn):
                r, used, sets_ = first_slot % RING0, turn * RING0 + first_slot, turn * (RING0 // GS0) + sets
                pool.wait_ge(slot0_used, used + GS0)
                src = eidx[:, 0, bass.ds(turn * RING0 + first_row, GS0)]
                g.tensor_copy(idx_ring[:, r:r + GS0], src).then_inc(idx_set, 1)
                pool.wait_ge(idx_set, sets_ + 1 + turn_slots)
                g.tensor_tensor(pad[:, :], pad[:, :], pad[:, :], ALU.add).then_inc(idx_seen, 1)
                for i in range(GS0):
                    g.indirect_dma_start(ring0[r + i], None, ins["peer_" + table][0],
                                         bass.IndirectOffsetOnAxis(ap=idx_ring[:, r + i:r + i + 1], axis=0))\
                        .then_inc(row0_in[r + i], 16)

            slot_ = 0
            for table in "uv":
                row = 0
                while row < SLOTS:
                    whole = (SLOTS - row) // RING0 if slot_ % RING0 == 0 else 0
                    if whole:
                        with pool.Fori(0, whole) as turn:
                            for n in range(RING0 // GS0):
                                rows0(table, slot_ + n * GS0, row + n * GS0, n, turn)
                        n = whole * RING0
                    else:
                        rows0(table, slot_, row, 0, 0)
                        n = GS0
                    slot_, row, sets = slot_ + n, row + n, sets + n // GS0

            groups = 0
            for step in steps:
                pool.wait_ge(route_ready, step[0][1] + 1)
                iters = len(step) * SLOTS // RING
                per = GS // len(step)
                with pool.Fori(0, iters) as it:
                    for n in range(NG):
                        pool.wait_ge(group_used, it * NG + (groups + n + 1))
                        for s, (table, c) in enumerate(step):
                            dst = idx_ring[:, n * GS:(n + 1) * GS].rearrange("p (q s) -> p q s", s=len(step))[:, :, s]
                            src = eidx[:, c, bass.ds(it * (per * NG) + n * per, per)]
                            g.tensor_copy(dst, src).then_inc(idx_set, 1)
                        pool.wait_ge(idx_set, it * (NG * len(step)) + (sets + (n + 1) * len(step)))
                        g.tensor_tensor(pad[:, :], pad[:, :], pad[:, :], ALU.add).then_inc(idx_seen, 1)
                        for i in range(GS):
                            r = n * GS + i
                            table, c = step[r % len(step)]
                            g.indirect_dma_start(ring[r], None, ins["peer_u" if table == "u" else "peer_v"][0],
                                                 bass.IndirectOffsetOnAxis(ap=idx_ring[:, r:r + 1], axis=0))\
                                .then_inc(row_in[r], 16)
                groups += iters * NG
                sets += iters * NG * len(step)



_INS = ['x_prompt', 'x_sample', 'c', 'cache_k', 'cache_v', 'state_h_fwd', 'state_h_bwd', 'c_ctx', 'norm_attn_g',
        'norm_ffn_g', 'final_g', 'w_ada', 'b_ada', 'w_in', 'attn_sink', 'conv_w', 'conv_b', 'lru_w_a', 'lru_b_a',
        'lru_w_i', 'lru_b_i', 'lru_lambda', 'w_attn_o', 'w_rnn_o', 'w_out', 'peer_w_q', 'peer_keys', 'peer_u',
        'peer_v']
_OUTS = [((1, 128, 1024), 'float32'), ((1, 512, 1024), 'float32'), ((1, 1, 128, 2, 128), 'float32'),
         ((1, 1, 128, 2, 128), 'float32'), ((1, 1, 1024), 'float32'), ((1, 1, 1024), 'float32')]


def _constants(np, tokens, head_dim, block, grid_w, topk):
    freqs = head_dim // 4
    rows = tokens // grid_w
    row = np.repeat(np.arange(rows, dtype=np.float32), grid_w)
    col = np.tile(np.arange(grid_w, dtype=np.float32), rows)
    inv = (np.float32(10000.0) ** (-np.arange(freqs, dtype=np.float32) / np.float32(freqs))).astype(np.float32)
    ang = np.concatenate([row[:, None] * inv, col[:, None] * inv], axis=-1).T
    cos, sin = np.cos(ang).astype(np.float32), np.sin(ang).astype(np.float32)
    q, k = np.arange(block)[:, None], np.arange(block)[None, :]
    before = np.where(k >= q, 0.0, -1e30).astype(np.float32)
    after = np.where(k <= q, 0.0, -1e30).astype(np.float32)
    none = np.zeros_like(before)
    return {
        "rope_cos": np.concatenate([cos, cos]), "rope_sin": np.concatenate([sin, -sin]),
        "mask": np.concatenate([before, none, after, none, before, none, none], axis=1),
        "ident": np.eye(block, dtype=np.float32),
        "iota16": np.broadcast_to(np.arange(topk, dtype=np.float32), (block, topk)).copy(),
    }


def kernel(**inputs):
    import numpy as _np
    import concourse.bacc as _bacc
    from concourse import mybir as _mybir
    from concourse.bass_utils import run_bass_kernel_spmd as _run

    nc = _bacc.Bacc("TRN2", target_bir_lowering=False, num_devices=1)
    arrays, ins, outs = {}, {}, []
    given = {name: _np.ascontiguousarray(inputs[name]) for name in _INS}
    given.update(_constants(_np, 512, 128, 128, 64, 16))
    for name, a in given.items():
        arrays[f"in_{name}_dram"] = a
        ins[name] = nc.dram_tensor(f"in_{name}_dram", a.shape, _mybir.dt.from_np(a.dtype), kind="ExternalInput").ap()
    for i, (shape, dtype) in enumerate(_OUTS):
        dt = _mybir.dt.from_np(_np.dtype(dtype))
        outs.append(nc.dram_tensor(f"out_{i}_dram", shape, dt, kind="ExternalOutput").ap())
    scratch = nc.dram_tensor("ada_scratch", (2, 6144), _mybir.dt.float32, kind="Internal").ap()
    hybrid_step(nc, ins, outs, scratch)
    r = _run(nc, [arrays], core_ids=[0])
    return tuple(r.results[0][f"out_{i}_dram"] for i in range(len(_OUTS)))
```
